# Optimizing a Trainium2 kernel written in Bass

```python
import math
import jax, jax.numpy as jnp
from jax import lax
import numpy as np

D_MODEL = 1024
BATCH = 1
SEQ = 512
DEPTH = 1

MEM_LEN = 256
EPS = 1e-6
CONV_WIDTH = 4
SSD_EXPAND = 2
SSD_WIDTH = SSD_EXPAND * D_MODEL
SSD_HEAD_DIM = 64
SSD_HEADS = SSD_WIDTH // SSD_HEAD_DIM
SSD_GROUPS = 4
SSD_STATE = 128
SSD_CHUNK = 128
SSD_CONV_CH = SSD_WIDTH + 2 * SSD_GROUPS * SSD_STATE
LRU_WIDTH = 3 * D_MODEL // 2
LRU_BLOCKS = 16
LRU_BLOCK = LRU_WIDTH // LRU_BLOCKS
LRU_C = 8.0
MEM_HEADS = 4
MEM_HEAD_DIM = D_MODEL // MEM_HEADS
N_BRANCH = 3
SPLIT_POINTS = (
    SSD_WIDTH,
    SSD_WIDTH + SSD_CONV_CH,
    SSD_WIDTH + SSD_CONV_CH + SSD_HEADS,
    SSD_WIDTH + SSD_CONV_CH + SSD_HEADS + LRU_WIDTH,
    SSD_WIDTH + SSD_CONV_CH + SSD_HEADS + 2 * LRU_WIDTH,
    SSD_WIDTH + SSD_CONV_CH + SSD_HEADS + 2 * LRU_WIDTH + D_MODEL,
)
IN_WIDTH = SSD_WIDTH + SSD_CONV_CH + SSD_HEADS + 2 * LRU_WIDTH + D_MODEL + N_BRANCH * D_MODEL


def rms_norm(x, g):
    xf = x.astype(jnp.float32)
    y = xf * lax.rsqrt(jnp.mean(xf * xf, axis=-1, keepdims=True) + EPS)
    return (y * g.astype(jnp.float32)).astype(x.dtype)

def causal_dwconv(x, w, b):
    k = w.shape[0]
    y = lax.conv_general_dilated(
        x, w[:, None, :].astype(x.dtype), window_strides=(1,), padding=[(k - 1, 0)],
        dimension_numbers=('NWC', 'WIO', 'NWC'), feature_group_count=x.shape[-1])
    return y + b

def ssd_scan(x, dt, a_neg, b_in, c_in):
    f32 = jnp.float32
    bsz, s, h, p = x.shape
    g, n = b_in.shape[2], b_in.shape[3]
    k = h // g
    l = SSD_CHUNK
    nc = s // l
    x = x.astype(f32).reshape(bsz, nc, l, g, k, p)
    dt = dt.astype(f32).reshape(bsz, nc, l, g, k)
    bm = b_in.astype(f32).reshape(bsz, nc, l, g, n)
    cm = c_in.astype(f32).reshape(bsz, nc, l, g, n)
    xdt = x * dt[..., None]
    a_cs = jnp.cumsum(dt * a_neg.astype(f32).reshape(g, k), axis=2)
    causal = jnp.tril(jnp.ones((l, l), dtype=bool))
    seg = a_cs[:, :, :, None] - a_cs[:, :, None, :]
    decay = jnp.exp(jnp.where(causal[:, :, None, None], seg, -jnp.inf))
    cb = jnp.einsum('bclgn,bcsgn->bclsg', cm, bm)
    y_diag = jnp.einsum('bclsgk,bcsgkp->bclgkp', decay * cb[..., None], xdt)
    decay_to_end = jnp.exp(a_cs[:, :, -1:] - a_cs)
    states = jnp.einsum('bclgn,bclgkp->bcgkpn', bm, xdt * decay_to_end[..., None])
    chunk_decay = jnp.exp(a_cs[:, :, -1])

    def step(carry, inp):
        st, dec = inp
        return carry * dec[..., None, None] + st, carry

    init = jnp.zeros((bsz, g, k, p, n), f32)
    _, prev = lax.scan(step, init, (jnp.moveaxis(states, 1, 0), jnp.moveaxis(chunk_decay, 1, 0)))
    prev = jnp.moveaxis(prev, 0, 1)
    y_off = jnp.einsum('bclgn,bcgkpn->bclgkp', cm, prev) * jnp.exp(a_cs)[..., None]
    return (y_diag + y_off).reshape(bsz, s, h, p)

def rg_lru(x, w_a, b_a, w_x, b_x, lam):
    f32 = jnp.float32
    bsz, s, w = x.shape
    xb = x.reshape(bsz, s, LRU_BLOCKS, LRU_BLOCK)
    r = jax.nn.sigmoid(jnp.einsum('bsni,nij->bsnj', xb, w_a) + b_a).reshape(bsz, s, w)
    i = jax.nn.sigmoid(jnp.einsum('bsni,nij->bsnj', xb, w_x) + b_x).reshape(bsz, s, w)
    log_a = (-LRU_C * r.astype(f32)) * jax.nn.softplus(-lam.astype(f32))
    a = jnp.exp(log_a)
    mult = jnp.sqrt(-jnp.expm1(2.0 * log_a))
    u = mult * (i * x).astype(f32)

    def combine(left, right):
        a1, b1 = left
        a2, b2 = right
        return a1 * a2, a2 * b1 + b2

    _, hs = lax.associative_scan(combine, (a, u), axis=1)
    return hs.astype(x.dtype)

def memory_attention(q, mem_n, w_kv):
    bsz, s, _ = q.shape
    m = mem_n.shape[1]
    kv = mem_n @ w_kv
    k, v = jnp.split(kv, 2, axis=-1)
    q = q.reshape(bsz, s, MEM_HEADS, MEM_HEAD_DIM)
    k = k.reshape(bsz, m, MEM_HEADS, MEM_HEAD_DIM)
    v = v.reshape(bsz, m, MEM_HEADS, MEM_HEAD_DIM)
    scores = jnp.einsum('bshd,bmhd->bhsm', q, k).astype(jnp.float32) * (MEM_HEAD_DIM ** -0.5)
    probs = jax.nn.softmax(scores, axis=-1).astype(v.dtype)
    return jnp.einsum('bhsm,bmhd->bshd', probs, v).reshape(bsz, s, D_MODEL)

def first_inputs(seed: int = 0) -> dict:
    key = jax.random.key(seed)
    ks = jax.random.split(key, 24)
    f32 = jnp.float32
    nrm = lambda k, shape, scale: jax.random.normal(k, shape, f32) * scale
    x = jax.random.normal(ks[0], (BATCH, SEQ, D_MODEL), f32)
    mem = jax.random.normal(ks[1], (BATCH, MEM_LEN, D_MODEL), f32)
    norm_g = 1.0 + nrm(ks[2], (DEPTH, D_MODEL), 0.02)
    w_in = nrm(ks[3], (DEPTH, D_MODEL, IN_WIDTH), D_MODEL ** -0.5)
    ssd_conv_w = nrm(ks[4], (DEPTH, CONV_WIDTH, SSD_CONV_CH), CONV_WIDTH ** -0.5)
    ssd_conv_b = nrm(ks[5], (DEPTH, SSD_CONV_CH), 0.02)
    dt0 = jnp.exp(jax.random.uniform(ks[6], (DEPTH, SSD_HEADS), f32, math.log(1e-3), math.log(1e-1)))
    ssd_dt_bias = dt0 + jnp.log(-jnp.expm1(-dt0))
    ssd_a_log = jnp.log(jax.random.uniform(ks[7], (DEPTH, SSD_HEADS), f32, 1.0, 16.0))
    ssd_d = 1.0 + nrm(ks[8], (DEPTH, SSD_HEADS), 0.02)
    ssd_norm_g = 1.0 + nrm(ks[9], (DEPTH, SSD_GROUPS, SSD_WIDTH // SSD_GROUPS), 0.02)
    lru_conv_w = nrm(ks[10], (DEPTH, CONV_WIDTH, LRU_WIDTH), CONV_WIDTH ** -0.5)
    lru_conv_b = nrm(ks[11], (DEPTH, LRU_WIDTH), 0.02)
    lru_w_a = nrm(ks[12], (DEPTH, LRU_BLOCKS, LRU_BLOCK, LRU_BLOCK), LRU_BLOCK ** -0.5)
    lru_b_a = nrm(ks[13], (DEPTH, LRU_BLOCKS, LRU_BLOCK), 0.02)
    lru_w_x = nrm(ks[14], (DEPTH, LRU_BLOCKS, LRU_BLOCK, LRU_BLOCK), LRU_BLOCK ** -0.5)
    lru_b_x = nrm(ks[15], (DEPTH, LRU_BLOCKS, LRU_BLOCK), 0.02)
    a8 = jax.random.uniform(ks[16], (DEPTH, LRU_WIDTH), f32, 0.9, 0.999)
    sig = a8 ** (1.0 / LRU_C)
    lru_lambda = jnp.log(sig) - jnp.log1p(-sig)
    mem_norm_g = 1.0 + nrm(ks[17], (DEPTH, D_MODEL), 0.02)
    w_kv = nrm(ks[18], (DEPTH, D_MODEL, 2 * D_MODEL), D_MODEL ** -0.5)
    w_br_ssd = nrm(ks[19], (DEPTH, SSD_WIDTH, D_MODEL), SSD_WIDTH ** -0.5)
    w_br_lru = nrm(ks[20], (DEPTH, LRU_WIDTH, D_MODEL), LRU_WIDTH ** -0.5)
    w_br_mem = nrm(ks[21], (DEPTH, D_MODEL, D_MODEL), D_MODEL ** -0.5)
    w_out = nrm(ks[22], (DEPTH, D_MODEL, D_MODEL), D_MODEL ** -0.5)
    final_g = 1.0 + nrm(ks[23], (D_MODEL,), 0.02)
    return {"x": x, "mem": mem, "norm_g": norm_g, "w_in": w_in,
            "ssd_conv_w": ssd_conv_w, "ssd_conv_b": ssd_conv_b, "ssd_dt_bias": ssd_dt_bias,
            "ssd_a_log": ssd_a_log, "ssd_d": ssd_d, "ssd_norm_g": ssd_norm_g,
            "lru_conv_w": lru_conv_w, "lru_conv_b": lru_conv_b, "lru_w_a": lru_w_a,
            "lru_b_a": lru_b_a, "lru_w_x": lru_w_x, "lru_b_x": lru_b_x, "lru_lambda": lru_lambda,
            "mem_norm_g": mem_norm_g, "w_kv": w_kv, "w_br_ssd": w_br_ssd, "w_br_lru": w_br_lru,
            "w_br_mem": w_br_mem, "w_out": w_out, "final_g": final_g}

def first_block(x, mem, norm_g, w_in, ssd_conv_w, ssd_conv_b, ssd_dt_bias, ssd_a_log, ssd_d,
              ssd_norm_g, lru_conv_w, lru_conv_b, lru_w_a, lru_b_a, lru_w_x, lru_b_x, lru_lambda,
              mem_norm_g, w_kv, w_br_ssd, w_br_lru, w_br_mem, w_out, final_g):
    bsz, s, _ = x.shape
    for l in range(DEPTH):
        h = rms_norm(x, norm_g[l])
        proj = h @ w_in[l]
        z, xbc, dt_raw, lru_gate, lru_x, q, gate_logits = jnp.split(proj, SPLIT_POINTS, axis=-1)

        xbc = jax.nn.silu(causal_dwconv(xbc, ssd_conv_w[l], ssd_conv_b[l]))
        xs, bs, cs = jnp.split(xbc, [SSD_WIDTH, SSD_WIDTH + SSD_GROUPS * SSD_STATE], axis=-1)
        xs = xs.reshape(bsz, s, SSD_HEADS, SSD_HEAD_DIM)
        dt = jax.nn.softplus((dt_raw + ssd_dt_bias[l]).astype(jnp.float32))
        y = ssd_scan(xs, dt, -jnp.exp(ssd_a_log[l].astype(jnp.float32)),
                     bs.reshape(bsz, s, SSD_GROUPS, SSD_STATE), cs.reshape(bsz, s, SSD_GROUPS, SSD_STATE))
        y = (y + xs.astype(jnp.float32) * ssd_d[l][:, None].astype(jnp.float32)).astype(x.dtype)
        y = y.reshape(bsz, s, SSD_WIDTH) * jax.nn.silu(z)
        y_ssd = rms_norm(y.reshape(bsz, s, SSD_GROUPS, SSD_WIDTH // SSD_GROUPS),
                         ssd_norm_g[l]).reshape(bsz, s, SSD_WIDTH)

        xl = causal_dwconv(lru_x, lru_conv_w[l], lru_conv_b[l])
        y_lru = rg_lru(xl, lru_w_a[l], lru_b_a[l], lru_w_x[l], lru_b_x[l], lru_lambda[l]) * jax.nn.silu(lru_gate)

        mem_n = rms_norm(mem, mem_norm_g[l])
        y_mem = memory_attention(q, mem_n, w_kv[l])

        gates = jax.nn.sigmoid(gate_logits).reshape(bsz, s, N_BRANCH, D_MODEL)
        merged = (gates[:, :, 0] * (y_ssd @ w_br_ssd[l])
                  + gates[:, :, 1] * (y_lru @ w_br_lru[l])
                  + gates[:, :, 2] * (y_mem @ w_br_mem[l]))
        x = x + merged @ w_out[l]
    return rms_norm(x, final_g)


_first_inputs = first_inputs


def first_inputs(seed=0):
    import zlib

    import numpy as np

    out = dict(_first_inputs(seed))
    spreads = {}
    factors = {'norm_g': 3.614,
     'ssd_conv_b': 17.533,
     'ssd_d': 64.0,
     'ssd_norm_g': 33.697,
     'lru_b_a': 33.029,
     'lru_b_x': 27.249,
     'mem_norm_g': 8.0,
     'final_g': 8.42,
     'lru_conv_b': 3.408}
    for name, (base, spread) in spreads.items():
        noise = np.random.default_rng([zlib.crc32(name.encode()), seed]).standard_normal(out[name].shape)
        drawn = base * np.exp(spread * noise) if base else spread * noise
        out[name] = __import__('jax').numpy.asarray(drawn.astype(out[name].dtype))
    for name, factor in factors.items():
        out[name] = (out[name] * factor).astype(out[name].dtype)
    return out


_narrow_inputs = first_inputs


def first_inputs(seed=0):

    out = dict(_narrow_inputs(seed))
    wider = {'ssd_d': 11.34,
     'ssd_norm_g': 3.36,
     'lru_conv_b': 3.27,
     'lru_b_a': 3.33,
     'lru_b_x': 3.3,
     'final_g': 3.28}
    for name, times in wider.items():
        mean = out[name].mean()
        out[name] = (mean + times * (out[name] - mean)).astype(out[name].dtype)
    return out


CHUNK = 64
NEG = -1e30

FOX_HEAD_DIM = 64
D_FOX = 3 * D_MODEL // 4
FOX_HEADS = D_FOX // FOX_HEAD_DIM
Q_BLOCK = 128

D_S5 = 3 * D_MODEL // 4
S5_GROUP = 16
S5_GROUPS = D_S5 // S5_GROUP
S5_STATE = 64

D_MEM = D_MODEL // 2
MEM_HEAD_DIM_2 = D_MEM // MEM_HEADS

IN_SIZES = (D_FOX, D_FOX, D_FOX, FOX_HEADS, D_FOX,
            D_S5, D_S5,
            D_MEM, D_MEM,
            N_BRANCH * D_MODEL)
N_IN = sum(IN_SIZES)


def rms_norm_2(x, g):
    xf = x.astype(jnp.float32)
    y = xf * lax.rsqrt(jnp.mean(xf * xf, axis=-1, keepdims=True) + EPS)
    return (y * g.astype(jnp.float32)).astype(x.dtype)

def split_cols(z):
    offs = np.cumsum(np.array(IN_SIZES))[:-1].tolist()
    return jnp.split(z, offs, axis=-1)

def forgetting_attention(q, k, v, log_f):
    Bn, L, H, Dh = q.shape
    nb = L // Q_BLOCK
    F = jnp.cumsum(log_f, axis=1).transpose(0, 2, 1)
    kh = k.astype(jnp.float32).transpose(0, 2, 1, 3)
    vh = v.astype(jnp.float32).transpose(0, 2, 1, 3)
    qb = (q.astype(jnp.float32) * (Dh ** -0.5)).reshape(Bn, nb, Q_BLOCK, H, Dh).transpose(1, 0, 3, 2, 4)
    Fq = F.reshape(Bn, H, nb, Q_BLOCK).transpose(2, 0, 1, 3)
    starts = jnp.arange(nb, dtype=jnp.int32) * Q_BLOCK
    key_pos = jnp.arange(L, dtype=jnp.int32)

    def block(args):
        qi, Fi, s0 = args
        s = jnp.einsum('bhqd,bhkd->bhqk', qi, kh)
        s = s + Fi[..., None] - F[:, :, None, :]
        qpos = s0 + jnp.arange(Q_BLOCK, dtype=jnp.int32)
        s = jnp.where(key_pos[None, :] <= qpos[:, None], s, NEG)
        p = jax.nn.softmax(s, axis=-1)
        return jnp.einsum('bhqk,bhkd->bhqd', p, vh)

    out = lax.map(block, (qb, Fq, starts))
    return out.transpose(1, 0, 3, 2, 4).reshape(Bn, L, H * Dh).astype(q.dtype)

def s5_ssm(u, lam_re, lam_im, log_step, b_re, b_im, c_re, c_im, d_skip):
    Bn, L, _ = u.shape
    f32 = jnp.float32
    uf = u.astype(f32).reshape(Bn, L, S5_GROUPS, S5_GROUP)
    step = jnp.exp(log_step.astype(f32))[:, None]
    lr, li = lam_re.astype(f32), lam_im.astype(f32)
    mag = jnp.exp(lr * step)
    ab_re, ab_im = mag * jnp.cos(li * step), mag * jnp.sin(li * step)
    den = lr * lr + li * li
    nr, ni = ab_re - 1.0, ab_im
    f_re = (nr * lr + ni * li) / den
    f_im = (ni * lr - nr * li) / den
    br, bi = b_re.astype(f32), b_im.astype(f32)
    bb_re = f_re[..., None] * br - f_im[..., None] * bi
    bb_im = f_re[..., None] * bi + f_im[..., None] * br
    x_re = jnp.einsum('gph,blgh->blgp', bb_re, uf)
    x_im = jnp.einsum('gph,blgh->blgp', bb_im, uf)
    a_re = jnp.broadcast_to(ab_re[None, None], (1, L, S5_GROUPS, S5_STATE))
    a_im = jnp.broadcast_to(ab_im[None, None], (1, L, S5_GROUPS, S5_STATE))

    def combine(e1, e2):
        a1r, a1i, b1r, b1i = e1
        a2r, a2i, b2r, b2i = e2
        return (a2r * a1r - a2i * a1i,
                a2r * a1i + a2i * a1r,
                a2r * b1r - a2i * b1i + b2r,
                a2r * b1i + a2i * b1r + b2i)

    _, _, h_re, h_im = lax.associative_scan(combine, (a_re, a_im, x_re, x_im), axis=1)
    y = (jnp.einsum('ghp,blgp->blgh', c_re.astype(f32), h_re)
         - jnp.einsum('ghp,blgp->blgh', c_im.astype(f32), h_im))
    y = y + d_skip.astype(f32).reshape(S5_GROUPS, S5_GROUP) * uf
    return y.reshape(Bn, L, D_S5).astype(u.dtype)

def memory_attention_2(q, mk, mv):
    Bn, L = q.shape[:2]
    s = jnp.einsum('blhd,bmhd->bhlm', q.astype(jnp.float32), mk.astype(jnp.float32)) * (MEM_HEAD_DIM_2 ** -0.5)
    p = jax.nn.softmax(s, axis=-1)
    o = jnp.einsum('bhlm,bmhd->blhd', p, mv.astype(jnp.float32))
    return o.reshape(Bn, L, D_MEM).astype(q.dtype)

def second_inputs(seed: int = 0) -> dict:
    key = jax.random.key(seed)
    ks = jax.random.split(key, 24)
    f32 = jnp.float32
    nrm = lambda k, shape, scale: jax.random.normal(k, shape, f32) * scale
    x = nrm(ks[0], (BATCH, SEQ, D_MODEL), 1.0)
    mem = nrm(ks[1], (BATCH, MEM_LEN, D_MODEL), 1.0)
    g_norm = 1.0 + nrm(ks[2], (DEPTH, D_MODEL), 0.02)
    g_mem_norm = 1.0 + nrm(ks[3], (DEPTH, D_MODEL), 0.02)
    g_final = 1.0 + nrm(ks[4], (D_MODEL,), 0.02)
    w_in = nrm(ks[5], (DEPTH, D_MODEL, N_IN), D_MODEL ** -0.5)
    b_forget = jax.random.uniform(ks[6], (DEPTH, FOX_HEADS), f32, 1.0, 4.0)
    b_merge = nrm(ks[7], (DEPTH, N_BRANCH * D_MODEL), 0.01)
    w_mem_kv = nrm(ks[8], (DEPTH, D_MODEL, 2 * D_MEM), D_MODEL ** -0.5)
    lam_re = -0.5 + nrm(ks[9], (DEPTH, S5_GROUPS, S5_STATE), 0.01)
    lam_im = (math.pi * jnp.arange(S5_STATE, dtype=f32))[None, None, :] + nrm(ks[10], (DEPTH, S5_GROUPS, S5_STATE), 0.01)
    log_step = jax.random.uniform(ks[11], (DEPTH, S5_GROUPS), f32, math.log(1e-3), math.log(1e-1))
    s5_b_re = nrm(ks[12], (DEPTH, S5_GROUPS, S5_STATE, S5_GROUP), (2 * S5_GROUP) ** -0.5)
    s5_b_im = nrm(ks[13], (DEPTH, S5_GROUPS, S5_STATE, S5_GROUP), (2 * S5_GROUP) ** -0.5)
    s5_c_re = nrm(ks[14], (DEPTH, S5_GROUPS, S5_GROUP, S5_STATE), (2 * S5_STATE) ** -0.5)
    s5_c_im = nrm(ks[15], (DEPTH, S5_GROUPS, S5_GROUP, S5_STATE), (2 * S5_STATE) ** -0.5)
    s5_d = nrm(ks[16], (DEPTH, D_S5), 1.0)
    w_glu = nrm(ks[17], (DEPTH, D_S5, D_S5), D_S5 ** -0.5)
    b_glu = nrm(ks[18], (DEPTH, D_S5), 0.01)
    w_proj_fox = nrm(ks[19], (DEPTH, D_FOX, D_MODEL), D_FOX ** -0.5)
    w_proj_s5 = nrm(ks[20], (DEPTH, D_S5, D_MODEL), D_S5 ** -0.5)
    w_proj_mem = nrm(ks[21], (DEPTH, D_MEM, D_MODEL), D_MEM ** -0.5)
    w_out = nrm(ks[22], (DEPTH, D_MODEL, D_MODEL), D_MODEL ** -0.5)
    return {"x": x, "mem": mem, "g_norm": g_norm, "g_mem_norm": g_mem_norm, "g_final": g_final,
            "w_in": w_in, "b_forget": b_forget, "b_merge": b_merge, "w_mem_kv": w_mem_kv,
            "lam_re": lam_re, "lam_im": lam_im, "log_step": log_step,
            "s5_b_re": s5_b_re, "s5_b_im": s5_b_im, "s5_c_re": s5_c_re, "s5_c_im": s5_c_im,
            "s5_d": s5_d, "w_glu": w_glu, "b_glu": b_glu,
            "w_proj_fox": w_proj_fox, "w_proj_s5": w_proj_s5, "w_proj_mem": w_proj_mem, "w_out": w_out}

def second_block(x, mem, g_norm, g_mem_norm, g_final, w_in, b_forget, b_merge, w_mem_kv,
              lam_re, lam_im, log_step, s5_b_re, s5_b_im, s5_c_re, s5_c_im, s5_d,
              w_glu, b_glu, w_proj_fox, w_proj_s5, w_proj_mem, w_out):
    Bn, L, _ = x.shape
    M = mem.shape[1]
    for l in range(DEPTH):
        h = rms_norm_2(x, g_norm[l])
        z = h @ w_in[l]
        q, k, v, fl, gf, u, gs, qm, gm, gl = split_cols(z)

        log_f = jax.nn.log_sigmoid(fl.astype(jnp.float32) + b_forget[l].astype(jnp.float32))
        y_fox = forgetting_attention(q.reshape(Bn, L, FOX_HEADS, FOX_HEAD_DIM),
                                     k.reshape(Bn, L, FOX_HEADS, FOX_HEAD_DIM),
                                     v.reshape(Bn, L, FOX_HEADS, FOX_HEAD_DIM), log_f)
        y_fox = y_fox * jax.nn.silu(gf)

        y_s5 = s5_ssm(u, lam_re[l], lam_im[l], log_step[l], s5_b_re[l], s5_b_im[l],
                      s5_c_re[l], s5_c_im[l], s5_d[l])
        y_s5 = jax.nn.gelu(y_s5)
        y_s5 = y_s5 * jax.nn.sigmoid(y_s5 @ w_glu[l] + b_glu[l])
        y_s5 = y_s5 * jax.nn.silu(gs)

        kv = rms_norm_2(mem, g_mem_norm[l]) @ w_mem_kv[l]
        mk, mv = jnp.split(kv, 2, axis=-1)
        y_mem = memory_attention_2(qm.reshape(Bn, L, MEM_HEADS, MEM_HEAD_DIM_2),
                                 mk.reshape(Bn, M, MEM_HEADS, MEM_HEAD_DIM_2),
                                 mv.reshape(Bn, M, MEM_HEADS, MEM_HEAD_DIM_2))
        y_mem = y_mem * jax.nn.silu(gm)

        gates = jax.nn.sigmoid(gl + b_merge[l]).reshape(Bn, L, N_BRANCH, D_MODEL)
        merged = (gates[:, :, 0] * (y_fox @ w_proj_fox[l])
                  + gates[:, :, 1] * (y_s5 @ w_proj_s5[l])
                  + gates[:, :, 2] * (y_mem @ w_proj_mem[l]))
        x = x + merged @ w_out[l]
    return rms_norm_2(x, g_final)


def setup_inputs(seed=0):
    out = dict(first_inputs(seed))
    for name, value in second_inputs(seed + 1).items():
        if name != "x":
            out[name + "_2"] = value
    return out


def reference(
    x, mem, norm_g, w_in, ssd_conv_w, ssd_conv_b, ssd_dt_bias, ssd_a_log, ssd_d, ssd_norm_g,
    lru_conv_w, lru_conv_b, lru_w_a, lru_b_a, lru_w_x, lru_b_x, lru_lambda, mem_norm_g, w_kv,
    w_br_ssd, w_br_lru, w_br_mem, w_out, final_g, mem_2, g_norm_2, g_mem_norm_2, g_final_2,
    w_in_2, b_forget_2, b_merge_2, w_mem_kv_2, lam_re_2, lam_im_2, log_step_2, s5_b_re_2,
    s5_b_im_2, s5_c_re_2, s5_c_im_2, s5_d_2, w_glu_2, b_glu_2, w_proj_fox_2, w_proj_s5_2,
    w_proj_mem_2, w_out_2,
):
    x = first_block(
        x, mem, norm_g, w_in, ssd_conv_w, ssd_conv_b, ssd_dt_bias, ssd_a_log, ssd_d, ssd_norm_g,
        lru_conv_w, lru_conv_b, lru_w_a, lru_b_a, lru_w_x, lru_b_x, lru_lambda, mem_norm_g,
        w_kv, w_br_ssd, w_br_lru, w_br_mem, w_out, final_g,
    )
    return second_block(
        x, mem_2, g_norm_2, g_mem_norm_2, g_final_2, w_in_2, b_forget_2, b_merge_2, w_mem_kv_2,
        lam_re_2, lam_im_2, log_step_2, s5_b_re_2, s5_b_im_2, s5_c_re_2, s5_c_im_2, s5_d_2,
        w_glu_2, b_glu_2, w_proj_fox_2, w_proj_s5_2, w_proj_mem_2, w_out_2,
    )


_drawn_inputs = setup_inputs


def setup_inputs(seed=0):
    import zlib

    import numpy as np

    out = dict(_drawn_inputs(seed))
    spreads = {}
    factors = {'mem_2': 8.0,
     'g_norm_2': 8.0,
     'g_mem_norm_2': 8.0,
     'g_final_2': 24.03,
     'b_forget_2': 200.0,
     'b_merge_2': 42.122,
     'w_mem_kv_2': 8.0,
     'lam_re_2': 64.0,
     'lam_im_2': 64.0,
     'log_step_2': 64.0,
     's5_b_re_2': 64.0,
     's5_b_im_2': 64.0,
     's5_c_re_2': 64.0,
     's5_c_im_2': 64.0,
     's5_d_2': 4.412,
     'w_glu_2': 8.0,
     'b_glu_2': 200.0,
     'w_proj_fox_2': 3.396,
     'w_proj_s5_2': 4.0,
     'w_proj_mem_2': 8.0}
    for name, (base, spread) in spreads.items():
        noise = np.random.default_rng([zlib.crc32(name.encode()), seed]).standard_normal(out[name].shape)
        drawn = base * np.exp(spread * noise) if base else spread * noise
        out[name] = __import__('jax').numpy.asarray(drawn.astype(out[name].dtype))
    for name, factor in factors.items():
        out[name] = (out[name] * factor).astype(out[name].dtype)
    return out
```

```python
import concourse.bass as bass
from concourse import mybir
from contextlib import ExitStack

P = 128
SEQ, MEM, DM = 512, 256, 1024
KT = DM // P
CH, NCH = 128, SEQ // 128
EPS = 1e-6
SLOTS, RAW = 4, 2
SQRT_2_OVER_PI = 0.7978845608028654

XBC_T, Z_T, LRU_T, MEMKV_T = 24, 16, 12, 16
B_DT = 0
B_XBC = B_DT + 1
B_Z = B_XBC + XBC_T
B_MSSD = B_Z + Z_T
B_LX = B_MSSD + 3 * KT
B_LG = B_LX + LRU_T
B_KV = B_LG + 2 * LRU_T
B_MLRU = B_KV + MEMKV_T
B_Q = B_MLRU + 3 * KT
B_MMEM = B_Q + KT
B_OUT = B_MMEM + 2 * KT
B_END1 = B_OUT + KT

PCOLS = [("norm_g", 8), ("conv_w", 4 * 24), ("conv_b", 24), ("ssd_d", 16), ("ssd_g", 16),
         ("lconv_w", 4 * 12), ("lconv_b", 12), ("lru_b_a", 12), ("lru_b_x", 12), ("lru_lam", 12),
         ("mem_g", 8), ("final_g", 8), ("dt_bias", 1), ("a_log", 1),
         ("g_norm_2", 8), ("g_mem_norm_2", 8), ("g_final_2", 8), ("b_merge", 24), ("lam_re", 24), ("lam_im", 24),
         ("log_step", 24), ("s5_d", 6), ("b_glu", 6), ("b_forget", 1)]
PC, _n = {}, 0
for _name, _w in PCOLS:
    PC[_name] = _n
    _n += _w
NPC = _n

B_FL = B_END1
B_UG = B_FL + 1
B_FOX = B_UG + 12
B_GLU = B_FOX + 24
B_KV2 = B_GLU + 6
B_QG = B_KV2 + 8
B_M2 = B_QG + 8
B_OUT2 = B_M2 + 6 * KT
B_END = B_OUT2 + KT
LRU_KS = ((0, 1), (0, 1, 2), (1, 2))
M_OF = {B_DT: 0, B_XBC: 1, B_Z: 25, B_MSSD: 25, B_LX: 33, B_KV: 45, B_MLRU: 61, B_Q: 69, B_MMEM: 77, B_OUT: 85,
        B_FL: 93, B_M2: 94, B_OUT2: 118}
BASE, ARENA = 16512, 212800
MAGIC = 12582912.0
def build(nc, A, out):
    f32, f32r = mybir.dt.float32, mybir.dt.float32r
    ALU, ACT, AX = mybir.AluOpType, mybir.ActivationFunctionType, mybir.AxisListType
    mult, add, sub, vmin, vmax = ALU.mult, ALU.add, ALU.subtract, ALU.min, ALU.max

    ctx = ExitStack()
    with ctx:
        ctx.enter_context(nc.sbuf_tensor("arena", [P, ARENA // 4], f32))

        def at(name, shape, kb, dt=f32):
            size = 4
            for s in shape[1:]:
                size *= s
            assert kb * 1024 + size <= ARENA, (name, kb, size)
            return nc.alloc_sbuf_tensor_at(name, shape, dt, offset=BASE + int(kb * 1024))

        def sem(name):
            return ctx.enter_context(nc.semaphore(name))

        h_hi, h_lo = at("h_hi", [P, KT, SEQ], 0, f32r), at("h_lo", [P, KT, SEQ], 16, f32r)
        raw = at("raw", [P, RAW, KT * P], 32)
        w_hi, w_lo = at("w_hi", [P, SLOTS, KT, P], 40, f32r), at("w_lo", [P, SLOTS, KT, P], 56, f32r)
        pcol = at("pcol", [P, NPC], 72)
        ones = at("ones", [P, P], 74.5)
        ident = at("ident", [P, P], 75)
        tril = at("tril", [P, P], 75.5)
        negm = at("negm", [P, P], 76)
        small = at("small", [P, 512], 76.5)
        tmp = [at(f"tmp{i}", [P, SEQ], 79 + 2 * i) for i in range(6)]
        tmp_r = at("tmp_r", [P, SEQ], 91, f32r)
        REG = 93
        xs = at("xs", [P, XBC_T, SEQ], REG)
        y_hi = at("y_hi", [P, 16, SEQ], REG, f32r)
        y_lo = at("y_lo", [P, 16, SEQ], REG + 48, f32r)
        W0 = REG + 80
        x_t = at("x_t", [P, KT, SEQ], REG + 48)
        acs = at("acs", [32, SEQ], W0)
        dt_c = at("dt_c", [32, SEQ], W0 + 2)
        b_cur = at("b_cur", [P, SEQ], W0 + 2)
        tok = at("tok", [P, 4, NCH, 32], W0 + 4)
        b_tok = at("b_tok", [P, NCH, P], W0 + 6)
        cb = at("cb", [P, NCH, P], W0 + 8)
        xdt = at("xdt", [P, NCH, P], W0 + 10)
        xde = at("xde", [P, NCH, P], W0 + 12)
        prev = at("prev", [P, NCH - 1, P], W0 + 14)
        ebc = at("ebc", [P, SEQ], W0 + 16)
        accm = at("accm", [32, 2, SEQ], W0 + 18)
        x_cur, seg, z_silu, y_tmp = tmp[0], [tmp[1], tmp[2]], tmp[3], tmp[4]
        merged = at("merged", [P, KT, SEQ], REG + 80)
        xl = at("xl", [P, LRU_T, SEQ], REG)
        l_hi = at("l_hi", [P, LRU_T, SEQ], REG, f32r)
        l_lo = at("l_lo", [P, LRU_T, SEQ], REG + 24, f32r)
        xl_hi, xl_lo = at("xl_hi", [P, 3, SEQ], REG + 48, f32r), at("xl_lo", [P, 3, SEQ], REG + 54, f32r)
        l_r, l_i, l_a = (at(n, [P, 3, SEQ], REG + o) for n, o in (("l_r", 60), ("l_i", 66), ("l_a", 72)))
        mem_t = at("mem_t", [P, KT, MEM], REG + 48)
        mk = at("mk", [P, KT, MEM], REG + 48)
        mv = at("mv", [P, 2, DM], REG + 56)
        m_hi, m_lo = at("m_hi", [P, KT, MEM], REG + 64, f32r), at("m_lo", [P, KT, MEM], REG + 72, f32r)
        q = at("q", [P, KT, SEQ], REG)
        ym_hi, ym_lo = at("ym_hi", [P, KT, SEQ], REG + 16, f32r), at("ym_lo", [P, KT, SEQ], REG + 32, f32r)
        probs = at("probs", [P, 4, MEM], REG + 64)
        probs_t = at("probs_t", [P, 2, SEQ], REG + 68)
        g_hi, g_lo = at("g_hi", [P, KT, SEQ], REG + 48, f32r), at("g_lo", [P, KT, SEQ], REG + 64, f32r)
        x1 = at("x1", [P, KT, SEQ], REG)

        x2_keep = nc.dram_tensor("x2_keep", (P, KT, SEQ), f32, kind="Internal").ap()
        u5 = at("u5", [P, 6, SEQ], REG)
        gs = at("gs", [P, 6, SEQ], REG + 12)
        s_lo, s_hi = at("s_lo", [P, 6, SEQ], REG, f32r), at("s_hi", [P, 6, SEQ], REG + 12, f32r)
        fq, fk = at("fq", [P, 6, SEQ], REG + 24), at("fk", [P, 6, SEQ], REG + 36)
        fv = at("fv", [P, NCH, 6 * P], REG + 48)
        fg = at("fg", [P, 6, SEQ], REG + 60)
        turn_v = at("turn_v", [P, 24, 32, 2], REG + 103)
        turn_u = at("turn_u", [P, 24, 16, 2], REG + 109)
        et = at("et", [P, 2, 2, SEQ], REG + 72)
        s5m = at("s5m", [P, 512], REG + 80)
        cf = at("cf", [P, 4, 2, 32], REG + 82)
        v_tmp = at("v_tmp", [P, SEQ], REG + 83)
        sc5 = at("sc5", [P, 20, 24], REG + 112)
        sum_f = at("sum_f", [P, SEQ], REG + 98)
        pool_t = at("pool_t", [P, SEQ], REG + 85)
        u_cur = at("u_cur", [P, SEQ], REG + 87)
        y5_hi, y5_lo = at("y5_hi", [P, 6, SEQ], REG + 72, f32r), at("y5_lo", [P, 6, SEQ], REG + 84, f32r)
        fq_cur = [at(f"fq_cur{e}", [P, SEQ], REG + 72 + 2 * e) for e in range(2)]
        fv_cur = at("fv_cur", [P, NCH, P], REG + 76)
        f_p = [at(f"f_p{t}", [P, SEQ], REG + 78 + 2 * t) for t in range(4)]
        f_pt = [at(f"f_pt{t}", [P, SEQ], REG + 86 + 2 * t) for t in range(4)]
        fm = at("fm", [P, SEQ], REG + 94)
        f_hi, f_lo = at("f_hi", [P, 6, SEQ], REG + 24, f32r), at("f_lo", [P, 6, SEQ], REG + 36, f32r)
        mem2 = at("mem2", [P, KT, MEM], REG + 48)
        mk2, mv2 = at("mk2", [P, 4, MEM], REG + 48), at("mv2", [P, 2, SEQ], REG + 52)
        m2_hi, m2_lo = at("m2_hi", [P, KT, MEM], REG + 56, f32r), at("m2_lo", [P, KT, MEM], REG + 64, f32r)
        yn_hi, yn_lo = at("yn_hi", [P, 4, SEQ], REG + 56, f32r), at("yn_lo", [P, 4, SEQ], REG + 64, f32r)
        gm = at("gm", [P, 4, SEQ], REG + 72)
        q2 = at("q2", [P, 4, SEQ], REG + 80)
        probs2, probs2_t = at("probs2", [P, 4, MEM], REG + 88), at("probs2_t", [P, 2, SEQ], REG + 92)
        g2_hi, g2_lo = at("g2_hi", [P, KT, SEQ], REG + 72, f32r), at("g2_lo", [P, KT, SEQ], REG + 88, f32r)
        x3 = at("x3", [P, KT, SEQ], REG)

        bank = [ctx.enter_context(nc.psum_tensor(f"bank{i}", [P, SEQ], f32)) for i in range(8)]
        acc = bank[0:2]
        p_gate, p_x, p_bc, p_y, p_off, p_st = bank[2], bank[2], bank[3:5], bank[5], bank[6], bank[7]
        p_norm = bank[7]

        address_step, s_act, s_dve, s_pe, s_pool = (sem(f"{n}_step") for n in ("address", "act", "dve", "pe", "pool"))
        raw_ready = [sem(f"raw_ready{i}") for i in range(RAW)]
        x_loaded, par_loaded, mem_loaded, xre_loaded, out_stored = (
            sem(n) for n in ("x_loaded", "par_loaded", "mem_loaded", "xre_loaded", "out_stored"))
        consts_ready, hi_ready, lo_ready, block_done, acc_free = (
            sem(n) for n in ("consts_ready", "hi_ready", "lo_ready", "block_done", "acc_free"))
        sq_ready, sq_summed, root_ready, split_in, split_hi, split_lo = (
            sem(n) for n in ("sq_ready", "sq_summed", "root_ready", "split_in", "split_hi", "split_lo"))
        u_ready, eu_ready, conv_ready, silu_done = (sem(n) for n in ("u_ready", "eu_ready", "conv_ready", "silu_done"))
        a_exp, acs_ready, tok_t, tok_sub, tok_exp = (
            sem(n) for n in ("a_exp", "acs_ready", "tok_t", "tok_sub", "tok_exp"))
        bcur_ready, b_t, btok_ready, cb_mm, cb_ready, x_cur_ready, x_tr, accm_ready, bc_mm = (
            sem(n) for n in ("bcur_ready", "b_t", "btok_ready", "cb_mm", "cb_ready", "x_cur_ready", "x_tr",
                             "accm_ready", "bc_mm"))
        xd_ready, seg_ready, exp_ready, g_ready, ebc_ready, st_mm, prev_ready, y_mm, z_ready, y_ready = (
            sem(n) for n in ("xd_ready", "seg_ready", "exp_ready", "g_ready", "ebc_ready", "st_mm",
                             "prev_ready", "y_mm", "z_ready", "y_ready"))
        gsq_ready, gsum_mm, groot_ready, gn_in, gn_hi, gn_lo, gn_done = (
            sem(n) for n in ("gsq_ready", "gsum_mm", "groot_ready", "gn_in", "gn_hi", "gn_lo", "gn_done"))
        gate_ready, merge_done = sem("gate_ready"), sem("merge_done")
        lx_done, lam_ready, xlh_ready, xls_ready, gmm_done, sig_ready, dec_ready, m2_ready, m_ready = (
            sem(n) for n in ("lx_done", "lam_ready", "xlh_ready", "xls_ready", "gmm_done", "sig_ready", "dec_ready",
                             "m2_ready", "m_ready"))
        lsilu_ready, ly_in, ly_hi, ly_done = (sem(n) for n in ("lsilu_ready", "ly_in", "ly_hi", "ly_done"))
        kv_ready, v_tr = sem("kv_ready"), sem("v_tr")
        q_ready, sc_mm, mx_ready, pe_ready, pn_ready, p_tr, pt_ready, o_mm, yo_in, yo_hi, yo_done = (
            sem(n) for n in ("q_ready", "sc_mm", "mx_ready", "pe_ready", "pn_ready", "p_tr", "pt_ready", "o_mm",
                             "yo_in", "yo_hi", "yo_done"))
        mg_hi, mg_done, x1_ready = sem("mg_hi"), sem("mg_done"), sem("x1_ready")
        x2_ready, x2_kept, nu_ready, enu_ready, f_ready = (
            sem(n) for n in ("x2_ready", "x2_kept", "nu_ready", "enu_ready", "f_ready"))
        acc_read, step_ready, t_exp, tables_ready = (
            sem(n) for n in ("acc_read", "step_ready", "t_exp", "tables_ready"))
        s5_loaded, fpt_dve, u_cur_ready, address_step2 = (sem(n) for n in ("s5_loaded", "fpt_dve", "u_cur_ready", "address_step2"))
        e_made, e_used, pq_mm, h_ready, h_free, cf_ready, y5_sq, y5_arg, y5_sig, y5_ready, v_evac, v5_tr = (
            sem(n) for n in ("e_made", "e_used", "pq_mm", "h_ready", "h_free", "cf_ready", "y5_sq", "y5_arg", "y5_sig",
                             "y5_ready", "v_evac", "v5_tr"))
        y5h, y5l, glu_ready, s5_in, s5_hi, s5_done = (
            sem(n) for n in ("y5h", "y5l", "glu_ready", "s5_in", "s5_hi", "s5_done"))
        fz_ready, fcur_ready, fm_ready, fs_mm, fmx_ready, fe_ready, fn_ready, fp_tr, fpt_ready, fo_mm, fo_ready = (
            sem(n) for n in ("fz_ready", "fcur_ready", "fm_ready", "fs_mm", "fmx_ready", "fe_ready", "fn_ready",
                             "fp_tr", "fpt_ready", "fo_mm", "fo_ready"))
        fh, fl_done, mem2_loaded, kv2_ready, v2_tr, mv2_ready, qg_ready = (
            sem(n) for n in ("fh", "fl_done", "mem2_loaded", "kv2_ready", "v2_tr", "mv2_ready", "qg_ready"))
        sc2_mm, mx2_ready, e2_ready, n2_ready, p2_tr, p2t_ready, o2_mm, yn_in, yn_hi_ready, yn_done = (
            sem(n) for n in ("sc2_mm", "mx2_ready", "e2_ready", "n2_ready", "p2_tr", "p2t_ready", "o2_mm", "yn_in",
                             "yn_hi_ready", "yn_done"))
        gate2_ready, merge2_done, mg2_hi, mg2_done, x3_loaded, x3_ready, fin_ready = (
            sem(n) for n in ("gate2_ready", "merge2_done", "mg2_hi", "mg2_done", "x3_loaded", "x3_ready", "fin_ready"))

        class Steps:

            def __init__(self, eng, own):
                self.eng, self.own, self.n, self.turn = eng, own, 0, 0

            def __call__(self, ins):
                ins.then_inc(self.own, 1)
                self.n += 1
                self.eng.wait_ge(self.own, self.turn + self.n)

            def loop(self, count, steps, body):
                first = self.n
                with self.eng.Fori(0, count) as i:
                    self.turn = i * steps
                    body(i)
                assert self.n - first == steps, f"{self.own}: {self.n - first} steps in a turn, not {steps}"
                self.turn, self.n = 0, first + count * steps

        def made(eng, ins, what, value):
            ins.then_inc(what, 1)
            eng.wait_ge(what, value)

        def col(name, j=0, rows=P):
            return pcol[0:rows, bass.ds(j + PC[name], 1)]

        def col12(name):
            return pcol[:, PC[name]:PC[name] + 12]

        def score(t):
            return bank[3 + t // 2][:, (t % 2) * MEM:(t % 2 + 1) * MEM]

        def scol(j, n=1, rows=P):
            return small[0:rows, j:j + n]

        block = ctx.enter_context(nc.Block())

        @block.sync
        def _(sp):
            sp.dma_start(x_t[:], A["x_t"]).then_inc(x_loaded, 16)
            sp.dma_start(pcol[:], A["pcol"]).then_inc(par_loaded, 16)
            for b in range(RAW):
                sp.dma_start(raw[:, b], A["wstream"][b]).then_inc(raw_ready[b], 16)

            def two_blocks(i):
                for r in range(RAW):
                    sp.wait_ge(lo_ready, i * RAW + (r + 1))
                    sp.dma_start(raw[:, r], A["wstream"][bass.ds(i * RAW + (RAW + r), 1)].rearrange("o p c -> (o p) c")
                                 ).then_inc(raw_ready[r], 16)
            with sp.Fori(0, (B_END - RAW) // RAW) as i:
                two_blocks(i)
            for b in range(B_END - (B_END - RAW) % RAW, B_END):
                sp.wait_ge(lo_ready, b - RAW + 1)
                sp.dma_start(raw[:, b % RAW], A["wstream"][b]).then_inc(raw_ready[b % RAW], 16)
            sp.wait_ge(out_stored, 16 * KT)

        @block.gpsimd
        def _(pool):
            step = Steps(pool, s_pool)
            step(pool.memset(ones[:], 1.0))
            step(pool.memset(negm[:], 0.0))
            step(pool.affine_select(out=ident[:], in_=ones[:], compare_op=ALU.is_equal, fill=0.0, base=0,
                                    pattern=[[-1, P]], channel_multiplier=1))
            step(pool.affine_select(out=tril[:], in_=ones[:], compare_op=ALU.is_ge, fill=0.0, base=0,
                                    pattern=[[1, P]], channel_multiplier=-1))
            made(pool, pool.affine_select(out=negm[:], in_=negm[:], compare_op=ALU.is_ge, fill=-1e30, base=0,
                                          pattern=[[-1, P]], channel_multiplier=1), consts_ready, 1)

            def lower_parts(first, off, count):
                for b in range(first, first + count):
                    pool.wait_ge(hi_ready, off + (b + 1))
                    made(pool, pool.tensor_tensor(w_lo[:, b % SLOTS].rearrange("p k c -> p (k c)"), raw[:, b % RAW],
                                                  w_hi[:, b % SLOTS].rearrange("p k c -> p (k c)").bitcast(f32), sub),
                         lo_ready, off + (b + 1))
            lower_parts(0, 0, SLOTS)
            with pool.Fori(1, B_FOX // SLOTS) as i:
                lower_parts(0, i * SLOTS, SLOTS)
            for b in range(B_FOX // SLOTS * SLOTS, B_FOX):
                lower_parts(b, 0, 1)
            pool.wait_ge(tables_ready, 1)

            def powers(j):
                for r in range(4):
                    lower_parts(B_FOX + r, j * 4, 1)
                    s, e = j * 4 + r, et[:, r % 2]
                    pool.wait_ge(e_used, s + 1)

                    def u(c):
                        return turn_u[:, bass.ds(s, 1), :, c].rearrange("p o a -> p (o a)").unsqueeze(2).to_broadcast([P, 16, 32])

                    def v(c):
                        return turn_v[:, bass.ds(s, 1), :, c].to_broadcast([P, 16, 32])
                    w = [x.rearrange("p (a b) -> p a b", a=16) for x in (e[:, 0], e[:, 1], pool_t[:])]

                    def product(out, a, b):
                        pool.sem_inc(address_step2, 1)
                        step(pool.tensor_tensor(out, a, b, mult))
                    product(w[0], u(0), v(0))
                    product(w[2], u(1), v(1))
                    step(pool.tensor_tensor(e[:, 0], e[:, 0], pool_t[:], sub))
                    product(w[1], u(0), v(1))
                    product(w[2], u(1), v(0))
                    made(pool, pool.tensor_tensor(e[:, 1], e[:, 1], pool_t[:], add), e_made, s + 1)
            step.loop(6, 20, powers)
            first = B_FOX + 24
            for b in range(first, -(-first // SLOTS) * SLOTS):
                lower_parts(b, 0, 1)
            with pool.Fori(-(-first // SLOTS), B_END // SLOTS) as i:
                lower_parts(0, i * SLOTS, SLOTS)
            for b in range(B_END // SLOTS * SLOTS, B_END):
                lower_parts(b, 0, 1)

        @block.scalar
        def _(act):
            step = Steps(act, s_act)

            def activate(out, *args, **more):
                act.sem_inc(address_step, 1)
                return act.activation(out, *args, **more)

            def upper(b, off):
                act.wait_ge(raw_ready[b % RAW], off * 8 + 16 * (b // RAW + 1))
                made(act, act.activation(w_hi[:, b % SLOTS].rearrange("p k c -> p (k c)"), raw[:, b % RAW], ACT.Copy),
                     hi_ready, off + (b + 1))

            def turn(b, off, more=True):
                act.wait_ge(block_done, off + (b + 1))
                if more:
                    upper(b + SLOTS, off)

            def squares(k, x, value):
                if k >= 2:
                    act.wait_ge(sq_summed, value - 2)
                made(act, act.activation(tmp[k % 2][:, 0:x.shape[1]], x, ACT.Square), sq_ready, value)

            def norm(t, x, ntiles, sq0, n):
                for k in range(ntiles):
                    squares(k, x(k), sq0 + k + 1)
                act.wait_ge(sq_summed, sq0 + ntiles)
                made(act, act.activation(tmp[2][:, 0:n], p_norm[:, 0:n], ACT.Sqrt, scale=1.0 / DM, bias=EPS),
                     root_ready, t + 1)

            def split(n0, ntiles, hi):
                for k in range(ntiles):
                    act.wait_ge(split_in, n0 + k + 1)
                    made(act, act.activation(hi[:, k], tmp[k % 2][:, 0:hi.shape[2]], ACT.Copy), split_hi, n0 + k + 1)

            for b in range(SLOTS):
                upper(b, 0) if b < RAW else None
            act.wait_ge(x_loaded, 16)
            norm(0, lambda k: x_t[:, k], KT, 0, SEQ)
            for b in range(RAW, SLOTS):
                upper(b, 0)
            split(0, KT, h_hi)

            turn(B_DT, 0)
            act.wait_ge(u_ready, 1)
            step(act.activation(tmp[1][0:32], tmp[0][0:32], ACT.Abs))
            made(act, act.activation(tmp[1][0:32], tmp[1][0:32], ACT.Exp, scale=-1.0), eu_ready, 1)
            made(act, act.activation(scol(0, 1, 32), col("a_log", 0, 32), ACT.Exp), a_exp, 1)

            def xbc(i):
                for r in range(4):
                    turn(B_XBC + r, i * 4)
                    act.wait_ge(conv_ready, i * 4 + (r + 1))
                    made(act, activate(xs[:, bass.ds(i * 4 + r, 1)].rearrange("p o t -> p (o t)"), tmp[2 + r % 2][:], ACT.Silu), silu_done, i * 4 + (r + 1))
            step.loop(XBC_T // 4, 0, xbc)

            act.wait_ge(tok_sub, 1)
            step(act.activation(tok[:, 2], tok[:, 2], ACT.Exp))
            made(act, act.activation(tok[:, 3].rearrange("p c h -> p (c h)"), p_x[:, 256:384], ACT.Exp), tok_exp, 1)

            def group(g):
                made(act, activate(b_cur[:], xs[:, bass.ds(g + 16, 1)].rearrange("p o t -> p (o t)"), ACT.Copy), bcur_ready, g + 1)
                act.wait_ge(b_t, g + 1)
                made(act, act.activation(b_tok[:].rearrange("p c n -> p (c n)"), p_x[:], ACT.Copy), btok_ready, g + 1)
                for r in range(4):
                    pair = g * 4 + r
                    made(act, activate(x_cur[:], xs[:, bass.ds(pair, 1)].rearrange("p o t -> p (o t)"), ACT.Copy),
                         x_cur_ready, pair + 1)
                    for e in range(2):
                        act.wait_ge(seg_ready, pair * 2 + (e + 1))
                        made(act, act.activation(seg[e][:], seg[e][:], ACT.Exp), exp_ready, pair * 2 + (e + 1))
                        ins = act.activation(ebc[64 * e:64 * e + 64], p_bc[e][64 * e:64 * e + 64, :], ACT.Exp)
                        made(act, ins, ebc_ready, pair * 2 + (e + 1))
                    turn(B_Z + r, g * 4)
                    made(act, act.activation(z_silu[:], acc[r % 2][:], ACT.Silu), z_ready, pair + 1)
                act.wait_ge(y_ready, g * 4 + 4)
                for r in range(4):
                    if r >= 2:
                        act.wait_ge(gsum_mm, g * 4 + (r - 1))
                    made(act, activate(tmp[r % 2][:], xs[:, bass.ds(g * 4 + r, 1)].rearrange("p o t -> p (o t)"),
                                             ACT.Square), gsq_ready, g * 4 + (r + 1))
                act.wait_ge(gsum_mm, g * 4 + 4)
                made(act, act.activation(tmp[2][:], p_norm[:], ACT.Sqrt, scale=1.0 / 512, bias=EPS), groot_ready, g + 1)
                for r in range(4):
                    t = g * 4 + (r + 1)
                    act.wait_ge(gn_in, t)
                    made(act, act.activation(tmp_r[:], tmp[r % 2][:], ACT.Copy), gn_hi, t)
                    made(act, activate(y_hi[:, bass.ds(g * 4 + r, 1)].rearrange("p o t -> p (o t)"),
                                             tmp[r % 2][:], ACT.Copy), gn_done, t)
                    act.wait_ge(gn_lo, t)
            step.loop(4, 0, group)

            def merge(base, per, gate0):
                tiles = 4 if per == 3 else 2

                def body(i):
                    for r in range(tiles):
                        for x in range(per):
                            turn(base + per * r + x, i * (tiles * per))
                            if x == 0:
                                v = i * tiles + (gate0 + r + 1)
                                made(act, act.activation(tmp[2 + r % 2][:], p_gate[:], ACT.Sigmoid), gate_ready, v)
                        act.wait_ge(merge_done, v)
                return body, KT // tiles

            body, count = merge(B_MSSD, 3, 0)
            step.loop(count, 0, body)

            def lru_x(i):
                for r in range(4):
                    turn(B_LX + r, i * 4)
            step.loop(LRU_T // 4, 0, lru_x)
            step(act.activation(scol(40, 12), col12("lru_lam"), ACT.Abs))
            made(act, act.activation(scol(52, 12), scol(40, 12), ACT.Exp, scale=-1.0), lam_ready, 1)
            act.wait_ge(lam_ready, 2)

            def lru_gates(i):
                for half in range(2):
                    g = i * 2 + half
                    for t in range(3):
                        if half or t:
                            pass
                        act.wait_ge(lx_done, g * 3 + (t + 1))
                        made(act, activate(xl_hi[:, t], xl[:, bass.ds(g * 3 + t, 1)].rearrange("p o t -> p (o t)"),
                                                 ACT.Copy), xlh_ready, g * 3 + (t + 1))
                    for t in range(3):
                        turn(B_LG + 6 * half + t, i * 12)
                        step(activate(l_r[:, t], bank[2 + (t % 2) * 2][:], ACT.Sigmoid, bias=col("lru_b_a", g * 3 + t)))
                        made(act, activate(l_i[:, t], bank[3 + (t % 2) * 2][:], ACT.Sigmoid,
                                                 bias=col("lru_b_x", g * 3 + t)), sig_ready, g * 3 + (t + 1))
                    for t in range(3):
                        step(activate(l_a[:, t], l_r[:, t], ACT.Exp, scale=small[:, bass.ds(g * 3 + (t + 64), 1)]))
                        step(activate(l_r[:, t], l_r[:, t], ACT.Tanh, scale=small[:, bass.ds(g * 3 + (t + 76), 1)]))
                    for t in range(3):
                        made(act, act.activation(tmp[2][:], l_a[:, t], ACT.Square), dec_ready, g * 3 + (t + 1))
                        act.wait_ge(m2_ready, g * 3 + (t + 1))
                    made(act, act.activation(l_r[:].rearrange("p t n -> p (t n)"), l_r[:].rearrange("p t n -> p (t n)"),
                                             ACT.Sqrt), m_ready, g + 1)
                    for t in range(3):
                        turn(B_LG + 6 * half + 3 + t, i * 12)
                        v = g * 3 + (t + 1)
                        made(act, act.activation(tmp[2 + t % 2][:], acc[(half + t) % 2][:], ACT.Silu), lsilu_ready, v)
                        act.wait_ge(ly_in, v)
                        made(act, activate(l_hi[:, bass.ds(g * 3 + t, 1)].rearrange("p o t -> p (o t)"),
                                                 tmp[4 + t % 2][:], ACT.Copy), ly_hi, v)
            step.loop(2, 18, lru_gates)

            act.wait_ge(ly_done, LRU_T)
            act.dma_start(mem_t[:], A["mem_t"]).then_inc(mem_loaded, 16)
            act.wait_ge(mem_loaded, 16)
            norm(1, lambda k: mem_t[:, k], KT, KT, MEM)
            split(KT, KT, m_hi)

            def kv(i):
                for r in range(4):
                    turn(B_KV + r, i * 4)
            step.loop(MEMKV_T // 4, 0, kv)
            act.wait_ge(step_ready, 1)
            step(act.activation(sc5[:, 3], sc5[:, 1], ACT.Sin))
            step(act.activation(sc5[:, 4], sc5[:, 1], ACT.Sin, scale=0.5))
            step(act.activation(sc5[:, 5], sc5[:, 2], ACT.Tanh, scale=0.5))
            step(act.activation(sc5[:, 7], sc5[:, 6], ACT.Exp))
            made(act, act.activation(sc5[:, 8], sc5[:, 9], ACT.Exp), t_exp, 1)
            body, count = merge(B_MLRU, 3, KT)
            step.loop(count, 0, body)

            def queries(i):
                for r in range(4):
                    turn(B_Q + r, i * 4)
            step.loop(2, 0, queries)

            for h in range(4):
                for t in range(4):
                    act.wait_ge(mx_ready, h + 1)
                    ins = act.activation(probs[:, t], score(t), ACT.Exp, scale=1.0 / 16, bias=scol(100 + t),
                                         accum_out=scol(104 + t))
                    made(act, ins, pe_ready, 4 * h + t + 1)
                for d in range(2):
                    v = 2 * h + d + 1
                    act.wait_ge(yo_in, v)
                    made(act, act.activation(ym_hi[:, 2 * h + d], tmp[d][:], ACT.Copy), yo_hi, v)

            def merge_mem(i):
                for r in range(2):
                    turn(B_MMEM + 2 * r, i * 4)
                    v = i * 2 + (r + 1)
                    made(act, act.activation(tmp[2 + r % 2][:], p_gate[:], ACT.Sigmoid), gate_ready, v + 2 * KT)
                    turn(B_MMEM + 2 * r + 1, i * 4)
                    act.wait_ge(merge_done, v + 2 * KT)
                    made(act, activate(g_hi[:, bass.ds(i * 2 + r, 1)].rearrange("p o t -> p (o t)"),
                                             merged[:, bass.ds(i * 2 + r, 1)].rearrange("p o t -> p (o t)"), ACT.Copy),
                         mg_hi, v)
            step.loop(4, 0, merge_mem)
            act.dma_start(x1[:], A["x_t"]).then_inc(xre_loaded, 16)

            def outs(i):
                for r in range(4):
                    turn(B_OUT + r, i * 4)
            step.loop(2, 0, outs)

            for k in range(KT):
                act.wait_ge(x1_ready, k + 1)
                squares(k, x1[:, k], 2 * KT + k + 1)
            act.wait_ge(sq_summed, 3 * KT)
            made(act, act.activation(tmp[2][:], p_norm[:], ACT.Sqrt, scale=1.0 / DM, bias=EPS), root_ready, 3)
            for k in range(KT):
                act.wait_ge(x2_ready, k + 1)
                squares(k, x1[:, k], 3 * KT + k + 1)
            act.dma_start(x2_keep, x1[:]).then_inc(x2_kept, 16)
            act.wait_ge(sq_summed, 4 * KT)
            made(act, act.activation(tmp[2][:], p_norm[:], ACT.Sqrt, scale=1.0 / DM, bias=EPS), root_ready, 4)
            split(2 * KT, KT, h_hi)

            turn(B_FL, 0)
            act.wait_ge(nu_ready, 1)
            step(act.activation(tmp[1][0:12], tmp[0][0:12], ACT.Abs))
            made(act, act.activation(tmp[1][0:12], tmp[1][0:12], ACT.Exp, scale=-1.0), enu_ready, 1)
            act.wait_ge(x2_kept, 16)
            act.sem_inc(acc_read, 2)

            def tile(x, j):
                return x[:, bass.ds(j, 1)].rearrange("p o t -> p (o t)")

            def read(out, *args, n, **more):
                made(act, activate(out, *args, **more), acc_read, n + 3)

            def u_gs(i):
                for r in range(4):
                    turn(B_UG + r, i * 4)
                    j, n = i * 2 + r // 2, i * 4 + r
                    read(tile(gs if r % 2 else u5, j), acc[r % 2][:], ACT.Silu if r % 2 else ACT.Copy, n=n)
            step.loop(3, 0, u_gs)
            act.dma_start(s5m[:], A["s5m"][0]).then_inc(s5_loaded, 16)

            def fox_s5(j):
                made(act, activate(u_cur[:], tile(u5, j), ACT.Copy), u_cur_ready, j + 1)
                for r in range(4):
                    turn(B_FOX + r, j * 4)
                    n = j * 4 + (12 + r)
                    if r == 0:
                        read(tile(fq, j), acc[0][:], ACT.Copy, n=n, scale=0.125)
                    elif r == 1:
                        read(tile(fk, j), acc[1][:], ACT.Copy, n=n)
                    elif r == 2:
                        read(v_tmp[:], acc[0][:], ACT.Copy, n=n)
                    else:
                        read(tile(fg, j), acc[1][:], ACT.Silu, n=n)
                act.dma_start(s5m[:], A["s5m"][bass.ds(j + 1, 1)].rearrange("o p c -> (o p) c")).then_inc(s5_loaded, 16)
                act.wait_ge(v5_tr, j + 1)
                made(act, activate(fv[:, :, bass.ds(j * P, P)], bank[7][:].rearrange("p (k d) -> p k d", k=NCH), ACT.Copy),
                     v_evac, j + 1)
                act.wait_ge(y5_ready, j * 2 + 1)
                made(act, activate(tmp[0][:], tile(u5, j), ACT.Square), y5_sq, j + 1)
                act.wait_ge(y5_arg, j + 1)
                made(act, act.activation(tmp[1][:], tmp[0][:], ACT.Sigmoid, scale=2 * SQRT_2_OVER_PI), y5_sig, j + 1)
            step.loop(6, 0, fox_s5)

            act.wait_ge(s5_loaded, 16 * 7)
            for j in range(6):
                act.wait_ge(y5_ready, 12)
                made(act, act.activation(y5_hi[:, j], u5[:, j], ACT.Copy), y5h, j + 1)
            for j in range(6):
                turn(B_GLU + j, 0)
                made(act, act.activation(tmp[2 + j % 2][:], acc[j % 2][:], ACT.Sigmoid, bias=col("b_glu", j)), acc_read, 2 + 36 + j + 1)
                act.wait_ge(s5_in, j + 1)
                made(act, act.activation(s_hi[:, j], tmp[j % 2][:], ACT.Copy), s5_hi, j + 1)

            act.wait_ge(fz_ready, 1)

            def fox(j):
                for e in range(2):
                    hs = slice(64 * e, 64 * e + 64)
                    step(activate(fq_cur[e][hs], fq[hs, bass.ds(j, 1)].rearrange("p o t -> p (o t)"), ACT.Copy))
                made(act, activate(fv_cur[:], fv[:, :, bass.ds(j * P, P)], ACT.Copy), fcur_ready, j + 1)
                for e in range(2):
                    h = j * 2 + e
                    for t in range(4):
                        w = (t + 1) * P
                        act.wait_ge(fmx_ready, h * 4 + (t + 1))
                        made(act, act.activation(f_p[t][:, 0:w], bank[2 + t][:, 0:w], ACT.Exp, bias=scol(304 + t),
                                                 accum_out=scol(308 + t)), fe_ready, h * 4 + (t + 1))
                    for k in range(2):
                        act.wait_ge(fp_tr, h * 4 + (2 * k + 1))
                        kk = 2 * k
                        made(act, act.activation(f_pt[kk][:, kk * P:], bank[2 + kk][:, kk * P:], ACT.Copy), fpt_ready,
                             h * 2 + (k + 1))
                act.wait_ge(fo_mm, j * 2 + 2)
            step.loop(6, 2, fox)
            act.wait_ge(fo_ready, 6)
            for j in range(6):
                made(act, act.activation(f_hi[:, j], fg[:, j], ACT.Copy), fh, j + 1)

            act.wait_ge(fl_done, 6)
            act.dma_start(mem2[:], A["mem2_t"]).then_inc(mem2_loaded, 16)
            act.wait_ge(mem2_loaded, 16)
            norm(4, lambda k: mem2[:, k], KT, 4 * KT, MEM)
            split(3 * KT, KT, m2_hi)
            for j in range(8):
                turn(B_KV2 + j, 0)
                if j < 4:
                    made(act, act.activation(mk2[:, j], acc[j % 2][:, 0:MEM], ACT.Copy), acc_read, 2 + 42 + j + 1)
                else:
                    made(act, act.activation(tmp[j % 2][:, 0:MEM], acc[j % 2][:, 0:MEM], ACT.Copy), acc_read, 2 + 42 + j + 1)
                    act.wait_ge(v2_tr, j - 3)
                    made(act, act.activation(mv2[:, :, (j - 4) * P:(j - 3) * P],
                                             bank[3 + j % 2][:, 0:MEM].rearrange("p (m d) -> p m d", m=2), ACT.Copy),
                         mv2_ready, j - 3)

            def q_gm(i):
                for r in range(4):
                    turn(B_QG + r, i * 4)
                    j, n = i * 2 + r // 2, i * 4 + (50 + r)
                    read(tile(gm if r % 2 else q2, j), acc[r % 2][:], ACT.Silu if r % 2 else ACT.Copy, n=n)
            step.loop(2, 0, q_gm)
            for h in range(4):
                for t in range(4):
                    act.wait_ge(mx2_ready, h + 1)
                    made(act, act.activation(probs2[:, t], score(t), ACT.Exp, scale=P ** -0.5, bias=scol(100 + t),
                                             accum_out=scol(104 + t)), e2_ready, 4 * h + t + 1)
                act.wait_ge(yn_in, h + 1)
                made(act, act.activation(yn_hi[:, h], tmp[h % 2][:], ACT.Copy), yn_hi_ready, h + 1)

            def merge2(i):
                for r in range(2):
                    for n in range(3):
                        v = i * 6 + (3 * r + n + 1)
                        turn(B_M2 + 6 * r + 2 * n, i * 12)
                        made(act, activate(tmp[2 + (r + n) % 2][:], p_gate[:], ACT.Sigmoid,
                                           bias=col("b_merge", i * 2 + (r + n * KT))), gate2_ready, v)
                        turn(B_M2 + 6 * r + 2 * n + 1, i * 12)
                        act.wait_ge(merge2_done, v)
                    v = i * 2 + (r + 1)
                    made(act, activate(tile(g2_hi, i * 2 + r), tmp[4][:], ACT.Copy), mg2_hi, v)
            step.loop(4, 0, merge2)
            act.dma_start(x3[:], x2_keep).then_inc(x3_loaded, 16)
            for j in range(8):
                turn(B_OUT2 + j, 0, more=B_OUT2 + j + SLOTS < B_END)
                act.wait_ge(x3_ready, j + 1)
                squares(j, x3[:, j], 5 * KT + j + 1)
            act.wait_ge(sq_summed, 6 * KT)
            made(act, act.activation(tmp[2][:], p_norm[:], ACT.Sqrt, scale=1.0 / DM, bias=EPS), root_ready, 6)
            for k in range(KT):
                act.wait_ge(fin_ready, k + 1)
                act.dma_start(out[:, k], x3[:, k]).then_inc(out_stored, 16)

        @block.vector
        def _(dve):
            step = Steps(dve, s_dve)

            def flat(ap):
                return ap.rearrange("p o t -> p (o t)")

            def tile(x, j):
                return flat(x[:, bass.ds(j, 1)])

            def free_acc(value):
                dve.sem_inc(acc_free, 1)

            def norm_split(t, n0, x, g, ntiles, hi, lo, n, dst=None):
                dve.wait_ge(root_ready, t + 1)
                step(dve.reciprocal(tmp[3][:, 0:n], tmp[2][:, 0:n]))

                def lower(k):
                    dve.wait_ge(split_hi, n0 + k + 1)
                    made(dve, dve.tensor_tensor(lo[:, k], tmp[k % 2][:, 0:n], hi[:, k].bitcast(f32), sub),
                         split_lo, n0 + k + 1)
                for k in range(ntiles):
                    made(dve, dve.scalar_tensor_tensor(tmp[k % 2][:, 0:n], x(k), col(g, k), tmp[3][:, 0:n], mult, mult),
                         split_in, n0 + k + 1)
                    if k:
                        lower(k - 1)
                lower(ntiles - 1)

            def log1p_exp(u, e, out, w, n):
                z, z2, s = w
                step(dve.tensor_scalar(z, e, 2.0, None, add))
                step(dve.reciprocal(z, z))
                step(dve.tensor_tensor(z, z, e, mult))
                step(dve.tensor_tensor(z2, z, z, mult))
                step(dve.tensor_scalar(s, z2, 1.0 / 17, None, mult))
                for m in (15, 13, 11, 9, 7, 5, 3):
                    step(dve.scalar_tensor_tensor(s, s, 1.0 / m, z2, add, mult))
                step(dve.scalar_tensor_tensor(s, s, 1.0, z, add, mult))
                step(dve.tensor_scalar(z2, u, 0.0, None, vmax))
                step(dve.scalar_tensor_tensor(out, s, 2.0, z2, mult, add))

            dve.sem_inc(acc_free, 2)
            dve.wait_ge(par_loaded, 16)
            dve.wait_ge(x_loaded, 16)
            norm_split(0, 0, lambda k: x_t[:, k], "norm_g", KT, h_hi, h_lo, SEQ)

            dve.wait_ge(block_done, B_DT + 1)
            made(dve, dve.tensor_scalar(tmp[0][0:32], acc[0][0:32, :], col("dt_bias", 0, 32), None, add), u_ready, 1)
            free_acc(1)
            dve.wait_ge(eu_ready, 1)
            log1p_exp(tmp[0][0:32], tmp[1][0:32], dt_c[:], (tmp[2][0:32], tmp[3][0:32], tmp[4][0:32]), SEQ)
            dve.wait_ge(a_exp, 1)
            step(dve.tensor_scalar(tmp[0][0:32], dt_c[:], scol(0, 1, 32), -1.0, mult, mult))
            dve.wait_ge(consts_ready, 1)
            for c in range(NCH):
                cs = slice(c * CH, (c + 1) * CH)
                step(dve.tensor_tensor_scan(acs[:, cs], ones[0:32, :], tmp[0][0:32, cs], 0.0, mult, add))
            for c in range(NCH):
                ins = dve.tensor_scalar(small[0:32, 128 + 32 * c:160 + 32 * c], ident[0:32, 0:32],
                                        acs[:, (c + 1) * CH - 1:(c + 1) * CH], None, mult)
                made(dve, ins, acs_ready, c + 1)

            def conv(j, src, y, w, b):
                step(dve.tensor_scalar(y[:], src[:], col(w, j * 4 + 3), col(b, j), mult, add))
                for d in (1, 2, 3):
                    ins = dve.scalar_tensor_tensor(y[:, d:SEQ], src[:, 0:SEQ - d], col(w, j * 4 + (3 - d)), y[:, d:SEQ],
                                                   mult, add)
                    if d < 3:
                        step(ins)
                return ins

            def xbc(i):
                for r in range(4):
                    j = i * 4 + r
                    dve.wait_ge(block_done, j + (B_XBC + 1))
                    dve.wait_ge(hi_ready, i * 4 + (B_XBC + SLOTS + r))
                    made(dve, conv(j, acc[(B_XBC + r) % 2], tmp[2 + r % 2], "conv_w", "conv_b"), conv_ready, j + 1)
                    free_acc(0)
            step.loop(XBC_T // 4, 12, xbc)

            dve.wait_ge(tok_t, 1)
            step(dve.tensor_copy(tok[:, 0:2].rearrange("p a c h -> p (a c h)"), p_x[:, 0:256]))
            made(dve, dve.tensor_tensor(tok[:, 2].rearrange("p c h -> p (c h)"), p_x[:, 256:384],
                                        tok[:, 1].rearrange("p c h -> p (c h)"), sub), tok_sub, 1)
            dve.wait_ge(tok_exp, 1)

            def heads(t, pair):
                return tok[:, t, :, bass.ds(pair * 2, 2)].unsqueeze(3).to_broadcast([P, NCH, 2, 64])

            def group(g):
                for r in range(4):
                    pair = g * 4 + r
                    for e in range(2):
                        made(dve, dve.tensor_scalar(accm[:, e], acs[:], ident[0:32, bass.ds(pair * 2 + e, 1)], None, mult),
                             accm_ready, pair * 2 + (e + 1))
                    if r == 0:
                        dve.wait_ge(cb_mm, g + 1)
                        made(dve, dve.tensor_tensor(cb[:], p_off[:].rearrange("p (c l) -> p c l", c=NCH),
                                                    tril[:].unsqueeze(1).to_broadcast([P, NCH, CH]), mult), cb_ready, g + 1)
                    dve.wait_ge(x_tr, pair + 1)
                    v4 = lambda a: a.rearrange("p (c e d) -> p c e d", c=NCH, e=2)
                    w4 = lambda a: a.rearrange("p c (e d) -> p c e d", e=2)
                    step(dve.tensor_tensor(w4(xdt[:]), v4(p_x[:]), heads(0, pair), mult))
                    made(dve, dve.tensor_tensor(w4(xde[:]), w4(xdt[:]), heads(2, pair), mult), xd_ready, pair + 1)
                    for e in range(2):
                        dve.wait_ge(bc_mm, pair * 2 + (e + 1))
                        for c in range(NCH):
                            cs = slice(c * CH, (c + 1) * CH)
                            ins = dve.tensor_scalar(seg[e][:, cs], p_bc[e][:, cs], tok[:, 1, c, bass.ds(pair * 2 + e, 1)],
                                                    0.0, sub, vmin)
                            if c < NCH - 1:
                                step(ins)
                        made(dve, ins, seg_ready, pair * 2 + (e + 1))
                    for e in range(2):
                        dve.wait_ge(exp_ready, pair * 2 + (e + 1))
                        made(dve, dve.tensor_tensor(seg[e][:], seg[e][:], cb[:].rearrange("p c l -> p (c l)"), mult),
                             g_ready, pair * 2 + (e + 1))
                    dve.wait_ge(st_mm, pair + 1)
                    step(dve.tensor_copy(prev[:, 0], p_st[:, 0:CH]))
                    for c in (1, 2):
                        for e in range(2):
                            hs = slice(64 * e, 64 * e + 64)
                            ins = dve.scalar_tensor_tensor(prev[:, c, hs], prev[:, c - 1, hs],
                                                           tok[:, 3, c, bass.ds(pair * 2 + e, 1)],
                                                           p_st[:, c * CH + 64 * e:c * CH + 64 * e + 64], mult, add)
                            if c == 2 and e == 1:
                                made(dve, ins, prev_ready, pair + 1)
                            else:
                                step(ins)
                    dve.wait_ge(y_mm, pair + 1)
                    dve.wait_ge(ebc_ready, pair * 2 + 2)
                    step(dve.scalar_tensor_tensor(y_tmp[:], tile(xs, pair), col("ssd_d", pair), p_y[:], mult, add))
                    step(dve.tensor_tensor(ebc[:, CH:], p_off[:, CH:], ebc[:, CH:], mult))
                    step(dve.tensor_tensor(y_tmp[:, CH:], y_tmp[:, CH:], ebc[:, CH:], add))
                    dve.wait_ge(z_ready, pair + 1)
                    made(dve, dve.tensor_tensor(tile(xs, pair), y_tmp[:], z_silu[:], mult), y_ready, pair + 1)
                dve.wait_ge(groot_ready, g + 1)
                step(dve.reciprocal(tmp[3][:], tmp[2][:]))
                for r in range(4):
                    t = g * 4 + (r + 1)
                    if r >= 1:
                        dve.wait_ge(gn_done, t - 1)
                    made(dve, dve.scalar_tensor_tensor(tmp[r % 2][:], tile(xs, g * 4 + r), col("ssd_g", g * 4 + r), tmp[3][:],
                                                       mult, mult), gn_in, t)
                    dve.wait_ge(gn_hi, t)
                    made(dve, dve.tensor_tensor(tile(y_lo, g * 4 + r), tmp[r % 2][:], tmp_r[:].bitcast(f32), sub), gn_lo, t)
            step.loop(4, 57, group)
            dve.wait_ge(gn_done, 16)

            def merge(base, per, gate0, first):
                tiles = 4 if per == 3 else 2

                def body(i):
                    for r in range(tiles):
                        j = i * tiles + r
                        v = i * tiles + (gate0 + r + 1)
                        dve.wait_ge(gate_ready, v)
                        dve.wait_ge(block_done, i * (tiles * per) + (base + per * (r + 1)))
                        if first:
                            made(dve, dve.tensor_tensor(tile(merged, j), acc[(M_OF[base] + r) % 2][:], tmp[2 + r % 2][:], mult),
                                 merge_done, v)
                            free_acc(0)
                        else:
                            step(dve.tensor_tensor(tmp[4][:], acc[(M_OF[base] + r) % 2][:], tmp[2 + r % 2][:], mult))
                            free_acc(0)
                            made(dve, dve.tensor_tensor(tile(merged, j), tile(merged, j), tmp[4][:], add), merge_done, v)
                return body, KT // tiles
            body, count = merge(B_MSSD, 3, 0, True)
            step.loop(count, 0, body)

            def lru_x(i):
                for r in range(4):
                    j = i * 4 + r
                    dve.wait_ge(block_done, j + (B_LX + 1))
                    y = tmp[2 + r % 2]
                    step(conv(j, acc[(M_OF[B_LX] + r) % 2], y, "lconv_w", "lconv_b"))
                    free_acc(0)
                    made(dve, dve.tensor_copy(tile(xl, j), y[:]), lx_done, j + 1)
            step.loop(LRU_T // 4, 16, lru_x)
            dve.wait_ge(lam_ready, 1)
            step(dve.tensor_scalar(scol(40, 12), col12("lru_lam"), -1.0, None, mult))
            log1p_exp(scol(40, 12), scol(52, 12), scol(88, 12), (scol(256, 12), scol(268, 12), scol(280, 12)), 12)
            step(dve.tensor_scalar(scol(64, 12), scol(88, 12), -8.0, None, mult))
            made(dve, dve.tensor_scalar(scol(76, 12), scol(88, 12), 8.0, None, mult), lam_ready, 2)

            def lru_gates(i):
                for half in range(2):
                    g = i * 2 + half
                    for t in range(3):
                        v = g * 3 + (t + 1)
                        dve.wait_ge(xlh_ready, v)
                        made(dve, dve.tensor_tensor(xl_lo[:, t], tile(xl, g * 3 + t), xl_hi[:, t].bitcast(f32), sub), xls_ready, v)
                    for t in range(3):
                        v = g * 3 + (t + 1)
                        dve.wait_ge(sig_ready, v)
                        step(dve.tensor_tensor(l_i[:, t], l_i[:, t], tile(xl, g * 3 + t), mult))
                    for t in range(3):
                        v = g * 3 + (t + 1)
                        dve.wait_ge(dec_ready, v)
                        made(dve, dve.scalar_tensor_tensor(l_r[:, t], tmp[2][:], 1.0, l_r[:, t], add, mult), m2_ready, v)
                    dve.wait_ge(m_ready, g + 1)
                    for t in range(3):
                        step(dve.tensor_tensor(l_i[:, t], l_i[:, t], l_r[:, t], mult))
                        step(dve.tensor_tensor_scan(l_r[:, t], l_a[:, t], l_i[:, t], 0.0, mult, add))
                    for t in range(3):
                        v = g * 3 + (t + 1)
                        y = tmp[4 + t % 2]
                        dve.wait_ge(lsilu_ready, v)
                        made(dve, dve.tensor_tensor(y[:], l_r[:, t], tmp[2 + t % 2][:], mult), ly_in, v)
                        dve.wait_ge(ly_hi, v)
                        made(dve, dve.tensor_tensor(tile(l_lo, g * 3 + t), y[:], tile(l_hi, g * 3 + t).bitcast(f32), sub),
                             ly_done, v)
            step.loop(2, 18, lru_gates)

            dve.wait_ge(mem_loaded, 16)
            norm_split(1, KT, lambda k: mem_t[:, k], "mem_g", KT, m_hi, m_lo, MEM)

            def kv(i):
                for r in range(4):
                    j = i * 4 + r
                    dve.wait_ge(block_done, j + (B_KV + 1))
                    made(dve, dve.tensor_copy(tile(mk, j), acc[(M_OF[B_KV] + r) % 2][:, 0:MEM]), kv_ready, j + 1)
                    free_acc(0)
            step.loop(2, 0, kv)

            def values(i):
                for r in range(4):
                    j = i * 4 + r
                    dve.wait_ge(block_done, j + (B_KV + KT + 1))
                    made(dve, dve.tensor_copy(tmp[r % 2][:, 0:MEM], acc[(M_OF[B_KV] + r) % 2][:, 0:MEM]), kv_ready, j + (KT + 1))
                    free_acc(0)
                    dve.wait_ge(v_tr, j + 1)
                    step(dve.tensor_copy(mv[:, :, bass.ds(j * P, P)],
                                         bank[3 + r % 2][:, 0:MEM].rearrange("p (m d) -> p m d", m=2)))
            step.loop(2, 4, values)
            def exponential(x, out, w):
                n, p, two_n = w
                step(dve.tensor_scalar(p, x, -88.0, 88.0, vmax, vmin))
                step(dve.tensor_scalar(n, p, 1.4426950408889634, MAGIC, mult, add))
                step(dve.tensor_scalar(n, n, -MAGIC, None, add))
                step(dve.scalar_tensor_tensor(p, n, -0.693359375, p, mult, add))
                step(dve.scalar_tensor_tensor(p, n, 2.12194440e-4, p, mult, add))
                step(dve.tensor_scalar(n, n, 127.0, 8388608.0, add, mult))
                step(dve.tensor_copy(two_n.bitcast(mybir.dt.int32), n))
                step(dve.tensor_scalar(out, p, 1.0 / 5040, None, mult))
                for c in (1.0 / 720, 1.0 / 120, 1.0 / 24, 1.0 / 6, 0.5, 1.0):
                    step(dve.scalar_tensor_tensor(out, out, c, p, add, mult))
                step(dve.tensor_scalar(out, out, 1.0, None, add))
                step(dve.tensor_tensor(out, out, two_n, mult))

            def cmul(or_, oi, ar, ai, br, bi, w):
                step(dve.tensor_tensor(w, ai, bi, mult))
                step(dve.tensor_tensor(or_, ar, br, mult))
                step(dve.tensor_tensor(or_, or_, w, sub))
                step(dve.tensor_tensor(w, ai, br, mult))
                step(dve.tensor_tensor(oi, ar, bi, mult))
                step(dve.tensor_tensor(oi, oi, w, add))

            s5 = lambda c: sc5[:, c]
            lam_re, lam_im, log_step = (pcol[:, PC[n]:PC[n] + 24] for n in ("lam_re", "lam_im", "log_step"))
            exponential(log_step, s5(0), (s5(10), s5(11), s5(12)))
            step(dve.tensor_tensor(s5(1), lam_im, s5(0), mult))
            step(dve.tensor_scalar(s5(10), s5(1), 0.15915494309189535, MAGIC, mult, add))
            step(dve.tensor_scalar(s5(10), s5(10), -MAGIC, None, add))
            for c in (6.28125, 1.9340515136718750e-3, 1.2556659146e-6):
                step(dve.scalar_tensor_tensor(s5(1), s5(10), -c, s5(1), mult, add))
            step(dve.tensor_scalar(s5(1), s5(1), 3.1415925, -3.1415925, vmin, vmax))
            step(dve.tensor_tensor(s5(13), lam_re, s5(0), mult))
            step(dve.tensor_scalar(s5(2), s5(13), 1.0, None, vmin))
            step(dve.tensor_scalar(s5(6), s5(13), 1.0, 88.0, vmax, vmin))
            made(dve, dve.memset(s5(9), 1.0), step_ready, 1)
            dve.wait_ge(t_exp, 1)
            step(dve.tensor_scalar(s5(10), s5(5), -1.0, 1.0, mult, add))
            step(dve.reciprocal(s5(10), s5(10)))
            step(dve.scalar_tensor_tensor(s5(10), s5(5), 2.0, s5(10), mult, mult))
            step(dve.tensor_tensor(s5(11), s5(7), s5(8), sub))
            step(dve.tensor_tensor(s5(10), s5(10), s5(11), add))
            step(dve.tensor_scalar(s5(14), s5(10), 1.0, None, add))
            step(dve.tensor_tensor(s5(11), s5(4), s5(4), mult))
            step(dve.tensor_scalar(s5(11), s5(11), -2.0, None, mult))
            step(dve.tensor_scalar(s5(12), s5(11), 1.0, None, add))
            step(dve.tensor_tensor(s5(13), s5(10), s5(12), mult))
            step(dve.tensor_tensor(s5(13), s5(13), s5(11), add))
            step(dve.tensor_tensor(s5(15), s5(14), s5(3), mult))
            step(dve.tensor_tensor(s5(16), lam_re, lam_re, mult))
            step(dve.tensor_tensor(s5(17), lam_im, lam_im, mult))
            step(dve.tensor_tensor(s5(16), s5(16), s5(17), add))
            step(dve.reciprocal(s5(16), s5(16)))
            for out_, a, b, op in ((18, (13, lam_re), (15, lam_im), add), (19, (15, lam_re), (13, lam_im), sub)):
                step(dve.tensor_tensor(s5(17), s5(a[0]), a[1], mult))
                step(dve.tensor_tensor(s5(10), s5(b[0]), b[1], mult))
                step(dve.tensor_tensor(s5(17), s5(17), s5(10), op))
                step(dve.tensor_tensor(s5(out_), s5(17), s5(16), mult))
            pr, pi, t = s5(12), s5(3), (s5(10), s5(11))
            for table, n in ((turn_v, 32), (turn_u, 16)):
                step(dve.memset(table[:, :, 0, 0], 1.0))
                step(dve.memset(table[:, :, 0, 1], 0.0))
                m = 1
                while m < n:
                    wide = lambda x: x.unsqueeze(2).to_broadcast([P, 24, m])
                    w = tmp[0][:, 0:24 * m].rearrange("p (s b) -> p s b", s=24)
                    cmul(table[:, :, m:2 * m, 0], table[:, :, m:2 * m, 1], table[:, :, 0:m, 0], table[:, :, 0:m, 1],
                         wide(pr), wide(pi), w)
                    cmul(t[0], t[1], pr, pi, pr, pi, s5(17))
                    step(dve.tensor_copy(pr, t[0]))
                    step(dve.tensor_copy(pi, t[1]))
                    m *= 2
            made(dve, dve.memset(s5(9), 1.0), tables_ready, 1)
            body, count = merge(B_MLRU, 3, KT, False)
            step.loop(count, 4, body)

            def queries(i):
                for r in range(4):
                    j = i * 4 + r
                    dve.wait_ge(block_done, j + (B_Q + 1))
                    made(dve, dve.tensor_copy(tile(q, j), acc[(M_OF[B_Q] + r) % 2][:]), q_ready, j + 1)
                    free_acc(0)
            step.loop(2, 0, queries)

            for h in range(4):
                dve.wait_ge(sc_mm, h + 1)
                for t in range(4):
                    step(dve.tensor_reduce(scol(96 + t), score(t), AX.X, vmax))
                made(dve, dve.tensor_scalar(scol(100, 4), scol(96, 4), -1.0 / 16, None, mult), mx_ready, h + 1)
                dve.wait_ge(pe_ready, 4 * h + 4)
                step(dve.reciprocal(scol(108, 4), scol(104, 4)))
                made(dve, dve.tensor_tensor(probs[:], probs[:], scol(108, 4).unsqueeze(2).to_broadcast([P, 4, MEM]), mult),
                     pn_ready, h + 1)
                for m in range(2):
                    dve.wait_ge(p_tr, 2 * h + m + 1)
                    made(dve, dve.tensor_copy(probs_t[:, m], bank[5 + m][:]), pt_ready, 2 * h + m + 1)
                for d in range(2):
                    v = 2 * h + d + 1
                    dve.wait_ge(o_mm, v)
                    made(dve, dve.tensor_copy(tmp[d][:], bank[7 - 5 * d][:]), yo_in, v)
                    dve.wait_ge(yo_hi, v)
                    made(dve, dve.tensor_tensor(ym_lo[:, 2 * h + d], tmp[d][:], ym_hi[:, 2 * h + d].bitcast(f32), sub),
                         yo_done, v)

            def merge_mem(i):
                for r in range(2):
                    j, v = i * 2 + r, i * 2 + (r + 1)
                    dve.wait_ge(gate_ready, v + 2 * KT)
                    dve.wait_ge(block_done, i * 4 + (B_MMEM + 2 * r + 2))
                    step(dve.tensor_tensor(tmp[4][:], acc[(M_OF[B_MMEM] + r) % 2][:], tmp[2 + r % 2][:], mult))
                    free_acc(0)
                    made(dve, dve.tensor_tensor(tile(merged, j), tile(merged, j), tmp[4][:], add), merge_done, v + 2 * KT)
                    dve.wait_ge(mg_hi, v)
                    made(dve, dve.tensor_tensor(tile(g_lo, j), tile(merged, j), tile(g_hi, j).bitcast(f32), sub), mg_done, v)
            step.loop(4, 2, merge_mem)

            dve.wait_ge(xre_loaded, 16)

            def outs(i):
                for r in range(4):
                    j = i * 4 + r
                    dve.wait_ge(block_done, j + (B_OUT + 1))
                    made(dve, dve.tensor_tensor(tile(x1, j), acc[(M_OF[B_OUT] + r) % 2][:], tile(x1, j), add), x1_ready, j + 1)
                    free_acc(0)
            step.loop(2, 0, outs)
            dve.wait_ge(root_ready, 3)
            step(dve.reciprocal(tmp[3][:], tmp[2][:]))
            for k in range(KT):
                made(dve, dve.scalar_tensor_tensor(x1[:, k], x1[:, k], col("final_g", k), tmp[3][:], mult, mult),
                     x2_ready, k + 1)
            norm_split(3, 2 * KT, lambda k: x1[:, k], "g_norm_2", KT, h_hi, h_lo, SEQ)
            dve.wait_ge(block_done, B_FL + 1)
            step(dve.tensor_scalar(tmp[0][0:12], acc[M_OF[B_FL] % 2][0:12, :], col("b_forget", 0, 12), -1.0, add, mult))
            free_acc(0)
            dve.sem_inc(nu_ready, 1)
            dve.wait_ge(enu_ready, 1)
            log1p_exp(tmp[0][0:12], tmp[1][0:12], tmp[5][0:12], (tmp[2][0:12], tmp[3][0:12], tmp[4][0:12]), SEQ)
            step(dve.memset(tmp[0][0:12], 1.0))
            step(dve.memset(sum_f[:], 0.0))
            made(dve, dve.tensor_tensor_scan(sum_f[0:12, :], tmp[0][0:12], tmp[5][0:12], 0.0, mult, add), f_ready, 1)

            dve.sem_inc(e_used, 2)

            def fox_s5(j):
                dve.wait_ge(s5_loaded, j * 16 + 16)
                cm = s5m[:, 256:512].rearrange("p (s c h) -> p s c h", s=4, c=2)
                f = [sc5[:, c, bass.ds(j * 4, 4)].unsqueeze(2).to_broadcast([P, 4, 32]) for c in (18, 19)]
                w = tmp[0][:, 0:128].rearrange("p (s h) -> p s h", s=4)
                step(dve.tensor_tensor(w, cm[:, :, 1], f[1], mult))
                step(dve.tensor_tensor(cf[:, :, 0], cm[:, :, 0], f[0], mult))
                step(dve.tensor_tensor(cf[:, :, 0], cf[:, :, 0], w, sub))
                step(dve.tensor_tensor(w, cm[:, :, 1], f[0], mult))
                step(dve.tensor_tensor(cf[:, :, 1], cm[:, :, 0], f[1], mult))
                made(dve, dve.scalar_tensor_tensor(cf[:, :, 1], cf[:, :, 1], -1.0, w, mult, sub), cf_ready, j + 1)
                for r in range(4):
                    s = j * 4 + r
                    er, ei = et[:, r % 2, 0], et[:, r % 2, 1]
                    p, q_ = bank[2 + 3 * (r % 2)][:], bank[3 + 3 * (r % 2)][:]
                    t = [x[:] for x in tmp]
                    dve.wait_ge(e_made, s + 1)
                    dve.wait_ge(pq_mm, s + 1)
                    step(dve.tensor_tensor(t[0], p, er, mult))
                    step(dve.tensor_tensor(t[1], q_, ei, mult))
                    step(dve.tensor_tensor(t[0], t[0], t[1], add))
                    step(dve.tensor_tensor(t[1], q_, er, mult))
                    step(dve.tensor_tensor(t[2], p, ei, mult))
                    step(dve.tensor_tensor(t[1], t[1], t[2], sub))
                    mag = sc5[:, 14, bass.ds(s, 1)].to_broadcast([P, SEQ])
                    step(dve.tensor_tensor_scan(t[2], mag, t[0], 0.0, mult, add))
                    step(dve.tensor_tensor_scan(t[3], mag, t[1], 0.0, mult, add))
                    step(dve.tensor_tensor(t[0], t[2], er, mult))
                    step(dve.tensor_tensor(t[1], t[3], ei, mult))
                    dve.wait_ge(h_free, s + 1)
                    step(dve.tensor_tensor(t[4], t[0], t[1], sub))
                    step(dve.tensor_tensor(t[0], t[3], er, mult))
                    step(dve.tensor_tensor(t[1], t[2], ei, mult))
                    made(dve, dve.tensor_tensor(t[5], t[0], t[1], add), h_ready, s + 1)
                    dve.sem_inc(e_used, 1)
                dve.wait_ge(h_free, j * 4 + 5)
                made(dve, dve.scalar_tensor_tensor(tile(u5, j), tile(u5, j), col("s5_d", j), bank[4][:], mult, add),
                     y5_ready, j * 2 + 1)
                dve.wait_ge(y5_sq, j + 1)
                step(dve.tensor_scalar(tmp[0][:], tmp[0][:], 0.044715, 1.0, mult, add))
                made(dve, dve.tensor_tensor(tmp[0][:], tmp[0][:], tile(u5, j), mult), y5_arg, j + 1)
                dve.wait_ge(y5_sig, j + 1)
                made(dve, dve.tensor_tensor(tile(u5, j), tile(u5, j), tmp[1][:], mult), y5_ready, j * 2 + 2)
            step.loop(6, 58, fox_s5)

            for j in range(6):
                dve.wait_ge(y5h, j + 1)
                made(dve, dve.tensor_tensor(y5_lo[:, j], u5[:, j], y5_hi[:, j].bitcast(f32), sub), y5l, j + 1)
            for j in range(6):
                dve.wait_ge(acc_read, 2 + 36 + j + 1)
                t = tmp[j % 2][:]
                step(dve.tensor_tensor(t, u5[:, j], tmp[2 + j % 2][:], mult))
                made(dve, dve.tensor_tensor(t, t, gs[:, j], mult), s5_in, j + 1)
                dve.wait_ge(s5_hi, j + 1)
                made(dve, dve.tensor_tensor(s_lo[:, j], t, s_hi[:, j].bitcast(f32), sub), s5_done, j + 1)

            dve.wait_ge(block_done, B_GLU + 6)
            step(dve.memset(fq_cur[0][:], 0.0))
            made(dve, dve.memset(fq_cur[1][:], 0.0), fz_ready, 1)

            def fox(j):
                for e in range(2):
                    h = j * 2 + e
                    made(dve, dve.tensor_scalar(fm[:], sum_f[:], ident[:, bass.ds(h, 1)], None, mult), fm_ready, h + 1)
                    for t in range(4):
                        w = (t + 1) * P
                        dve.wait_ge(fs_mm, h * 4 + (t + 1))
                        step(dve.tensor_tensor(bank[2 + t][:, t * P:w], bank[2 + t][:, t * P:w], negm[:], add))
                        step(dve.tensor_reduce(scol(300 + t), bank[2 + t][:, 0:w], AX.X, vmax))
                        made(dve, dve.tensor_scalar(scol(304 + t), scol(300 + t), -1.0, None, mult), fmx_ready,
                             h * 4 + (t + 1))
                    for t in range(4):
                        w = (t + 1) * P
                        dve.wait_ge(fe_ready, h * 4 + (t + 1))
                        step(dve.reciprocal(scol(312 + t), scol(308 + t)))
                        made(dve, dve.tensor_scalar(f_p[t][:, 0:w], f_p[t][:, 0:w], scol(312 + t), None, mult), fn_ready,
                             h * 4 + (t + 1))
                    for k in (1, 3):
                        dve.wait_ge(fp_tr, h * 4 + (k + 1))
                        step(dve.tensor_copy(f_pt[k][:, k * P:], bank[2 + k][:, k * P:]))
                    dve.sem_inc(fpt_dve, 1)
                dve.wait_ge(fo_mm, j * 2 + 2)
                made(dve, dve.tensor_tensor(tile(fg, j), bank[6][:], tile(fg, j), mult), fo_ready, j + 1)
            step.loop(6, 28, fox)
            for j in range(6):
                dve.wait_ge(fh, j + 1)
                made(dve, dve.tensor_tensor(f_lo[:, j], fg[:, j], f_hi[:, j].bitcast(f32), sub), fl_done, j + 1)

            dve.wait_ge(mem2_loaded, 16)
            norm_split(4, 3 * KT, lambda k: mem2[:, k], "g_mem_norm_2", KT, m2_hi, m2_lo, MEM)
            for h in range(4):
                dve.wait_ge(sc2_mm, h + 1)
                for t in range(4):
                    step(dve.tensor_reduce(scol(96 + t), score(t), AX.X, vmax))
                made(dve, dve.tensor_scalar(scol(100, 4), scol(96, 4), -(P ** -0.5), None, mult), mx2_ready, h + 1)
                dve.wait_ge(e2_ready, 4 * h + 4)
                step(dve.reciprocal(scol(108, 4), scol(104, 4)))
                made(dve, dve.tensor_tensor(probs2[:], probs2[:], scol(108, 4).unsqueeze(2).to_broadcast([P, 4, MEM]), mult),
                     n2_ready, h + 1)
                for m in range(2):
                    dve.wait_ge(p2_tr, 2 * h + m + 1)
                    made(dve, dve.tensor_copy(probs2_t[:, m], bank[5 + m][:]), p2t_ready, 2 * h + m + 1)
                dve.wait_ge(o2_mm, h + 1)
                made(dve, dve.tensor_tensor(tmp[h % 2][:], bank[7][:], gm[:, h], mult), yn_in, h + 1)
                dve.wait_ge(yn_hi_ready, h + 1)
                made(dve, dve.tensor_tensor(yn_lo[:, h], tmp[h % 2][:], yn_hi[:, h].bitcast(f32), sub), yn_done, h + 1)

            def merge2(i):
                for r in range(2):
                    for n in range(3):
                        v, a = i * 6 + (3 * r + n + 1), acc[(M_OF[B_M2] + 3 * r + n) % 2][:]
                        g = tmp[2 + (r + n) % 2][:]
                        dve.wait_ge(gate2_ready, v)
                        dve.wait_ge(block_done, i * 12 + (B_M2 + 6 * r + 2 * n + 2))
                        if n == 0:
                            made(dve, dve.tensor_tensor(tmp[4][:], a, g, mult), merge2_done, v)
                            free_acc(0)
                        else:
                            step(dve.tensor_tensor(tmp[5][:], a, g, mult))
                            free_acc(0)
                            made(dve, dve.tensor_tensor(tmp[4][:], tmp[4][:], tmp[5][:], add), merge2_done, v)
                    v = i * 2 + (r + 1)
                    dve.wait_ge(mg2_hi, v)
                    made(dve, dve.tensor_tensor(tile(g2_lo, i * 2 + r), tmp[4][:], tile(g2_hi, i * 2 + r).bitcast(f32), sub),
                         mg2_done, v)
            step.loop(4, 4, merge2)
            dve.wait_ge(x3_loaded, 16)
            for j in range(8):
                dve.wait_ge(block_done, B_OUT2 + j + 1)
                made(dve, dve.tensor_tensor(x3[:, j], acc[(M_OF[B_OUT2] + j) % 2][:], x3[:, j], add), x3_ready, j + 1)
                free_acc(0)
            dve.wait_ge(root_ready, 6)
            step(dve.reciprocal(tmp[3][:], tmp[2][:]))
            for k in range(KT):
                made(dve, dve.scalar_tensor_tensor(x3[:, k], x3[:, k], col("g_final_2", k), tmp[3][:], mult, mult),
                     fin_ready, k + 1)

        @block.tensor
        def _(pe):
            step = Steps(pe, s_pe)

            def tile(x, j):
                return x[:, bass.ds(j, 1)].rearrange("p o t -> p (o t)")

            def weights(b, off, out, hi, lo, ks, slots=None, start=True, stop=True):
                pe.wait_ge(lo_ready, off + (b + 1))
                slots = slots or range(len(ks))
                for n, (s, k) in enumerate(zip(slots, ks)):
                    whi, wlo = w_hi[:, b % SLOTS, s], w_lo[:, b % SLOTS, s]
                    pe.matmul(out, whi, hi(k), start=start and n == 0, stop=False)
                    pe.matmul(out, whi, lo(k), start=False, stop=False)
                    last = pe.matmul(out, wlo, hi(k), start=False, stop=stop and n == len(ks) - 1)
                return last

            H = (lambda k: h_hi[:, k], lambda k: h_lo[:, k])

            def sum_square(k, value, ntiles=KT, n=SEQ):
                pe.wait_ge(sq_ready, value)
                pe.matmul(p_norm[:, 0:n], ones[:], tmp[k % 2][:, 0:n], start=k == 0, stop=k == ntiles - 1
                          ).then_inc(sq_summed, 1)

            def sum_squares(sq0, ntiles, n):
                for k in range(ntiles):
                    sum_square(k, sq0 + k + 1, ntiles, n)

            def free(m, off=0):
                pe.wait_ge(acc_free, off + (m + 1))

            pe.wait_ge(consts_ready, 1)
            sum_squares(0, KT, SEQ)
            pe.wait_ge(split_lo, KT)
            free(0)
            weights(B_DT, 0, acc[0][:], *H, range(KT)).then_inc(block_done, 1)

            def simple(base, count):
                m = M_OF[base]

                def body(i):
                    for r in range(4):
                        free(m + r, i * 4)
                        weights(base + r, i * 4, acc[(m + r) % 2][:], *H, range(KT)).then_inc(block_done, 1)
                with pe.Fori(0, count) as i:
                    body(i)
            simple(B_XBC, XBC_T // 4)

            pe.wait_ge(acs_ready, 4)
            for c in range(NCH):
                pe.transpose(p_x[:, 32 * c:32 * c + 32], dt_c[:, c * CH:(c + 1) * CH], ident[0:32, 0:32])
            for c in range(NCH):
                pe.transpose(p_x[:, 128 + 32 * c:160 + 32 * c], acs[:, c * CH:(c + 1) * CH], ident[0:32, 0:32])
            for c in range(NCH):
                ins = pe.matmul(p_x[:, 256 + 32 * c:288 + 32 * c], ones[0:32, :], small[0:32, 128 + 32 * c:160 + 32 * c],
                                start=True, stop=True)
            ins.then_inc(tok_t, 1)
            pe.wait_ge(tok_exp, 1)
            pe.wait_ge(silu_done, XBC_T)
            pe.wait_ge(acc_free, M_OF[B_Z] + 2)

            def group(g):
                pe.wait_ge(bcur_ready, g + 1)
                for c in range(NCH):
                    ins = pe.transpose(p_x[:, c * CH:(c + 1) * CH], b_cur[:, c * CH:(c + 1) * CH], ident[:])
                ins.then_inc(b_t, 1)
                for c in range(NCH):
                    ins = pe.matmul(p_off[:, c * CH:(c + 1) * CH], b_cur[:, c * CH:(c + 1) * CH],
                                    xs[:, bass.ds(g + 20, 1), c * CH:(c + 1) * CH].rearrange("p o t -> p (o t)"),
                                    start=True, stop=True)
                ins.then_inc(cb_mm, 1)
                pe.wait_ge(btok_ready, g + 1)
                for r in range(4):
                    pair = g * 4 + r
                    pe.wait_ge(x_cur_ready, pair + 1)
                    for c in range(NCH):
                        ins = pe.transpose(p_x[:, c * CH:(c + 1) * CH], x_cur[:, c * CH:(c + 1) * CH], ident[:])
                    ins.then_inc(x_tr, 1)
                    for e in range(2):
                        pe.wait_ge(accm_ready, pair * 2 + (e + 1))
                        pe.matmul(p_bc[e][:], ones[0:32, :], accm[:, e], start=True, stop=True).then_inc(bc_mm, 1)
                    weights(B_Z + r, g * 4, acc[r % 2][:], *H, range(KT)).then_inc(block_done, 1)
                    pe.wait_ge(xd_ready, pair + 1)
                    for c in range(NCH - 1):
                        ins = pe.matmul(p_st[:, c * CH:(c + 1) * CH], b_tok[:, c], xde[:, c], start=True, stop=True)
                    ins.then_inc(st_mm, 1)
                    for e in range(2):
                        pe.wait_ge(g_ready, pair * 2 + (e + 1))
                        for c in range(NCH):
                            pe.matmul(p_y[64 * e:64 * e + 64, c * CH:(c + 1) * CH], xdt[:, c, 64 * e:64 * e + 64],
                                      seg[e][:, c * CH:(c + 1) * CH], start=True, stop=True)
                    pe.wait_ge(prev_ready, pair + 1)
                    for c in range(1, NCH):
                        ins = pe.matmul(p_off[:, c * CH:(c + 1) * CH], prev[:, c - 1],
                                        xs[:, bass.ds(g + 20, 1), c * CH:(c + 1) * CH].rearrange("p o t -> p (o t)"),
                                        start=True, stop=True)
                    ins.then_inc(y_mm, 1)
                for r in range(4):
                    pe.wait_ge(gsq_ready, g * 4 + (r + 1))
                    pe.matmul(p_norm[:], ones[:], tmp[r % 2][:], start=r == 0, stop=r == 3).then_inc(gsum_mm, 1)
                pe.wait_ge(gn_lo, g * 4 + 4)
            with pe.Fori(0, 4) as g:
                group(g)
            pe.wait_ge(gn_done, 16)
            pe.wait_ge(gn_lo, 16)

            def merge(base, gate0, hi, lo, k1, k2):
                per, tiles, m = (3, 4, M_OF[base]) if k2 else (2, 2, M_OF[base])

                def body(i):
                    off = i * (tiles * per)
                    for r in range(tiles):
                        b = base + per * r
                        weights(b, off, p_gate[:], *H, range(KT)).then_inc(block_done, 1)
                        free(m + r, i * tiles)
                        weights(b + 1, off, acc[(m + r) % 2][:], hi, lo, range(k1), stop=not k2).then_inc(block_done, 1)
                        if k2:
                            weights(b + 2, off, acc[(m + r) % 2][:], hi, lo, range(KT, KT + k2), start=False
                                    ).then_inc(block_done, 1)
                        pe.wait_ge(gate_ready, i * tiles + (gate0 + r + 1))
                with pe.Fori(0, KT // tiles) as i:
                    body(i)
            merge(B_MSSD, 0, lambda k: y_hi[:, k], lambda k: y_lo[:, k], KT, KT)

            simple(B_LX, LRU_T // 4)

            def lru_gates(i):
                for half in range(2):
                    g = i * 2 + half
                    pe.wait_ge(xls_ready, g * 3 + 3)
                    for t in range(3):
                        b = B_LG + 6 * half + t
                        if t == 2:
                            pe.wait_ge(sig_ready, g * 3 + 1)
                        pa, px = bank[2 + (t % 2) * 2], bank[3 + (t % 2) * 2]
                        X = (lambda k: xl_hi[:, k], lambda k: xl_lo[:, k])
                        ks = LRU_KS[t]
                        weights(b, i * 12, pa[:], *X, ks, slots=ks)
                        weights(b, i * 12, px[:], *X, ks, slots=[3 + k for k in ks]).then_inc(block_done, 1)
                    for t in range(3):
                        if t == 2:
                            pe.wait_ge(lsilu_ready, g * 3 + 1)
                        elif t == 0 and not half:
                            pe.wait_ge(acc_free, M_OF[B_LX] + LRU_T + 2)
                        weights(B_LG + 6 * half + 3 + t, i * 12, acc[(half + t) % 2][:], *H, range(KT)).then_inc(block_done, 1)
            with pe.Fori(0, 2) as i:
                lru_gates(i)

            sum_squares(KT, KT, MEM)
            pe.wait_ge(split_lo, 2 * KT)
            pe.wait_ge(ly_done, LRU_T)
            MM = (lambda k: m_hi[:, k], lambda k: m_lo[:, k])

            def keys(i):
                for r in range(4):
                    free(M_OF[B_KV] + r, i * 4)
                    weights(B_KV + r, i * 4, acc[(M_OF[B_KV] + r) % 2][:, 0:MEM], *MM, range(KT)).then_inc(block_done, 1)
            with pe.Fori(0, 2) as i:
                keys(i)

            def values(i):
                for r in range(4):
                    j = i * 4 + r
                    free(M_OF[B_KV] + KT + r, i * 4)
                    weights(B_KV + KT + r, i * 4, acc[(M_OF[B_KV] + r) % 2][:, 0:MEM], *MM, range(KT)
                            ).then_inc(block_done, 1)
                    pe.wait_ge(kv_ready, j + (KT + 1))
                    for m in range(2):
                        ins = pe.transpose(bank[3 + r % 2][:, m * P:(m + 1) * P], tmp[r % 2][:, m * P:(m + 1) * P], ident[:])
                    ins.then_inc(v_tr, 1)
            with pe.Fori(0, 2) as i:
                values(i)

            merge(B_MLRU, KT, lambda k: l_hi[:, k], lambda k: l_lo[:, k], KT, 4)
            simple(B_Q, 2)

            pe.wait_ge(q_ready, KT)
            for h in range(4):
                for t in range(4):
                    for k in range(2):
                        ins = pe.matmul(score(t), q[:, 2 * h + k, t * P:(t + 1) * P], mk[:, 2 * h + k], start=k == 0, stop=k == 1)
                ins.then_inc(sc_mm, 1)
                pe.wait_ge(pn_ready, h + 1)
                for m in range(2):
                    for t in range(4):
                        ins = pe.transpose(bank[5 + m][:, t * P:(t + 1) * P], probs[:, t, m * P:(m + 1) * P], ident[:])
                    ins.then_inc(p_tr, 1)
                pe.wait_ge(pt_ready, 2 * h + 2)
                for d in range(2):
                    for m in range(2):
                        c0 = (2 * h + d) * P
                        ins = pe.matmul(bank[7 - 5 * d][:], mv[:, m, c0:c0 + P], probs_t[:, m], start=m == 0, stop=m == 1)
                    ins.then_inc(o_mm, 1)
            pe.wait_ge(yo_done, KT)

            merge(B_MMEM, 2 * KT, lambda k: ym_hi[:, k], lambda k: ym_lo[:, k], KT, 0)
            pe.wait_ge(mg_done, KT)

            def outs(i):
                for r in range(4):
                    m = M_OF[B_OUT] + r
                    free(m, i * 4)
                    weights(B_OUT + r, i * 4, acc[m % 2][:], lambda k: g_hi[:, k], lambda k: g_lo[:, k], range(KT)
                            ).then_inc(block_done, 1)
            with pe.Fori(0, 2) as i:
                outs(i)
            sum_squares(2 * KT, KT, SEQ)
            sum_squares(3 * KT, KT, SEQ)
            pe.wait_ge(split_lo, 3 * KT)
            free(M_OF[B_FL])
            weights(B_FL, 0, acc[M_OF[B_FL] % 2][:], *H, range(KT)).then_inc(block_done, 1)
            pe.wait_ge(acc_free, M_OF[B_FL] + 3)

            def read(n):
                pe.wait_ge(acc_read, n + 1)

            def u_gs(i):
                for r in range(4):
                    read(i * 4 + r)
                    weights(B_UG + r, i * 4, acc[r % 2][:], *H, range(KT)).then_inc(block_done, 1)
            with pe.Fori(0, 3) as i:
                u_gs(i)
            pe.wait_ge(acc_read, 2 + 12)

            def inputs(j, r):
                rows = slice(32 * r, 32 * r + 32)
                for c in range(2):
                    ins = pe.matmul(bank[2 + 3 * (r % 2) + c][:], s5m[rows, c * P:(c + 1) * P],
                                    u_cur[rows, :], start=True, stop=True)
                ins.then_inc(pq_mm, 1)

            def fox_s5(j):
                pe.wait_ge(s5_loaded, j * 16 + 16)
                pe.wait_ge(u_cur_ready, j + 1)
                inputs(j, 0)
                for r in range(4):
                    read(j * 4 + (12 + r))
                    weights(B_FOX + r, j * 4, acc[r % 2][:], *H, range(KT)).then_inc(block_done, 1)
                    if r < 3:
                        inputs(j, r + 1)
                    if r == 3:
                        pe.wait_ge(acc_read, j * 4 + 17)
                        for k in range(NCH):
                            ins = pe.transpose(bank[7][:, k * P:(k + 1) * P], v_tmp[:, k * P:(k + 1) * P], ident[:])
                        ins.then_inc(v5_tr, 1)
                    if r == 0:
                        pe.wait_ge(cf_ready, j + 1)
                    pe.wait_ge(h_ready, j * 4 + (r + 1))
                    for c in range(2):
                        ins = pe.matmul(bank[4][32 * r:32 * r + 32, :], cf[:, r, c], tmp[4 + c][:], start=c == 0, stop=c == 1)
                    ins.then_inc(h_free, 1)
                pe.wait_ge(v_evac, j + 1)
            pe.sem_inc(h_free, 1)
            with pe.Fori(0, 6) as j:
                fox_s5(j)
            pe.wait_ge(y5l, 6)
            for j in range(6):
                read(36 + j)
                weights(B_GLU + j, 0, acc[j % 2][:], lambda k: y5_hi[:, k], lambda k: y5_lo[:, k], range(6)
                        ).then_inc(block_done, 1)

            def fox(j):
                pe.wait_ge(fcur_ready, j + 1)
                for e in range(2):
                    h = j * 2 + e
                    pe.wait_ge(fm_ready, h + 1)
                    for t in range(4):
                        w = (t + 1) * P
                        pe.matmul(bank[2 + t][:, 0:w], fq_cur[e][:, t * P:w],
                                  fk[:, bass.ds(j, 1), 0:w].rearrange("p o t -> p (o t)"), start=True, stop=False)
                        pe.matmul(bank[2 + t][:, 0:w], ones[:], fm[:, 0:w], start=False, stop=True).then_inc(fs_mm, 1)
                    for k in range(4):
                        pe.wait_ge(fn_ready, h * 4 + 4)
                        for t in range(k, 4):
                            ins = pe.transpose(bank[2 + k][:, t * P:(t + 1) * P], f_p[t][:, k * P:(k + 1) * P], ident[:])
                        ins.then_inc(fp_tr, 1)
                    pe.wait_ge(fpt_ready, h * 2 + 2)
                    pe.wait_ge(fpt_dve, h + 1)
                    for k in range(4):
                        ins = pe.matmul(bank[6][64 * e:64 * e + 64, k * P:], fv_cur[:, k, 64 * e:64 * e + 64],
                                        f_pt[k][:, k * P:], start=k == 0, stop=k == 3)
                    ins.then_inc(fo_mm, 1)
            with pe.Fori(0, 6) as j:
                fox(j)

            sum_squares(4 * KT, KT, MEM)
            pe.wait_ge(split_lo, 4 * KT)
            for j in range(8):
                read(42 + j)
                weights(B_KV2 + j, 0, acc[j % 2][:, 0:MEM], lambda k: m2_hi[:, k], lambda k: m2_lo[:, k], range(KT)
                        ).then_inc(block_done, 1)
                if j >= 4:
                    pe.wait_ge(acc_read, 2 + 42 + j + 1)
                    for m in range(2):
                        ins = pe.transpose(bank[3 + j % 2][:, m * P:(m + 1) * P], tmp[j % 2][:, m * P:(m + 1) * P], ident[:])
                    ins.then_inc(v2_tr, 1)

            def q_gm(i):
                for r in range(4):
                    read(i * 4 + (50 + r))
                    weights(B_QG + r, i * 4, acc[r % 2][:], *H, range(KT)).then_inc(block_done, 1)
            with pe.Fori(0, 2) as i:
                q_gm(i)
            pe.wait_ge(acc_read, 2 + 58)
            pe.wait_ge(mv2_ready, 4)
            for h in range(4):
                for t in range(4):
                    ins = pe.matmul(score(t), q2[:, h, t * P:(t + 1) * P], mk2[:, h], start=True, stop=True)
                ins.then_inc(sc2_mm, 1)
                pe.wait_ge(n2_ready, h + 1)
                for m in range(2):
                    for t in range(4):
                        ins = pe.transpose(bank[5 + m][:, t * P:(t + 1) * P], probs2[:, t, m * P:(m + 1) * P], ident[:])
                    ins.then_inc(p2_tr, 1)
                pe.wait_ge(p2t_ready, 2 * h + 2)
                for m in range(2):
                    ins = pe.matmul(bank[7][:], mv2[:, m, h * P:(h + 1) * P], probs2_t[:, m], start=m == 0, stop=m == 1)
                ins.then_inc(o2_mm, 1)
            pe.wait_ge(yn_done, 4)

            branches = ((lambda k: f_hi[:, k], lambda k: f_lo[:, k], 6), (lambda k: s_hi[:, k], lambda k: s_lo[:, k], 6),
                        (lambda k: yn_hi[:, k], lambda k: yn_lo[:, k], 4))

            def merge2(i):
                for r in range(2):
                    for n, (hi, lo, ks) in enumerate(branches):
                        b, m = B_M2 + 6 * r + 2 * n, M_OF[B_M2] + 3 * r + n
                        weights(b, i * 12, p_gate[:], *H, range(KT)).then_inc(block_done, 1)
                        free(m, i * 6)
                        weights(b + 1, i * 12, acc[m % 2][:], hi, lo, range(ks)).then_inc(block_done, 1)
                        pe.wait_ge(gate2_ready, i * 6 + (3 * r + n + 1))
            with pe.Fori(0, 4) as i:
                merge2(i)
            pe.wait_ge(mg2_done, KT)
            for j in range(8):
                m = M_OF[B_OUT2] + j
                free(m)
                weights(B_OUT2 + j, 0, acc[m % 2][:], lambda k: g2_hi[:, k], lambda k: g2_lo[:, k], range(KT)
                        ).then_inc(block_done, 1)
                if j >= 1:
                    sum_square(j - 1, 5 * KT + j)
            sum_square(KT - 1, 6 * KT)

def _stream2(I, np):
    w_in = I["w_in_2"][0]
    o_q, o_k, o_v, o_f, o_gf, o_u, o_gs, o_qm, o_gm, o_gl = 0, 768, 1536, 2304, 2316, 3084, 3852, 4620, 5132, 5644
    cols = lambda w, c, n=P: _block(w, slice(0, DM), slice(c, c + n), np)
    out = [cols(w_in, o_f, 12)]
    for j in range(6):
        out += [cols(w_in, o_u + j * P), cols(w_in, o_gs + j * P)]
    for j in range(6):
        out += [cols(w_in, o + j * P) for o in (o_q, o_k, o_v, o_gf)]
    out += [cols(I["w_glu_2"][0], j * P) for j in range(6)]
    out += [cols(I["w_mem_kv_2"][0], j * P) for j in range(8)]
    for j in range(4):
        out += [cols(w_in, o_qm + j * P), cols(w_in, o_gm + j * P)]
    for j in range(KT):
        for n, w in enumerate(("w_proj_fox_2", "w_proj_s5_2", "w_proj_mem_2")):
            out += [cols(w_in, o_gl + n * DM + j * P), cols(I[w][0], j * P)]
    return out + [cols(I["w_out_2"][0], j * P) for j in range(KT)]


def _params2(I, np):
    return [_columns(I["g_norm_2"][0], np), _columns(I["g_mem_norm_2"][0], np), _columns(I["g_final_2"], np),
            _columns(I["b_merge_2"][0], np), _columns(I["lam_re_2"][0].reshape(-1), np),
            _columns(I["lam_im_2"][0].reshape(-1), np), _columns(np.repeat(I["log_step_2"][0], 64), np),
            _columns(I["s5_d_2"][0], np), _columns(I["b_glu_2"][0], np), _columns(I["b_forget_2"][0], np)]


def _arrays2(I, np):
    s5m = np.zeros((7, P, 512), np.float32)
    for j in range(6):
        c = s5m[j, :, 256:].reshape(P, 4, 2, 32)
        for g in range(8):
            s, e = g // 2, g % 2
            for n, (b_, c_) in enumerate((("s5_b_re_2", "s5_c_re_2"), ("s5_b_im_2", "s5_c_im_2"))):
                s5m[j, 16 * g:16 * g + 16, n * P + 64 * e:n * P + 64 * e + 64] = I[b_][0, 8 * j + g].T
                c[64 * e:64 * e + 64, s, n, 16 * e:16 * e + 16] = I[c_][0, 8 * j + g].T
    return {"mem2_t": _channels_first(I["mem_2"][0], np), "s5m": s5m}


def _columns(v, np):
    v = np.asarray(v)
    if v.shape[-1] % P:
        padded = np.zeros(v.shape[:-1] + (P,), v.dtype)
        padded[..., :v.shape[-1]] = v
        v = padded
    return np.moveaxis(v.reshape(v.shape[:-1] + (-1, P)), -1, 0)


def _taps(w, np):
    return np.swapaxes(_columns(w, np), 1, 2).reshape(P, -1)


def _block(w, rows, cols, np):
    part = w[rows, cols]
    padded = np.zeros((KT * P, P), w.dtype)
    padded[:part.shape[0], :part.shape[1]] = part
    return padded.reshape(KT, P, P).transpose(1, 0, 2)


def _channels_first(x, np):
    return np.ascontiguousarray(x.T.reshape(-1, P, x.shape[0]).transpose(1, 0, 2))


def _lru_blocks(w_a, w_x, group, t, np):
    block = np.zeros((P, KT, P), w_a.dtype)
    for n, w in enumerate((w_a, w_x)):
        wide = np.zeros((3 * P, 3 * P), w.dtype)
        for b in range(4):
            wide[96 * b:96 * b + 96, 96 * b:96 * b + 96] = w[4 * group + b]
        block[:, 3 * n:3 * n + 3] = wide[:, t * P:(t + 1) * P].reshape(3, P, P).transpose(1, 0, 2)
    return block


def _stream1(I, np):
    w_in = I["w_in"][0]
    c_z, c_xbc, c_dt, c_lg, c_lx, c_q, c_g = 0, 2048, 5120, 5152, 6688, 8224, 9248
    wide = lambda w, c, n: [_block(w, slice(0, DM), slice(c + j * P, min(c + (j + 1) * P, c + n)), np)
                            for j in range((n + P - 1) // P)]
    out = wide(w_in, c_dt, 32) + wide(w_in, c_xbc, 3072) + wide(w_in, c_z, 2048)
    gates = [wide(w_in, c_g + DM * n, DM) for n in range(3)]

    def branch(n, w):
        parts = [[_block(w, slice(k, min(k + DM, w.shape[0])), slice(j * P, (j + 1) * P), np)
                  for k in range(0, w.shape[0], DM)] for j in range(KT)]
        return [b for j in range(KT) for b in [gates[n][j]] + parts[j]]
    out += branch(0, I["w_br_ssd"][0])
    out += wide(w_in, c_lx, 1536)
    lg = wide(w_in, c_lg, 1536)
    for g in range(4):
        out += [_lru_blocks(I["lru_w_a"][0], I["lru_w_x"][0], g, t, np) for t in range(3)] + lg[3 * g:3 * g + 3]
    out += wide(I["w_kv"][0], 0, 2048)
    out += branch(1, I["w_br_lru"][0])
    out += wide(w_in, c_q, DM)
    out += branch(2, I["w_br_mem"][0])
    out += wide(I["w_out"][0], 0, DM)
    return out


def _params(I, np):
    rep = np.repeat(I["ssd_d"][0], 64)
    t = [_columns(I["norm_g"][0], np), _taps(I["ssd_conv_w"][0], np), _columns(I["ssd_conv_b"][0], np), _columns(rep, np),
         _columns(I["ssd_norm_g"][0].reshape(-1), np), _taps(I["lru_conv_w"][0], np), _columns(I["lru_conv_b"][0], np),
         _columns(I["lru_b_a"][0].reshape(-1), np), _columns(I["lru_b_x"][0].reshape(-1), np),
         _columns(I["lru_lambda"][0], np), _columns(I["mem_norm_g"][0], np), _columns(I["final_g"], np),
         _columns(I["ssd_dt_bias"][0], np), _columns(I["ssd_a_log"][0], np)]
    t += _params2(I, np)
    return np.ascontiguousarray(np.concatenate(t, axis=1))


def kernel(**inputs):
    import numpy as np
    import concourse.bacc as bacc
    from concourse.bass_utils import run_bass_kernel_spmd

    I = {k: np.asarray(v) for k, v in inputs.items()}
    arrays = {
        "x_t": _channels_first(I["x"][0], np),
        "mem_t": _channels_first(I["mem"][0], np),
        "pcol": _params(I, np),
        "wstream": np.ascontiguousarray(np.stack(_stream1(I, np) + _stream2(I, np)).reshape(-1, P, KT * P)),
    }
    arrays.update(_arrays2(I, np))
    nc = bacc.Bacc("TRN2", target_bir_lowering=False, num_devices=1)
    A = {k: nc.dram_tensor(f"in_{k}", a.shape, mybir.dt.float32, kind="ExternalInput").ap() for k, a in arrays.items()}
    out = nc.dram_tensor("out", (P, KT, SEQ), mybir.dt.float32, kind="ExternalOutput").ap()
    build(nc, A, out)
    r = run_bass_kernel_spmd(nc, [{f"in_{k}": a for k, a in arrays.items()}], core_ids=[0])
    y = r.results[0]["out"]
    return np.ascontiguousarray(y.transpose(1, 0, 2).reshape(1, DM, SEQ).transpose(0, 2, 1))
```

```python
import concourse.bass as bass
from concourse import mybir
from contextlib import ExitStack

P = 128
SEQ, MEM, DM = 512, 256, 1024
KT = DM // P
CH, NCH = 128, SEQ // 128
EPS = 1e-6
SLOTS, RAW = 4, 2
SQRT_2_OVER_PI = 0.7978845608028654

XBC_T, Z_T, LRU_T, MEMKV_T = 24, 16, 12, 16
B_DT = 0
B_XBC = B_DT + 1
B_Z = B_XBC + XBC_T
B_MSSD = B_Z + Z_T
B_LX = B_MSSD + 3 * KT
B_LG = B_LX + LRU_T
B_KV = B_LG + 2 * LRU_T
B_MLRU = B_KV + MEMKV_T
B_Q = B_MLRU + 3 * KT
B_MMEM = B_Q + KT
B_OUT = B_MMEM + 2 * KT
B_END1 = B_OUT + KT

PCOLS = [("norm_g", 8), ("conv_w", 4 * 24), ("conv_b", 24), ("ssd_d", 16), ("ssd_g", 16),
         ("lconv_w", 4 * 12), ("lconv_b", 12), ("lru_b_a", 12), ("lru_b_x", 12), ("lru_lam", 12),
         ("mem_g", 8), ("final_g", 8), ("dt_bias", 1), ("a_log", 1),
         ("g_norm_2", 8), ("g_mem_norm_2", 8), ("g_final_2", 8), ("b_merge", 24), ("lam_re", 24), ("lam_im", 24),
         ("log_step", 24), ("s5_d", 6), ("b_glu", 6), ("b_forget", 1)]
PC, _n = {}, 0
for _name, _w in PCOLS:
    PC[_name] = _n
    _n += _w
NPC = _n

B_FL = B_END1
B_UG = B_FL + 1
B_FOX = B_UG + 12
B_GLU = B_FOX + 24
B_KV2 = B_GLU + 6
B_QG = B_KV2 + 8
B_M2 = B_QG + 8
B_OUT2 = B_M2 + 6 * KT
B_END = B_OUT2 + KT
LRU_KS = ((0, 1), (0, 1, 2), (1, 2))
M_OF = {B_DT: 0, B_XBC: 1, B_Z: 25, B_MSSD: 25, B_LX: 33, B_KV: 45, B_MLRU: 61, B_Q: 69, B_MMEM: 77, B_OUT: 85,
        B_FL: 93, B_M2: 94, B_OUT2: 118}
FOX_AT = (7 * P, 8 * P, 4 * P, 0)
FOX_T_AT = (0, 4 * P, 8 * P, 7 * P)
BASE, ARENA = 16512, 212800
MAGIC = 12582912.0
def build(nc, A, out):
    f32, f32r = mybir.dt.float32, mybir.dt.float32r
    ALU, ACT, AX = mybir.AluOpType, mybir.ActivationFunctionType, mybir.AxisListType
    mult, add, sub, vmin, vmax = ALU.mult, ALU.add, ALU.subtract, ALU.min, ALU.max

    ctx = ExitStack()
    with ctx:
        ctx.enter_context(nc.sbuf_tensor("arena", [P, ARENA // 4], f32))

        def at(name, shape, kb, dt=f32):
            size = 4
            for s in shape[1:]:
                size *= s
            assert kb * 1024 + size <= ARENA, (name, kb, size)
            return nc.alloc_sbuf_tensor_at(name, shape, dt, offset=BASE + int(kb * 1024))

        def sem(name):
            return ctx.enter_context(nc.semaphore(name))

        h_hi, h_lo = at("h_hi", [P, KT, SEQ], 0, f32r), at("h_lo", [P, KT, SEQ], 16, f32r)
        raw = at("raw", [P, RAW, KT * P], 32)
        w_hi, w_lo = at("w_hi", [P, SLOTS, KT, P], 40, f32r), at("w_lo", [P, SLOTS, KT, P], 56, f32r)
        pcol = at("pcol", [P, NPC], 72)
        ones = at("ones", [P, P], 74.5)
        ident = at("ident", [P, P], 75)
        tril = at("tril", [P, P], 75.5)
        negm = at("negm", [P, P], 76)
        small = at("small", [P, 512], 76.5)
        tmp = [at(f"tmp{i}", [P, SEQ], 79 + 2 * i) for i in range(6)]
        REG = 93
        xs = at("xs", [P, XBC_T, SEQ], REG)
        y_hi = at("y_hi", [P, 16, SEQ], REG, f32r)
        y_lo = at("y_lo", [P, 16, SEQ], REG + 48, f32r)
        W0 = REG + 80
        x_t = at("x_t", [P, KT, SEQ], REG + 48)
        acs = at("acs", [32, SEQ], W0)
        dt_c = at("dt_c", [32, SEQ], W0 + 2)
        b_cur = at("b_cur", [P, SEQ], W0 + 2)
        tok = at("tok", [P, 4, NCH, 32], W0 + 4)
        b_tok = at("b_tok", [P, NCH, P], W0 + 6)
        cb = at("cb", [P, NCH, P], W0 + 8)
        xdt = [at(f"xdt{i}", [P, NCH, P], W0 + 10 + 2 * i) for i in range(2)]
        xde = at("xde", [P, NCH, P], W0 + 14)
        prev = at("prev", [P, NCH - 1, P], W0 + 16)
        sel = at("sel", [32, 2, 2, P], W0 + 17.5)
        ebc = [at(f"ebc{i}", [P, SEQ], W0 + 19.5 + 2 * i) for i in range(2)]
        gss, gsq = at("gss", [P, SEQ], W0 + 23.5), at("gsq", [P, SEQ], W0 + 25.5)
        gn = [at(f"gn{i}", [P, SEQ], W0 + 27.5 + 2 * i) for i in range(2)]
        rinv = at("rinv", [P, SEQ], W0 + 31.5)
        x_cur, z_silu, y_tmp = at("x_cur", [P, SEQ], 79), at("z_silu", [P, SEQ], 89), at("y_tmp", [P, SEQ], 91)
        seg = [[at(f"seg{i}{e}", [P, SEQ], 81 + 4 * i + 2 * e) for e in range(2)] for i in range(2)]
        merged = at("merged", [P, KT, SEQ], REG + 80)
        xl = at("xl", [P, LRU_T, SEQ], REG)
        l_hi = at("l_hi", [P, LRU_T, SEQ], REG, f32r)
        l_lo = at("l_lo", [P, LRU_T, SEQ], REG + 24, f32r)
        xl_hi, xl_lo = at("xl_hi", [P, 3, SEQ], REG + 48, f32r), at("xl_lo", [P, 3, SEQ], REG + 54, f32r)
        l_r, l_i, l_a = (at(n, [P, 3, SEQ], REG + o) for n, o in (("l_r", 60), ("l_i", 66), ("l_a", 72)))
        mem_t = at("mem_t", [P, KT, MEM], REG + 48)
        mk = at("mk", [P, KT, MEM], REG + 48)
        mv = at("mv", [P, 2, DM], REG + 56)
        m_hi, m_lo = at("m_hi", [P, KT, MEM], REG + 64, f32r), at("m_lo", [P, KT, MEM], REG + 72, f32r)
        q = at("q", [P, KT, SEQ], REG)
        ym_hi, ym_lo = at("ym_hi", [P, KT, SEQ], REG + 16, f32r), at("ym_lo", [P, KT, SEQ], REG + 32, f32r)
        probs = [at(f"probs{i}", [P, 4, MEM], REG + 64 + 4 * i) for i in range(2)]
        probs_t = at("probs_t", [P, 2, SEQ], REG + 72)
        g_hi, g_lo = at("g_hi", [P, KT, SEQ], REG + 48, f32r), at("g_lo", [P, KT, SEQ], REG + 64, f32r)
        x1 = at("x1", [P, KT, SEQ], REG)

        x2_keep = nc.dram_tensor("x2_keep", (P, KT, SEQ), f32, kind="Internal").ap()
        ug = at("ug", [P, 12, SEQ], REG)
        u5, gs = ug[:, 0:6], ug[:, 6:12]
        s_lo, s_hi = at("s_lo", [P, 6, SEQ], REG, f32r), at("s_hi", [P, 6, SEQ], REG + 12, f32r)
        fq, fk = at("fq", [P, 6, SEQ], REG + 24), at("fk", [P, 6, SEQ], REG + 36)
        fv = at("fv", [P, NCH, 6 * P], REG + 48)
        fg = at("fg", [P, 6, SEQ], REG + 60)
        turn_v = at("turn_v", [P, 24, 32, 2], REG + 103)
        turn_u = at("turn_u", [P, 24, 16, 2], REG + 109)
        et = at("et", [P, 2, 2, SEQ], REG + 72)
        s5m = at("s5m", [P, 512], REG + 80)
        cf = at("cf", [P, 4, 2, 32], REG + 82)
        cf_tmp = at("cf_tmp", [P, P], REG + 93)
        v_tmp = at("v_tmp", [P, SEQ], REG + 83)
        sc5 = at("sc5", [P, 20, 24], REG + 112)
        sum_f = at("sum_f", [P, SEQ], REG + 98)
        pool_t = at("pool_t", [P, SEQ], REG + 85)
        u_cur = at("u_cur", [P, SEQ], REG + 87)
        gelu_arg, gelu_sig = at("gelu_arg", [P, SEQ], REG + 89), at("gelu_sig", [P, SEQ], REG + 91)
        s5_a, s5_b = at("s5_a", [P, 2, SEQ], 79), at("s5_b", [P, 2, SEQ], 83)
        y5_hi, y5_lo = at("y5_hi", [P, 6, SEQ], REG + 72, f32r), at("y5_lo", [P, 6, SEQ], REG + 84, f32r)
        PAIR_AT = (REG + 100, REG + 72)
        fq_cur = [[at(f"fq_cur{b}{e}", [P, SEQ], PAIR_AT[b] + 2 * e) for e in range(2)] for b in range(2)]
        fk_cur = [[at(f"fk_cur{b}{e}", [P, SEQ], PAIR_AT[b] + 4 + 2 * e) for e in range(2)] for b in range(2)]
        fv_cur = [at(f"fv_cur{b}", [P, NCH, P], PAIR_AT[b] + 8) for b in range(2)]
        f_p = [at(f"f_p{e}", [P, 1280], REG + 82 + 5 * e) for e in range(2)]
        f_pt = at("f_pt", [P, 1280], REG + 92)
        f_hi, f_lo = at("f_hi", [P, 6, SEQ], REG + 24, f32r), at("f_lo", [P, 6, SEQ], REG + 36, f32r)
        mem2 = at("mem2", [P, KT, MEM], REG + 48)
        mk2, mv2 = at("mk2", [P, 4, MEM], REG + 48), at("mv2", [P, 2, SEQ], REG + 52)
        m2_hi, m2_lo = at("m2_hi", [P, KT, MEM], REG + 56, f32r), at("m2_lo", [P, KT, MEM], REG + 64, f32r)
        yn_hi, yn_lo = at("yn_hi", [P, 4, SEQ], REG + 56, f32r), at("yn_lo", [P, 4, SEQ], REG + 64, f32r)
        gm = at("gm", [P, 4, SEQ], REG + 72)
        q2 = at("q2", [P, 4, SEQ], REG + 80)
        probs2 = [at(f"probs2_{i}", [P, 4, MEM], REG + 88 + 4 * i) for i in range(2)]
        probs2_t = at("probs2_t", [P, 2, SEQ], REG + 96)
        g2_hi, g2_lo = at("g2_hi", [P, KT, SEQ], REG + 72, f32r), at("g2_lo", [P, KT, SEQ], REG + 88, f32r)
        x3 = at("x3", [P, KT, SEQ], REG)

        psum = ctx.enter_context(nc.psum_tensor("psum", [P, 8, SEQ], f32))
        bank = [psum[:, i] for i in range(8)]
        acc = bank[0:2]
        p_gate, p_x, p_bc, p_y, p_off, p_st = bank[2], bank[2], bank[3:5], bank[5], bank[6], bank[7]
        p_norm = bank[7]

        address_step, s_act, s_dve, s_pe, s_pool = (sem(f"{n}_step") for n in ("address", "act", "dve", "pe", "pool"))
        raw_ready = [sem(f"raw_ready{i}") for i in range(RAW)]
        x_loaded, par_loaded, mem_loaded, xre_loaded, out_stored = (
            sem(n) for n in ("x_loaded", "par_loaded", "mem_loaded", "xre_loaded", "out_stored"))
        consts_ready, hi_ready, lo_ready, block_done, acc_free = (
            sem(n) for n in ("consts_ready", "hi_ready", "lo_ready", "block_done", "acc_free"))
        sq_ready, sq_summed, root_ready, split_in, split_hi, split_lo = (
            sem(n) for n in ("sq_ready", "sq_summed", "root_ready", "split_in", "split_hi", "split_lo"))
        u_ready, eu_ready, conv_ready, silu_done = (sem(n) for n in ("u_ready", "eu_ready", "conv_ready", "silu_done"))
        a_exp, acs_ready, tok_t, tok_sub, tok_exp = (
            sem(n) for n in ("a_exp", "acs_ready", "tok_t", "tok_sub", "tok_exp"))
        bcur_ready, b_t, btok_ready, cb_mm, cb_ready, x_cur_ready, x_tr, sel_ready, bc_mm = (
            sem(n) for n in ("bcur_ready", "b_t", "btok_ready", "cb_mm", "cb_ready", "x_cur_ready", "x_tr",
                             "sel_ready", "bc_mm"))
        xd_ready, xde_ready, seg_ready, exp_ready, g_ready, ebc_ready, st_mm, prev_ready, y_mm, z_ready, y_ready = (
            sem(n) for n in ("xd_ready", "xde_ready", "seg_ready", "exp_ready", "g_ready", "ebc_ready", "st_mm",
                             "prev_ready", "y_mm", "z_ready", "y_ready"))
        gss_ready, gsum_mm, groot_ready, gn_in, gn_hi, gn_lo = (
            sem(n) for n in ("gss_ready", "gsum_mm", "groot_ready", "gn_in", "gn_hi", "gn_lo"))
        gate_ready, merge_done = sem("gate_ready"), sem("merge_done")
        lx_done, lam_ready, xlh_ready, xls_ready, gmm_done, sig_ready, dec_ready, m2_ready, m_ready = (
            sem(n) for n in ("lx_done", "lam_ready", "xlh_ready", "xls_ready", "gmm_done", "sig_ready", "dec_ready",
                             "m2_ready", "m_ready"))
        lsilu_ready, ly_in, ly_hi, ly_done = (sem(n) for n in ("lsilu_ready", "ly_in", "ly_hi", "ly_done"))
        kv_ready, v_tr = sem("kv_ready"), sem("v_tr")
        q_ready, sc_mm, mx_ready, pe_ready, pn_ready, p_tr, pt_ready, o_mm, yo_in, yo_hi, yo_done = (
            sem(n) for n in ("q_ready", "sc_mm", "mx_ready", "pe_ready", "pn_ready", "p_tr", "pt_ready", "o_mm",
                             "yo_in", "yo_hi", "yo_done"))
        mg_hi, mg_done, x1_ready = sem("mg_hi"), sem("mg_done"), sem("x1_ready")
        x2_ready, x2_kept, nu_ready, enu_ready, f_ready = (
            sem(n) for n in ("x2_ready", "x2_kept", "nu_ready", "enu_ready", "f_ready"))
        acc_read, step_ready, t_exp, tables_ready = (
            sem(n) for n in ("acc_read", "step_ready", "t_exp", "tables_ready"))
        s5_loaded, fpt_dve, u_cur_ready, address_step2 = (sem(n) for n in ("s5_loaded", "fpt_dve", "u_cur_ready", "address_step2"))
        e_made, e_used, pq_mm, h_ready, h_free, cf_ready, y5_sq, y5_arg, y5_sig, y5_sum, y5_ready, v_evac, v5_tr = (
            sem(n) for n in ("e_made", "e_used", "pq_mm", "h_ready", "h_free", "cf_ready", "y5_sq", "y5_arg", "y5_sig",
                             "y5_sum", "y5_ready", "v_evac", "v5_tr"))
        y5h, y5l, glu_ready, s5_in, s5_hi, s5_done = (
            sem(n) for n in ("y5h", "y5l", "glu_ready", "s5_in", "s5_hi", "s5_done"))
        fz_ready, fcur_ready, fm_ready, fs_mm, fmx_ready, fe_ready, fn_ready, fp_tr, fpt_ready, fo_mm, fo_ready = (
            sem(n) for n in ("fz_ready", "fcur_ready", "fm_ready", "fs_mm", "fmx_ready", "fe_ready", "fn_ready",
                             "fp_tr", "fpt_ready", "fo_mm", "fo_ready"))
        fh, frow_ready, fl_done, mem2_loaded, kv2_ready, v2_tr, mv2_ready, qg_ready = (
            sem(n) for n in ("fh", "frow_ready", "fl_done", "mem2_loaded", "kv2_ready", "v2_tr", "mv2_ready", "qg_ready"))
        sc2_mm, mx2_ready, e2_ready, n2_ready, p2_tr, p2t_ready, o2_mm, yn_in, yn_hi_ready, yn_done = (
            sem(n) for n in ("sc2_mm", "mx2_ready", "e2_ready", "n2_ready", "p2_tr", "p2t_ready", "o2_mm", "yn_in",
                             "yn_hi_ready", "yn_done"))
        gate2_ready, merge2_done, mg2_hi, mg2_done, x3_loaded, x3_ready, fin_ready = (
            sem(n) for n in ("gate2_ready", "merge2_done", "mg2_hi", "mg2_done", "x3_loaded", "x3_ready", "fin_ready"))

        class Steps:

            def __init__(self, eng, own):
                self.eng, self.own, self.n, self.turn = eng, own, 0, 0

            def __call__(self, ins):
                ins.then_inc(self.own, 1)
                self.n += 1
                self.eng.wait_ge(self.own, self.turn + self.n)

            def loop(self, count, steps, body):
                first = self.n
                with self.eng.Fori(0, count) as i:
                    self.turn = i * steps
                    body(i)
                assert self.n - first == steps, f"{self.own}: {self.n - first} steps in a turn, not {steps}"
                self.turn, self.n = 0, first + count * steps

        def made(eng, ins, what, value):
            ins.then_inc(what, 1)
            eng.wait_ge(what, value)

        def col(name, j=0, rows=P):
            return pcol[0:rows, bass.ds(j + PC[name], 1)]

        def col12(name):
            return pcol[:, PC[name]:PC[name] + 12]

        def score(h, t):
            return bank[3 * (1 - h % 2) + t // 2][:, (t % 2) * MEM:(t % 2 + 1) * MEM]

        def maxima(h, t, n=1, what=0):
            return scol(96 + 16 * (h % 2) + 4 * what + t, n)

        def fbank(e, n):
            return bank[2 + 3 * e + n]

        def fcol(e, t, what, n=1):
            return scol(300 + 16 * e + 4 * what + t, n)

        def scol(j, n=1, rows=P):
            return small[0:rows, j:j + n]

        block = ctx.enter_context(nc.Block())

        @block.sync
        def _(sp):
            sp.dma_start(x_t[:], A["x_t"]).then_inc(x_loaded, 16)
            sp.dma_start(pcol[:], A["pcol"]).then_inc(par_loaded, 16)
            for b in range(RAW):
                sp.dma_start(raw[:, b], A["wstream"][b]).then_inc(raw_ready[b], 16)

            def two_blocks(i):
                for r in range(RAW):
                    sp.wait_ge(lo_ready, i * RAW + (r + 1))
                    sp.dma_start(raw[:, r], A["wstream"][bass.ds(i * RAW + (RAW + r), 1)].rearrange("o p c -> (o p) c")
                                 ).then_inc(raw_ready[r], 16)
            with sp.Fori(0, (B_END - RAW) // RAW) as i:
                two_blocks(i)
            for b in range(B_END - (B_END - RAW) % RAW, B_END):
                sp.wait_ge(lo_ready, b - RAW + 1)
                sp.dma_start(raw[:, b % RAW], A["wstream"][b]).then_inc(raw_ready[b % RAW], 16)
            sp.wait_ge(out_stored, 16 * KT)

        @block.gpsimd
        def _(pool):
            step = Steps(pool, s_pool)
            step(pool.memset(ones[:], 1.0))
            step(pool.memset(negm[:], 0.0))
            step(pool.affine_select(out=ident[:], in_=ones[:], compare_op=ALU.is_equal, fill=0.0, base=0,
                                    pattern=[[-1, P]], channel_multiplier=1))
            step(pool.affine_select(out=tril[:], in_=ones[:], compare_op=ALU.is_ge, fill=0.0, base=0,
                                    pattern=[[1, P]], channel_multiplier=-1))
            made(pool, pool.affine_select(out=negm[:], in_=negm[:], compare_op=ALU.is_ge, fill=-1e30, base=0,
                                          pattern=[[-1, P]], channel_multiplier=1), consts_ready, 1)

            def lower_parts(first, off, count):
                for b in range(first, first + count):
                    pool.wait_ge(hi_ready, off + (b + 1))
                    made(pool, pool.tensor_tensor(w_lo[:, b % SLOTS].rearrange("p k c -> p (k c)"), raw[:, b % RAW],
                                                  w_hi[:, b % SLOTS].rearrange("p k c -> p (k c)").bitcast(f32), sub),
                         lo_ready, off + (b + 1))
            
            def blocks(first, end):
                up = min(-(-first // SLOTS) * SLOTS, end)
                for b in range(first, up):
                    lower_parts(b, 0, 1)
                if end // SLOTS > up // SLOTS:
                    with pool.Fori(up // SLOTS, end // SLOTS) as i:
                        lower_parts(0, i * SLOTS, SLOTS)
                    up = end // SLOTS * SLOTS
                for b in range(up, end):
                    lower_parts(b, 0, 1)
            blocks(0, B_Z + SLOTS)

            def select(pair, i):
                pool.wait_ge(bc_mm, pair * 2)
                for e in range(2):
                    pool.sem_inc(address_step2, 1)
                    made(pool, pool.tensor_copy(sel[:, i, e], ident[0:32, bass.ds(pair * 2 + e, 1)].to_broadcast([32, P])),
                         sel_ready, pair * 2 + (e + 1))

            def to_end(pair, i):
                pool.wait_ge(xd_ready, pair + 1)
                if not isinstance(pair, int) or pair:
                    pool.wait_ge(st_mm, pair)
                w4 = lambda a: a.rearrange("p c (e d) -> p c e d", e=2)
                decay = tok[:, 2, :, bass.ds(pair * 2, 2)].unsqueeze(3).to_broadcast([P, NCH, 2, 64])
                pool.sem_inc(address_step2, 1)
                made(pool, pool.tensor_tensor(w4(xde[:]), w4(xdt[i][:]), decay, mult), xde_ready, pair + 1)

            def tile_p(x, j):
                return x[:, bass.ds(j, 1)].rearrange("p o t -> p (o t)")

            def squared(g, r):
                y = tile_p(xs, g * 4 + r)
                pool.wait_ge(y_ready, g * 4 + (r + 2))
                pool.sem_inc(address_step2, 1)
                if r == 0:
                    step(pool.tensor_tensor(gss[:], y, y, mult))
                    return
                step(pool.tensor_tensor(gsq[:], y, y, mult))
                ins = pool.tensor_tensor(gss[:], gss[:], gsq[:], add)
                step(ins) if r < 3 else made(pool, ins, gss_ready, g + 1)

            def group_lower(g, tiles):
                for t in tiles:
                    v = g * 4 + (t + 1)
                    pool.wait_ge(gn_hi, v)
                    pool.sem_inc(address_step2, 1)
                    made(pool, pool.tensor_tensor(tile_p(y_lo, g * 4 + t), gn[t % 2][:], tile_p(y_hi, g * 4 + t).bitcast(f32),
                                                  sub), gn_lo, v)

            def group(g, first=False, last=False):
                for r in range(4):
                    pair = g * 4 + r
                    if not (last and r == 3):
                        select(pair + 1, (r + 1) % 2)
                    lower_parts(B_Z + r + SLOTS, g * 4, 1)
                    if not (last and r == 3):
                        to_end(pair + 1, (r + 1) % 2)
                    if not first and r in (1, 2):
                        group_lower(g - 1, (0, 1) if r == 1 else (2, 3))
                    if r == 0 and not first:
                        pool.wait_ge(gsum_mm, g)
                    squared(g, r)
            pool.wait_ge(tok_exp, 1)
            for e in range(2):
                made(pool, pool.tensor_copy(sel[:, 0, e], ident[0:32, e:e + 1].to_broadcast([32, P])), sel_ready, e + 1)
            to_end(0, 0)
            group(0, first=True)
            step.loop(2, 6, lambda i: group(i + 1))
            group(3, last=True)
            group_lower(3, range(4))
            blocks(B_Z + Z_T + SLOTS, B_FOX)
            pool.wait_ge(tables_ready, 1)

            def powers(j):
                for r in range(4):
                    lower_parts(B_FOX + r, j * 4, 1)
                    s, e = j * 4 + r, et[:, r % 2]
                    pool.wait_ge(e_used, s + 1)

                    def u(c):
                        return turn_u[:, bass.ds(s, 1), :, c].rearrange("p o a -> p (o a)").unsqueeze(2).to_broadcast([P, 16, 32])

                    def v(c):
                        return turn_v[:, bass.ds(s, 1), :, c].to_broadcast([P, 16, 32])
                    w = [x.rearrange("p (a b) -> p a b", a=16) for x in (e[:, 0], e[:, 1], pool_t[:])]

                    def product(out, a, b):
                        pool.sem_inc(address_step2, 1)
                        step(pool.tensor_tensor(out, a, b, mult))
                    product(w[0], u(0), v(0))
                    product(w[2], u(1), v(1))
                    step(pool.tensor_tensor(e[:, 0], e[:, 0], pool_t[:], sub))
                    product(w[1], u(0), v(1))
                    product(w[2], u(1), v(0))
                    made(pool, pool.tensor_tensor(e[:, 1], e[:, 1], pool_t[:], add), e_made, s + 1)
            step.loop(6, 20, powers)
            def forget(b):
                for e in range(2):
                    other = slice(64 - 64 * e, 128 - 64 * e)
                    made(pool, pool.tensor_copy(fk_cur[b][e][other], sum_f[other]), fz_ready, 2 * b + e + 1)

            def rows(i, b):
                j = i * 2 + b
                pool.wait_ge(fo_mm, j * 2 + 2)
                for e in range(2):
                    other = slice(64 - 64 * e, 128 - 64 * e)
                    pool.sem_inc(address_step2, 1)
                    made(pool, pool.tensor_copy(fq_cur[b][e][other],
                                                ident[other, bass.ds(j * 2 + (64 * (1 - e) + e), 1)].to_broadcast([64, SEQ])),
                         frow_ready, j * 2 + (e + 1))
            blocks(B_FOX + 24, B_GLU + SLOTS)
            pool.wait_ge(y5_ready, 6)
            pool.wait_ge(f_ready, 1)
            forget(0)
            rows(0, 0)
            blocks(B_GLU + SLOTS, B_KV2 + SLOTS)
            pool.wait_ge(block_done, B_GLU + 6)
            forget(1)
            rows(0, 1)

            def pairs(i):
                for b in range(2):
                    rows(i + 1, b)
            with pool.Fori(0, 2) as i:
                pairs(i)
            blocks(B_KV2 + SLOTS, B_END)

        @block.scalar
        def _(act):
            step = Steps(act, s_act)

            def activate(out, *args, **more):
                act.sem_inc(address_step, 1)
                return act.activation(out, *args, **more)

            def upper(b, off):
                act.wait_ge(raw_ready[b % RAW], off * 8 + 16 * (b // RAW + 1))
                made(act, act.activation(w_hi[:, b % SLOTS].rearrange("p k c -> p (k c)"), raw[:, b % RAW], ACT.Copy),
                     hi_ready, off + (b + 1))

            def turn(b, off, more=True):
                act.wait_ge(block_done, off + (b + 1))
                if more:
                    upper(b + SLOTS, off)

            def squares(k, x, value):
                if k >= 2:
                    act.wait_ge(sq_summed, value - 2)
                made(act, act.activation(tmp[k % 2][:, 0:x.shape[1]], x, ACT.Square), sq_ready, value)

            def norm(t, x, ntiles, sq0, n):
                for k in range(ntiles):
                    squares(k, x(k), sq0 + k + 1)
                act.wait_ge(sq_summed, sq0 + ntiles)
                made(act, act.activation(tmp[2][:, 0:n], p_norm[:, 0:n], ACT.Sqrt, scale=1.0 / DM, bias=EPS),
                     root_ready, t + 1)

            def split(n0, ntiles, hi):
                for k in range(ntiles):
                    act.wait_ge(split_in, n0 + k + 1)
                    made(act, act.activation(hi[:, k], tmp[k % 2][:, 0:hi.shape[2]], ACT.Copy), split_hi, n0 + k + 1)

            for b in range(SLOTS):
                upper(b, 0) if b < RAW else None
            act.wait_ge(x_loaded, 16)
            norm(0, lambda k: x_t[:, k], KT, 0, SEQ)
            for b in range(RAW, SLOTS):
                upper(b, 0)
            split(0, KT, h_hi)

            turn(B_DT, 0)
            act.wait_ge(u_ready, 1)
            step(act.activation(tmp[1][0:32], tmp[0][0:32], ACT.Abs))
            made(act, act.activation(tmp[1][0:32], tmp[1][0:32], ACT.Exp, scale=-1.0), eu_ready, 1)
            made(act, act.activation(scol(0, 1, 32), col("a_log", 0, 32), ACT.Exp), a_exp, 1)

            def xbc(i):
                for r in range(4):
                    turn(B_XBC + r, i * 4)
                    act.wait_ge(conv_ready, i * 4 + (r + 1))
                    made(act, activate(xs[:, bass.ds(i * 4 + r, 1)].rearrange("p o t -> p (o t)"), tmp[2 + r % 2][:], ACT.Silu), silu_done, i * 4 + (r + 1))
            step.loop(XBC_T // 4, 0, xbc)

            act.wait_ge(tok_sub, 1)
            step(act.activation(tok[:, 2], tok[:, 2], ACT.Exp))
            made(act, act.activation(tok[:, 3].rearrange("p c h -> p (c h)"), p_x[:, 256:384], ACT.Exp), tok_exp, 1)

            def x_copy(pair):
                act.wait_ge(x_tr, pair) if not isinstance(pair, int) or pair else None
                made(act, activate(x_cur[:], xs[:, bass.ds(pair, 1)].rearrange("p o t -> p (o t)"), ACT.Copy),
                     x_cur_ready, pair + 1)

            def decays(pair, i):
                for e in range(2):
                    v = pair * 2 + (e + 1)
                    act.wait_ge(seg_ready, v)
                    made(act, act.activation(ebc[i][64 * e:64 * e + 64], p_bc[e][64 * e:64 * e + 64, :], ACT.Exp), ebc_ready, v)
                    made(act, act.activation(seg[i][e][:], seg[i][e][:], ACT.Exp), exp_ready, v)

            def group_root(g):
                act.wait_ge(gsum_mm, g + 1)
                made(act, act.activation(rinv[:], p_st[:], ACT.Sqrt, scale=1.0 / 512, bias=EPS), groot_ready, g + 1)

            def group_upper(g, tiles):
                for t in tiles:
                    v = g * 4 + (t + 1)
                    act.wait_ge(gn_in, v)
                    made(act, activate(y_hi[:, bass.ds(g * 4 + t, 1)].rearrange("p o t -> p (o t)"), gn[t % 2][:], ACT.Copy),
                         gn_hi, v)

            def group(g, first=False, last=False):
                made(act, activate(b_cur[:], xs[:, bass.ds(g + 16, 1)].rearrange("p o t -> p (o t)"), ACT.Copy), bcur_ready, g + 1)
                for r in range(4):
                    pair = g * 4 + r
                    if r == 1 and not first:
                        group_root(g - 1)
                    if not (last and r == 3):
                        x_copy(pair + 1)
                    turn(B_Z + r, g * 4)
                    act.wait_ge(y_ready, pair + 1)
                    made(act, act.activation(z_silu[:], acc[r % 2][:], ACT.Silu), z_ready, pair + 1)
                    if r == 0:
                        act.wait_ge(b_t, g + 1)
                        made(act, act.activation(b_tok[:].rearrange("p c n -> p (c n)"), p_x[:], ACT.Copy), btok_ready, g + 1)
                    if not (last and r == 3):
                        decays(pair + 1, (r + 1) % 2)
                    if not first and r in (1, 2):
                        group_upper(g - 1, (0, 1) if r == 1 else (2, 3))
            x_copy(0)
            decays(0, 0)
            group(0, first=True)
            step.loop(2, 0, lambda i: group(i + 1))
            group(3, last=True)
            group_root(3)
            group_upper(3, range(4))

            def merge(base, per, gate0):
                tiles = 4 if per == 3 else 2

                def body(i):
                    for r in range(tiles):
                        for x in range(per):
                            turn(base + per * r + x, i * (tiles * per))
                            if x == 0:
                                v = i * tiles + (gate0 + r + 1)
                                made(act, act.activation(tmp[2 + r % 2][:], p_gate[:], ACT.Sigmoid), gate_ready, v)
                        act.wait_ge(merge_done, v)
                return body, KT // tiles

            body, count = merge(B_MSSD, 3, 0)
            step.loop(count, 0, body)

            def lru_x(i):
                for r in range(4):
                    turn(B_LX + r, i * 4)
            step.loop(LRU_T // 4, 0, lru_x)
            step(act.activation(scol(40, 12), col12("lru_lam"), ACT.Abs))
            made(act, act.activation(scol(52, 12), scol(40, 12), ACT.Exp, scale=-1.0), lam_ready, 1)
            act.wait_ge(lam_ready, 2)

            def lru_gates(i):
                for half in range(2):
                    g = i * 2 + half
                    for t in range(3):
                        if half or t:
                            pass
                        act.wait_ge(lx_done, g * 3 + (t + 1))
                        made(act, activate(xl_hi[:, t], xl[:, bass.ds(g * 3 + t, 1)].rearrange("p o t -> p (o t)"),
                                                 ACT.Copy), xlh_ready, g * 3 + (t + 1))
                    for t in range(3):
                        turn(B_LG + 6 * half + t, i * 12)
                        step(activate(l_r[:, t], bank[2 + (t % 2) * 2][:], ACT.Sigmoid, bias=col("lru_b_a", g * 3 + t)))
                        made(act, activate(l_i[:, t], bank[3 + (t % 2) * 2][:], ACT.Sigmoid,
                                                 bias=col("lru_b_x", g * 3 + t)), sig_ready, g * 3 + (t + 1))
                    for t in range(3):
                        step(activate(l_a[:, t], l_r[:, t], ACT.Exp, scale=small[:, bass.ds(g * 3 + (t + 64), 1)]))
                        step(activate(l_r[:, t], l_r[:, t], ACT.Tanh, scale=small[:, bass.ds(g * 3 + (t + 76), 1)]))
                    for t in range(3):
                        made(act, act.activation(tmp[2][:], l_a[:, t], ACT.Square), dec_ready, g * 3 + (t + 1))
                        act.wait_ge(m2_ready, g * 3 + (t + 1))
                    made(act, act.activation(l_r[:].rearrange("p t n -> p (t n)"), l_r[:].rearrange("p t n -> p (t n)"),
                                             ACT.Sqrt), m_ready, g + 1)
                    for t in range(3):
                        turn(B_LG + 6 * half + 3 + t, i * 12)
                        v = g * 3 + (t + 1)
                        made(act, act.activation(tmp[2 + t % 2][:], acc[(half + t) % 2][:], ACT.Silu), lsilu_ready, v)
                        act.wait_ge(ly_in, v)
                        made(act, activate(l_hi[:, bass.ds(g * 3 + t, 1)].rearrange("p o t -> p (o t)"),
                                                 tmp[4 + t % 2][:], ACT.Copy), ly_hi, v)
            step.loop(2, 18, lru_gates)

            act.wait_ge(ly_done, LRU_T)
            act.dma_start(mem_t[:], A["mem_t"]).then_inc(mem_loaded, 16)
            act.wait_ge(mem_loaded, 16)
            norm(1, lambda k: mem_t[:, k], KT, KT, MEM)
            split(KT, KT, m_hi)

            def kv(i):
                for r in range(4):
                    turn(B_KV + r, i * 4)
            step.loop(MEMKV_T // 4, 0, kv)
            act.wait_ge(step_ready, 1)
            step(act.activation(sc5[:, 3], sc5[:, 1], ACT.Sin))
            step(act.activation(sc5[:, 4], sc5[:, 1], ACT.Sin, scale=0.5))
            step(act.activation(sc5[:, 5], sc5[:, 2], ACT.Tanh, scale=0.5))
            step(act.activation(sc5[:, 7], sc5[:, 6], ACT.Exp))
            made(act, act.activation(sc5[:, 8], sc5[:, 9], ACT.Exp), t_exp, 1)
            body, count = merge(B_MLRU, 3, KT)
            step.loop(count, 0, body)

            def queries(i):
                for r in range(4):
                    turn(B_Q + r, i * 4)
            step.loop(2, 0, queries)

            def exponentials(h):
                act.wait_ge(mx_ready, h + 1)
                if h >= 2:
                    act.wait_ge(p_tr, 2 * h - 2)
                for t in range(4):
                    ins = act.activation(probs[h % 2][:, t], score(h, t), ACT.Exp, scale=1.0 / 16, bias=maxima(h, t, what=1),
                                         accum_out=maxima(h, t, what=2))
                    made(act, ins, pe_ready, 4 * h + t + 1)
            exponentials(0)
            for h in range(4):
                if h < 3:
                    exponentials(h + 1)
                for d in range(2):
                    v = 2 * h + d + 1
                    act.wait_ge(yo_in, v)
                    made(act, act.activation(ym_hi[:, 2 * h + d], tmp[d][:], ACT.Copy), yo_hi, v)

            def merge_mem(i):
                for r in range(2):
                    turn(B_MMEM + 2 * r, i * 4)
                    v = i * 2 + (r + 1)
                    made(act, act.activation(tmp[2 + r % 2][:], p_gate[:], ACT.Sigmoid), gate_ready, v + 2 * KT)
                    turn(B_MMEM + 2 * r + 1, i * 4)
                    act.wait_ge(merge_done, v + 2 * KT)
                    made(act, activate(g_hi[:, bass.ds(i * 2 + r, 1)].rearrange("p o t -> p (o t)"),
                                             merged[:, bass.ds(i * 2 + r, 1)].rearrange("p o t -> p (o t)"), ACT.Copy),
                         mg_hi, v)
            step.loop(4, 0, merge_mem)
            act.dma_start(x1[:], A["x_t"]).then_inc(xre_loaded, 16)

            def outs(i):
                for r in range(4):
                    turn(B_OUT + r, i * 4)
            step.loop(2, 0, outs)

            for k in range(KT):
                act.wait_ge(x1_ready, k + 1)
                squares(k, x1[:, k], 2 * KT + k + 1)
            act.wait_ge(sq_summed, 3 * KT)
            made(act, act.activation(tmp[2][:], p_norm[:], ACT.Sqrt, scale=1.0 / DM, bias=EPS), root_ready, 3)
            for k in range(KT):
                act.wait_ge(x2_ready, k + 1)
                squares(k, x1[:, k], 3 * KT + k + 1)
            act.dma_start(x2_keep, x1[:]).then_inc(x2_kept, 16)
            act.wait_ge(sq_summed, 4 * KT)
            made(act, act.activation(tmp[2][:], p_norm[:], ACT.Sqrt, scale=1.0 / DM, bias=EPS), root_ready, 4)
            split(2 * KT, KT, h_hi)

            turn(B_FL, 0)
            act.wait_ge(nu_ready, 1)
            step(act.activation(tmp[1][:], tmp[0][:], ACT.Abs))
            made(act, act.activation(tmp[1][:], tmp[1][:], ACT.Exp, scale=-1.0), enu_ready, 1)
            act.wait_ge(x2_kept, 16)
            act.sem_inc(acc_read, 2)

            def tile(x, j):
                return x[:, bass.ds(j, 1)].rearrange("p o t -> p (o t)")

            def read(out, *args, n, **more):
                made(act, activate(out, *args, **more), acc_read, n + 3)

            def u_gs(i):
                for r in range(4):
                    turn(B_UG + r, i * 4)
                    j, n = i * 2 + r // 2, i * 4 + r
                    read(tile(ug, j + 6 * (r % 2)), acc[r % 2][:], ACT.Silu if r % 2 else ACT.Copy, n=n)
            step.loop(3, 0, u_gs)
            act.dma_start(s5m[:], A["s5m"][0]).then_inc(s5_loaded, 16)

            made(act, act.activation(u_cur[:], u5[:, 0], ACT.Copy), u_cur_ready, 1)

            def gelu_square(j):
                act.wait_ge(y5_sum, j + 2)
                made(act, activate(gelu_arg[:], tile(ug, j), ACT.Square), y5_sq, j + 1)

            def gelu_sigmoid(j):
                act.wait_ge(y5_arg, j + 1)
                made(act, act.activation(gelu_sig[:], gelu_arg[:], ACT.Sigmoid, scale=2 * SQRT_2_OVER_PI), y5_sig, j + 1)

            def fox_s5(j, before=None):
                for r in range(4):
                    turn(B_FOX + r, j * 4)
                    n = j * 4 + (12 + r)
                    if r == 0:
                        read(tile(fq, j), acc[0][:], ACT.Copy, n=n, scale=0.125)
                        if before is not None:
                            gelu_square(before)
                    elif r == 1:
                        read(tile(fk, j), acc[1][:], ACT.Copy, n=n)
                        if before is not None:
                            gelu_sigmoid(before)
                    elif r == 2:
                        read(v_tmp[:], acc[0][:], ACT.Copy, n=n)
                        act.wait_ge(pq_mm, j * 4 + 4)
                        act.wait_ge(cf_ready, j + 1)
                        act.dma_start(s5m[:], A["s5m"][bass.ds(j + 1, 1)].rearrange("o p c -> (o p) c")).then_inc(s5_loaded, 16)
                        made(act, activate(u_cur[:], tile(ug, j + 1), ACT.Copy), u_cur_ready, j + 2)
                    else:
                        read(tile(fg, j), acc[1][:], ACT.Silu, n=n)
                act.wait_ge(v5_tr, j + 1)
                made(act, activate(fv[:, :, bass.ds(j * P, P)], bank[7][:].rearrange("p (k d) -> p k d", k=NCH), ACT.Copy),
                     v_evac, j + 1)
            fox_s5(0)
            step.loop(5, 0, lambda i: fox_s5(i + 1, i))
            gelu_square(5)
            gelu_sigmoid(5)

            act.wait_ge(s5_loaded, 16 * 7)
            for j in range(6):
                act.wait_ge(y5_ready, 6)
                made(act, act.activation(y5_hi[:, j], u5[:, j], ACT.Copy), y5h, j + 1)
            for j in range(6):
                turn(B_GLU + j, 0)
                made(act, act.activation(tmp[2 + j % 2][:], acc[j % 2][:], ACT.Sigmoid, bias=col("b_glu", j)), acc_read, 2 + 36 + j + 1)
                act.wait_ge(s5_in, j + 1)
                made(act, act.activation(s_hi[:, j], tmp[j % 2][:], ACT.Copy), s5_hi, j + 1)

            def fox_turned(h, e):
                act.wait_ge(fp_tr, h * 3 + 1)
                step(act.activation(f_pt[:, 0:SEQ], fbank(e, 0)[:], ACT.Copy))
                act.wait_ge(fp_tr, h * 3 + 3)
                made(act, act.activation(f_pt[:, 2 * SEQ:], fbank(e, 2)[:, 0:2 * P], ACT.Copy), fpt_ready, h + 1)

            def fox_exp(h, e):
                act.wait_ge(fmx_ready, h + 1)
                for t in range(4):
                    o, w = FOX_AT[t], (t + 1) * P
                    ins = act.activation(f_p[e][:, o:o + w], fbank(e, o // SEQ)[:, o % SEQ:o % SEQ + w], ACT.Exp,
                                         bias=fcol(e, t, 1), accum_out=fcol(e, t, 2))
                    made(act, ins, fe_ready, h * 4 + (t + 1))

            def fox_copies(i, b):
                j = i * 2 + b
                act.wait_ge(fo_mm, j * 2 + 2)
                copies = [(x[hs], y[hs, bass.ds(j, 1)].rearrange("p o t -> p (o t)"))
                          for e in range(2) for hs in (slice(64 * e, 64 * e + 64),)
                          for x, y in ((fq_cur[b][e], fq), (fk_cur[b][e], fk))]
                for n, (out_, x) in enumerate(copies + [(fv_cur[b][:], fv[:, :, bass.ds(j * P, P)])]):
                    made(act, activate(out_, x, ACT.Copy), fcur_ready, j * 5 + (n + 1))

            def fox(i, first=False):
                fox_copies(i, 0)
                for n in range(4):
                    h = i * 4 + n
                    if not (first and n == 0):
                        fox_turned(h - 1, (n + 1) % 2)
                    if first and n == 0:
                        act.wait_ge(block_done, B_GLU + 6)
                        fox_copies(i, 1)
                    fox_exp(h, n % 2)
                    if n == 0 and not first:
                        fox_copies(i, 1)
            fox(0, True)
            step.loop(2, 4, lambda i: fox(i + 1))
            fox_turned(11, 1)
            act.wait_ge(fo_ready, 2 + 6)
            for j in range(6):
                made(act, act.activation(f_hi[:, j], fg[:, j], ACT.Copy), fh, j + 1)

            act.wait_ge(fl_done, 6)
            act.dma_start(mem2[:], A["mem2_t"]).then_inc(mem2_loaded, 16)
            act.wait_ge(mem2_loaded, 16)
            norm(4, lambda k: mem2[:, k], KT, 4 * KT, MEM)
            split(3 * KT, KT, m2_hi)
            for j in range(8):
                turn(B_KV2 + j, 0)
                if j < 4:
                    made(act, act.activation(mk2[:, j], acc[j % 2][:, 0:MEM], ACT.Copy), acc_read, 2 + 42 + j + 1)
                else:
                    made(act, act.activation(tmp[j % 2][:, 0:MEM], acc[j % 2][:, 0:MEM], ACT.Copy), acc_read, 2 + 42 + j + 1)
                    act.wait_ge(v2_tr, j - 3)
                    made(act, act.activation(mv2[:, :, (j - 4) * P:(j - 3) * P],
                                             bank[3 + j % 2][:, 0:MEM].rearrange("p (m d) -> p m d", m=2), ACT.Copy),
                         mv2_ready, j - 3)

            def q_gm(i):
                for r in range(4):
                    turn(B_QG + r, i * 4)
                    j, n = i * 2 + r // 2, i * 4 + (50 + r)
                    read(tile(gm if r % 2 else q2, j), acc[r % 2][:], ACT.Silu if r % 2 else ACT.Copy, n=n)
            step.loop(2, 0, q_gm)

            def exponentials2(h):
                act.wait_ge(mx2_ready, h + 1)
                if h >= 2:
                    act.wait_ge(p2_tr, 2 * h - 2)
                for t in range(4):
                    ins = act.activation(probs2[h % 2][:, t], score(h, t), ACT.Exp, scale=P ** -0.5,
                                         bias=maxima(h, t, what=1), accum_out=maxima(h, t, what=2))
                    made(act, ins, e2_ready, 4 * h + t + 1)
            exponentials2(0)
            for h in range(4):
                if h < 3:
                    exponentials2(h + 1)
                act.wait_ge(yn_in, h + 1)
                made(act, act.activation(yn_hi[:, h], tmp[h % 2][:], ACT.Copy), yn_hi_ready, h + 1)

            def merge2(i):
                for r in range(2):
                    for n in range(3):
                        v = i * 6 + (3 * r + n + 1)
                        turn(B_M2 + 6 * r + 2 * n, i * 12)
                        made(act, activate(tmp[2 + (r + n) % 2][:], p_gate[:], ACT.Sigmoid,
                                           bias=col("b_merge", i * 2 + (r + n * KT))), gate2_ready, v)
                        turn(B_M2 + 6 * r + 2 * n + 1, i * 12)
                        act.wait_ge(merge2_done, v)
                    v = i * 2 + (r + 1)
                    made(act, activate(tile(g2_hi, i * 2 + r), tmp[4][:], ACT.Copy), mg2_hi, v)
            step.loop(4, 0, merge2)
            act.dma_start(x3[:], x2_keep).then_inc(x3_loaded, 16)
            for j in range(8):
                turn(B_OUT2 + j, 0, more=B_OUT2 + j + SLOTS < B_END)
                act.wait_ge(x3_ready, j + 1)
                squares(j, x3[:, j], 5 * KT + j + 1)
            act.wait_ge(sq_summed, 6 * KT)
            made(act, act.activation(tmp[2][:], p_norm[:], ACT.Sqrt, scale=1.0 / DM, bias=EPS), root_ready, 6)
            for k in range(KT):
                act.wait_ge(fin_ready, k + 1)
                act.dma_start(out[:, k], x3[:, k]).then_inc(out_stored, 16)

        @block.vector
        def _(dve):
            step = Steps(dve, s_dve)

            def flat(ap):
                return ap.rearrange("p o t -> p (o t)")

            def tile(x, j):
                return flat(x[:, bass.ds(j, 1)])

            def free_acc(value):
                dve.sem_inc(acc_free, 1)

            def norm_split(t, n0, x, g, ntiles, hi, lo, n, dst=None):
                dve.wait_ge(root_ready, t + 1)
                step(dve.reciprocal(tmp[3][:, 0:n], tmp[2][:, 0:n]))

                def lower(k):
                    dve.wait_ge(split_hi, n0 + k + 1)
                    made(dve, dve.tensor_tensor(lo[:, k], tmp[k % 2][:, 0:n], hi[:, k].bitcast(f32), sub),
                         split_lo, n0 + k + 1)
                for k in range(ntiles):
                    made(dve, dve.scalar_tensor_tensor(tmp[k % 2][:, 0:n], x(k), col(g, k), tmp[3][:, 0:n], mult, mult),
                         split_in, n0 + k + 1)
                    if k:
                        lower(k - 1)
                lower(ntiles - 1)

            def log1p_exp(u, e, out, w, n):
                z, z2, s = w
                step(dve.tensor_scalar(z, e, 2.0, None, add))
                step(dve.reciprocal(z, z))
                step(dve.tensor_tensor(z, z, e, mult))
                step(dve.tensor_tensor(z2, z, z, mult))
                step(dve.tensor_scalar(s, z2, 1.0 / 17, None, mult))
                for m in (15, 13, 11, 9, 7, 5, 3):
                    step(dve.scalar_tensor_tensor(s, s, 1.0 / m, z2, add, mult))
                step(dve.scalar_tensor_tensor(s, s, 1.0, z, add, mult))
                step(dve.tensor_scalar(z2, u, 0.0, None, vmax))
                step(dve.scalar_tensor_tensor(out, s, 2.0, z2, mult, add))

            dve.sem_inc(acc_free, 2)
            dve.wait_ge(par_loaded, 16)
            dve.wait_ge(x_loaded, 16)
            norm_split(0, 0, lambda k: x_t[:, k], "norm_g", KT, h_hi, h_lo, SEQ)

            dve.wait_ge(block_done, B_DT + 1)
            made(dve, dve.tensor_scalar(tmp[0][0:32], acc[0][0:32, :], col("dt_bias", 0, 32), None, add), u_ready, 1)
            free_acc(1)
            dve.wait_ge(eu_ready, 1)
            log1p_exp(tmp[0][0:32], tmp[1][0:32], dt_c[:], (tmp[2][0:32], tmp[3][0:32], tmp[4][0:32]), SEQ)
            dve.wait_ge(a_exp, 1)
            step(dve.tensor_scalar(tmp[0][0:32], dt_c[:], scol(0, 1, 32), -1.0, mult, mult))
            dve.wait_ge(consts_ready, 1)
            for c in range(NCH):
                cs = slice(c * CH, (c + 1) * CH)
                step(dve.tensor_tensor_scan(acs[:, cs], ones[0:32, :], tmp[0][0:32, cs], 0.0, mult, add))
            for c in range(NCH):
                ins = dve.tensor_scalar(small[0:32, 128 + 32 * c:160 + 32 * c], ident[0:32, 0:32],
                                        acs[:, (c + 1) * CH - 1:(c + 1) * CH], None, mult)
                made(dve, ins, acs_ready, c + 1)

            def conv(j, src, y, w, b):
                step(dve.tensor_scalar(y[:], src[:], col(w, j * 4 + 3), col(b, j), mult, add))
                for d in (1, 2, 3):
                    ins = dve.scalar_tensor_tensor(y[:, d:SEQ], src[:, 0:SEQ - d], col(w, j * 4 + (3 - d)), y[:, d:SEQ],
                                                   mult, add)
                    if d < 3:
                        step(ins)
                return ins

            def xbc(i):
                for r in range(4):
                    j = i * 4 + r
                    dve.wait_ge(block_done, j + (B_XBC + 1))
                    dve.wait_ge(hi_ready, i * 4 + (B_XBC + SLOTS + r))
                    made(dve, conv(j, acc[(B_XBC + r) % 2], tmp[2 + r % 2], "conv_w", "conv_b"), conv_ready, j + 1)
                    free_acc(0)
            step.loop(XBC_T // 4, 12, xbc)

            dve.wait_ge(tok_t, 1)
            step(dve.tensor_copy(tok[:, 0:2].rearrange("p a c h -> p (a c h)"), p_x[:, 0:256]))
            made(dve, dve.tensor_tensor(tok[:, 2].rearrange("p c h -> p (c h)"), p_x[:, 256:384],
                                        tok[:, 1].rearrange("p c h -> p (c h)"), sub), tok_sub, 1)
            dve.wait_ge(tok_exp, 1)

            def heads(t, pair):
                return tok[:, t, :, bass.ds(pair * 2, 2)].unsqueeze(3).to_broadcast([P, NCH, 2, 64])

            def inputs(pair, i):
                dve.wait_ge(x_tr, pair + 1)
                v4 = p_x[:].rearrange("p (c e d) -> p c e d", c=NCH, e=2)
                made(dve, dve.tensor_tensor(xdt[i][:].rearrange("p c (e d) -> p c e d", e=2), v4, heads(0, pair), mult),
                     xd_ready, pair + 1)

            def exponents(pair, i, e):
                dve.wait_ge(bc_mm, pair * 2 + (e + 3))
                for c in range(NCH):
                    cs = slice(c * CH, (c + 1) * CH)
                    ins = dve.tensor_scalar(seg[i][e][:, cs], p_bc[e][:, cs], tok[:, 1, c, bass.ds(pair * 2 + e, 1)],
                                            0.0, sub, vmin)
                    if c < NCH - 1:
                        step(ins)
                made(dve, ins, seg_ready, pair * 2 + (e + 1))

            def weighted(pair, i):
                for e in range(2):
                    dve.wait_ge(exp_ready, pair * 2 + (e + 1))
                    made(dve, dve.tensor_tensor(seg[i][e][:], seg[i][e][:], cb[:].rearrange("p c l -> p (c l)"), mult),
                         g_ready, pair * 2 + (e + 1))

            def carried(pair):
                dve.wait_ge(st_mm, pair + 1)
                step(dve.tensor_copy(prev[:, 0], p_st[:, 0:CH]))
                for c in (1, 2):
                    for e in range(2):
                        hs = slice(64 * e, 64 * e + 64)
                        ins = dve.scalar_tensor_tensor(prev[:, c, hs], prev[:, c - 1, hs],
                                                       tok[:, 3, c, bass.ds(pair * 2 + e, 1)],
                                                       p_st[:, c * CH + 64 * e:c * CH + 64 * e + 64], mult, add)
                        if c == 2 and e == 1:
                            made(dve, ins, prev_ready, pair + 1)
                        else:
                            step(ins)

            def outputs(pair, i):
                dve.wait_ge(y_mm, pair + 1)
                dve.wait_ge(ebc_ready, pair * 2 + 2)
                step(dve.scalar_tensor_tensor(y_tmp[:], tile(xs, pair), col("ssd_d", pair), p_y[:], mult, add))
                step(dve.tensor_tensor(ebc[i][:, CH:], p_off[:, CH:], ebc[i][:, CH:], mult))
                step(dve.tensor_tensor(y_tmp[:, CH:], y_tmp[:, CH:], ebc[i][:, CH:], add))
                dve.wait_ge(z_ready, pair + 1)
                made(dve, dve.tensor_tensor(tile(xs, pair), y_tmp[:], z_silu[:], mult), y_ready, pair + 2)

            def group_norm(g, tiles):
                if 0 in tiles:
                    dve.wait_ge(groot_ready, g + 1)
                    step(dve.reciprocal(rinv[:], rinv[:]))
                for t in tiles:
                    if t >= 2:
                        dve.wait_ge(gn_lo, g * 4 + (t - 1))
                    made(dve, dve.scalar_tensor_tensor(gn[t % 2][:], tile(xs, g * 4 + t), col("ssd_g", g * 4 + t), rinv[:],
                                                       mult, mult), gn_in, g * 4 + (t + 1))

            def group(g, first=False, last=False):
                for r in range(4):
                    pair, i = g * 4 + r, r % 2
                    if r == 0:
                        dve.wait_ge(cb_mm, g + 1)
                        made(dve, dve.tensor_tensor(cb[:], p_off[:].rearrange("p (c l) -> p c l", c=NCH),
                                                    tril[:].unsqueeze(1).to_broadcast([P, NCH, CH]), mult), cb_ready, g + 1)
                    weighted(pair, i)
                    if not first and r in (1, 2):
                        group_norm(g - 1, (0, 1) if r == 1 else (2, 3))
                    if not (last and r == 3):
                        inputs(pair + 1, 1 - i)
                        exponents(pair + 1, 1 - i, 0)
                    carried(pair)
                    if not (last and r == 3):
                        exponents(pair + 1, 1 - i, 1)
                    outputs(pair, i)
            dve.sem_inc(y_ready, 1)
            inputs(0, 0)
            for e in range(2):
                exponents(0, 0, e)
            group(0, first=True)
            step.loop(2, 53, lambda i: group(i + 1))
            group(3, last=True)
            group_norm(3, range(4))
            dve.wait_ge(gn_lo, 16)

            def merge(base, per, gate0, first):
                tiles = 4 if per == 3 else 2

                def body(i):
                    for r in range(tiles):
                        j = i * tiles + r
                        v = i * tiles + (gate0 + r + 1)
                        dve.wait_ge(gate_ready, v)
                        dve.wait_ge(block_done, i * (tiles * per) + (base + per * (r + 1)))
                        if first:
                            made(dve, dve.tensor_tensor(tile(merged, j), acc[(M_OF[base] + r) % 2][:], tmp[2 + r % 2][:], mult),
                                 merge_done, v)
                            free_acc(0)
                        else:
                            step(dve.tensor_tensor(tmp[4][:], acc[(M_OF[base] + r) % 2][:], tmp[2 + r % 2][:], mult))
                            free_acc(0)
                            made(dve, dve.tensor_tensor(tile(merged, j), tile(merged, j), tmp[4][:], add), merge_done, v)
                return body, KT // tiles
            body, count = merge(B_MSSD, 3, 0, True)
            step.loop(count, 0, body)

            def lru_x(i):
                for r in range(4):
                    j = i * 4 + r
                    dve.wait_ge(block_done, j + (B_LX + 1))
                    y = tmp[2 + r % 2]
                    step(conv(j, acc[(M_OF[B_LX] + r) % 2], y, "lconv_w", "lconv_b"))
                    free_acc(0)
                    made(dve, dve.tensor_copy(tile(xl, j), y[:]), lx_done, j + 1)
            step.loop(LRU_T // 4, 16, lru_x)
            dve.wait_ge(lam_ready, 1)
            step(dve.tensor_scalar(scol(40, 12), col12("lru_lam"), -1.0, None, mult))
            log1p_exp(scol(40, 12), scol(52, 12), scol(88, 12), (scol(256, 12), scol(268, 12), scol(280, 12)), 12)
            step(dve.tensor_scalar(scol(64, 12), scol(88, 12), -8.0, None, mult))
            made(dve, dve.tensor_scalar(scol(76, 12), scol(88, 12), 8.0, None, mult), lam_ready, 2)

            def lru_gates(i):
                for half in range(2):
                    g = i * 2 + half
                    for t in range(3):
                        v = g * 3 + (t + 1)
                        dve.wait_ge(xlh_ready, v)
                        made(dve, dve.tensor_tensor(xl_lo[:, t], tile(xl, g * 3 + t), xl_hi[:, t].bitcast(f32), sub), xls_ready, v)
                    for t in range(3):
                        v = g * 3 + (t + 1)
                        dve.wait_ge(sig_ready, v)
                        step(dve.tensor_tensor(l_i[:, t], l_i[:, t], tile(xl, g * 3 + t), mult))
                    for t in range(3):
                        v = g * 3 + (t + 1)
                        dve.wait_ge(dec_ready, v)
                        made(dve, dve.scalar_tensor_tensor(l_r[:, t], tmp[2][:], 1.0, l_r[:, t], add, mult), m2_ready, v)
                    dve.wait_ge(m_ready, g + 1)
                    for t in range(3):
                        step(dve.tensor_tensor(l_i[:, t], l_i[:, t], l_r[:, t], mult))
                        step(dve.tensor_tensor_scan(l_r[:, t], l_a[:, t], l_i[:, t], 0.0, mult, add))
                    for t in range(3):
                        v = g * 3 + (t + 1)
                        y = tmp[4 + t % 2]
                        dve.wait_ge(lsilu_ready, v)
                        made(dve, dve.tensor_tensor(y[:], l_r[:, t], tmp[2 + t % 2][:], mult), ly_in, v)
                        dve.wait_ge(ly_hi, v)
                        made(dve, dve.tensor_tensor(tile(l_lo, g * 3 + t), y[:], tile(l_hi, g * 3 + t).bitcast(f32), sub),
                             ly_done, v)
            step.loop(2, 18, lru_gates)

            dve.wait_ge(mem_loaded, 16)
            norm_split(1, KT, lambda k: mem_t[:, k], "mem_g", KT, m_hi, m_lo, MEM)

            def kv(i):
                for r in range(4):
                    j = i * 4 + r
                    dve.wait_ge(block_done, j + (B_KV + 1))
                    made(dve, dve.tensor_copy(tile(mk, j), acc[(M_OF[B_KV] + r) % 2][:, 0:MEM]), kv_ready, j + 1)
                    free_acc(0)
            step.loop(2, 0, kv)

            def values(i):
                for r in range(4):
                    j = i * 4 + r
                    dve.wait_ge(block_done, j + (B_KV + KT + 1))
                    made(dve, dve.tensor_copy(tmp[r % 2][:, 0:MEM], acc[(M_OF[B_KV] + r) % 2][:, 0:MEM]), kv_ready, j + (KT + 1))
                    free_acc(0)
                    dve.wait_ge(v_tr, j + 1)
                    step(dve.tensor_copy(mv[:, :, bass.ds(j * P, P)],
                                         bank[3 + r % 2][:, 0:MEM].rearrange("p (m d) -> p m d", m=2)))
            step.loop(2, 4, values)
            def exponential(x, out, w):
                n, p, two_n = w
                step(dve.tensor_scalar(p, x, -88.0, 88.0, vmax, vmin))
                step(dve.tensor_scalar(n, p, 1.4426950408889634, MAGIC, mult, add))
                step(dve.tensor_scalar(n, n, -MAGIC, None, add))
                step(dve.scalar_tensor_tensor(p, n, -0.693359375, p, mult, add))
                step(dve.scalar_tensor_tensor(p, n, 2.12194440e-4, p, mult, add))
                step(dve.tensor_scalar(n, n, 127.0, 8388608.0, add, mult))
                step(dve.tensor_copy(two_n.bitcast(mybir.dt.int32), n))
                step(dve.tensor_scalar(out, p, 1.0 / 5040, None, mult))
                for c in (1.0 / 720, 1.0 / 120, 1.0 / 24, 1.0 / 6, 0.5, 1.0):
                    step(dve.scalar_tensor_tensor(out, out, c, p, add, mult))
                step(dve.tensor_scalar(out, out, 1.0, None, add))
                step(dve.tensor_tensor(out, out, two_n, mult))

            def cmul(or_, oi, ar, ai, br, bi, w):
                step(dve.tensor_tensor(w, ai, bi, mult))
                step(dve.tensor_tensor(or_, ar, br, mult))
                step(dve.tensor_tensor(or_, or_, w, sub))
                step(dve.tensor_tensor(w, ai, br, mult))
                step(dve.tensor_tensor(oi, ar, bi, mult))
                step(dve.tensor_tensor(oi, oi, w, add))

            s5 = lambda c: sc5[:, c]
            lam_re, lam_im, log_step = (pcol[:, PC[n]:PC[n] + 24] for n in ("lam_re", "lam_im", "log_step"))
            exponential(log_step, s5(0), (s5(10), s5(11), s5(12)))
            step(dve.tensor_tensor(s5(1), lam_im, s5(0), mult))
            step(dve.tensor_scalar(s5(10), s5(1), 0.15915494309189535, MAGIC, mult, add))
            step(dve.tensor_scalar(s5(10), s5(10), -MAGIC, None, add))
            for c in (6.28125, 1.9340515136718750e-3, 1.2556659146e-6):
                step(dve.scalar_tensor_tensor(s5(1), s5(10), -c, s5(1), mult, add))
            step(dve.tensor_scalar(s5(1), s5(1), 3.1415925, -3.1415925, vmin, vmax))
            step(dve.tensor_tensor(s5(13), lam_re, s5(0), mult))
            step(dve.tensor_scalar(s5(2), s5(13), 1.0, None, vmin))
            step(dve.tensor_scalar(s5(6), s5(13), 1.0, 88.0, vmax, vmin))
            made(dve, dve.memset(s5(9), 1.0), step_ready, 1)
            dve.wait_ge(t_exp, 1)
            step(dve.tensor_scalar(s5(10), s5(5), -1.0, 1.0, mult, add))
            step(dve.reciprocal(s5(10), s5(10)))
            step(dve.scalar_tensor_tensor(s5(10), s5(5), 2.0, s5(10), mult, mult))
            step(dve.tensor_tensor(s5(11), s5(7), s5(8), sub))
            step(dve.tensor_tensor(s5(10), s5(10), s5(11), add))
            step(dve.tensor_scalar(s5(14), s5(10), 1.0, None, add))
            step(dve.tensor_tensor(s5(11), s5(4), s5(4), mult))
            step(dve.tensor_scalar(s5(11), s5(11), -2.0, None, mult))
            step(dve.tensor_scalar(s5(12), s5(11), 1.0, None, add))
            step(dve.tensor_tensor(s5(13), s5(10), s5(12), mult))
            step(dve.tensor_tensor(s5(13), s5(13), s5(11), add))
            step(dve.tensor_tensor(s5(15), s5(14), s5(3), mult))
            step(dve.tensor_tensor(s5(16), lam_re, lam_re, mult))
            step(dve.tensor_tensor(s5(17), lam_im, lam_im, mult))
            step(dve.tensor_tensor(s5(16), s5(16), s5(17), add))
            step(dve.reciprocal(s5(16), s5(16)))
            for out_, a, b, op in ((18, (13, lam_re), (15, lam_im), add), (19, (15, lam_re), (13, lam_im), sub)):
                step(dve.tensor_tensor(s5(17), s5(a[0]), a[1], mult))
                step(dve.tensor_tensor(s5(10), s5(b[0]), b[1], mult))
                step(dve.tensor_tensor(s5(17), s5(17), s5(10), op))
                step(dve.tensor_tensor(s5(out_), s5(17), s5(16), mult))
            pr, pi, t = s5(12), s5(3), (s5(10), s5(11))
            for table, n in ((turn_v, 32), (turn_u, 16)):
                step(dve.memset(table[:, :, 0, 0], 1.0))
                step(dve.memset(table[:, :, 0, 1], 0.0))
                m = 1
                while m < n:
                    wide = lambda x: x.unsqueeze(2).to_broadcast([P, 24, m])
                    w = tmp[0][:, 0:24 * m].rearrange("p (s b) -> p s b", s=24)
                    cmul(table[:, :, m:2 * m, 0], table[:, :, m:2 * m, 1], table[:, :, 0:m, 0], table[:, :, 0:m, 1],
                         wide(pr), wide(pi), w)
                    cmul(t[0], t[1], pr, pi, pr, pi, s5(17))
                    step(dve.tensor_copy(pr, t[0]))
                    step(dve.tensor_copy(pi, t[1]))
                    m *= 2
            made(dve, dve.memset(s5(9), 1.0), tables_ready, 1)
            body, count = merge(B_MLRU, 3, KT, False)
            step.loop(count, 4, body)

            def queries(i):
                for r in range(4):
                    j = i * 4 + r
                    dve.wait_ge(block_done, j + (B_Q + 1))
                    made(dve, dve.tensor_copy(tile(q, j), acc[(M_OF[B_Q] + r) % 2][:]), q_ready, j + 1)
                    free_acc(0)
            step.loop(2, 0, queries)

            def largest(h, done, ready, scale):
                dve.wait_ge(done, h + 1)
                for t in (0, 2):
                    two = bank[3 * (1 - h % 2) + t // 2][:].rearrange("p (t m) -> p t m", t=2)
                    step(dve.tensor_reduce(maxima(h, t, 2), two, AX.X, vmax))
                made(dve, dve.tensor_scalar(maxima(h, 0, 4, 1), maxima(h, 0, 4), -scale, None, mult), ready, h + 1)

            def quotients(h, p, done, ready):
                dve.wait_ge(done, 4 * h + 4)
                step(dve.reciprocal(maxima(h, 0, 4, 3), maxima(h, 0, 4, 2)))
                inverse = maxima(h, 0, 4, 3).unsqueeze(2).to_broadcast([P, 4, MEM])
                made(dve, dve.tensor_tensor(p[h % 2][:], p[h % 2][:], inverse, mult), ready, h + 1)
            largest(0, sc_mm, mx_ready, 1.0 / 16)
            for h in range(4):
                quotients(h, probs, pe_ready, pn_ready)
                if h < 3:
                    largest(h + 1, sc_mm, mx_ready, 1.0 / 16)
                for m in range(2):
                    dve.wait_ge(p_tr, 2 * h + m + 1)
                    made(dve, dve.tensor_copy(probs_t[:, m], bank[5 + m][:]), pt_ready, 2 * h + m + 1)
                for d in range(2):
                    v = 2 * h + d + 1
                    dve.wait_ge(o_mm, v)
                    made(dve, dve.tensor_copy(tmp[d][:], bank[7 - 5 * d][:]), yo_in, v)
                    dve.wait_ge(yo_hi, v)
                    made(dve, dve.tensor_tensor(ym_lo[:, 2 * h + d], tmp[d][:], ym_hi[:, 2 * h + d].bitcast(f32), sub),
                         yo_done, v)

            def merge_mem(i):
                for r in range(2):
                    j, v = i * 2 + r, i * 2 + (r + 1)
                    dve.wait_ge(gate_ready, v + 2 * KT)
                    dve.wait_ge(block_done, i * 4 + (B_MMEM + 2 * r + 2))
                    step(dve.tensor_tensor(tmp[4][:], acc[(M_OF[B_MMEM] + r) % 2][:], tmp[2 + r % 2][:], mult))
                    free_acc(0)
                    made(dve, dve.tensor_tensor(tile(merged, j), tile(merged, j), tmp[4][:], add), merge_done, v + 2 * KT)
                    dve.wait_ge(mg_hi, v)
                    made(dve, dve.tensor_tensor(tile(g_lo, j), tile(merged, j), tile(g_hi, j).bitcast(f32), sub), mg_done, v)
            step.loop(4, 2, merge_mem)

            dve.wait_ge(xre_loaded, 16)

            def outs(i):
                for r in range(4):
                    j = i * 4 + r
                    dve.wait_ge(block_done, j + (B_OUT + 1))
                    made(dve, dve.tensor_tensor(tile(x1, j), acc[(M_OF[B_OUT] + r) % 2][:], tile(x1, j), add), x1_ready, j + 1)
                    free_acc(0)
            step.loop(2, 0, outs)
            dve.wait_ge(root_ready, 3)
            step(dve.reciprocal(tmp[3][:], tmp[2][:]))
            for k in range(KT):
                made(dve, dve.scalar_tensor_tensor(x1[:, k], x1[:, k], col("final_g", k), tmp[3][:], mult, mult),
                     x2_ready, k + 1)
            norm_split(3, 2 * KT, lambda k: x1[:, k], "g_norm_2", KT, h_hi, h_lo, SEQ)
            dve.wait_ge(block_done, B_FL + 1)
            step(dve.tensor_scalar(tmp[0][:], acc[M_OF[B_FL] % 2][:], col("b_forget"), -1.0, add, mult))
            free_acc(0)
            dve.sem_inc(nu_ready, 1)
            dve.wait_ge(enu_ready, 1)
            log1p_exp(tmp[0][:], tmp[1][:], tmp[5][:], (tmp[2][:], tmp[3][:], tmp[4][:]), SEQ)
            step(dve.memset(tmp[0][:], 1.0))
            made(dve, dve.tensor_tensor_scan(sum_f[:], tmp[0][:], tmp[5][:], 0.0, mult, add), f_ready, 1)

            dve.sem_inc(e_used, 2)

            dve.sem_inc(y5_sum, 1)

            def factor(j):
                dve.wait_ge(s5_loaded, j * 16 + 16)
                cm = s5m[:, 256:512].rearrange("p (s c h) -> p s c h", s=4, c=2)
                f = [sc5[:, c, bass.ds(j * 4, 4)].unsqueeze(2).to_broadcast([P, 4, 32]) for c in (18, 19)]
                w = cf_tmp[:].rearrange("p (s h) -> p s h", s=4)
                step(dve.tensor_tensor(w, cm[:, :, 1], f[1], mult))
                step(dve.tensor_tensor(cf[:, :, 0], cm[:, :, 0], f[0], mult))
                step(dve.tensor_tensor(cf[:, :, 0], cf[:, :, 0], w, sub))
                step(dve.tensor_tensor(w, cm[:, :, 1], f[0], mult))
                step(dve.tensor_tensor(cf[:, :, 1], cm[:, :, 0], f[1], mult))
                made(dve, dve.scalar_tensor_tensor(cf[:, :, 1], cf[:, :, 1], -1.0, w, mult, sub), cf_ready, j + 1)

            def s5_sum(j):
                dve.wait_ge(h_free, j * 4 + 5)
                made(dve, dve.scalar_tensor_tensor(tile(ug, j), tile(ug, j), col("s5_d", j), bank[4][:], mult, add),
                     y5_sum, j + 2)

            def gelu_argument(j):
                dve.wait_ge(y5_sq, j + 1)
                step(dve.tensor_scalar(gelu_arg[:], gelu_arg[:], 0.044715, 1.0, mult, add))
                made(dve, dve.tensor_tensor(gelu_arg[:], gelu_arg[:], tile(ug, j), mult), y5_arg, j + 1)

            def gelu(j):
                dve.wait_ge(y5_sig, j + 1)
                made(dve, dve.tensor_tensor(tile(ug, j), tile(ug, j), gelu_sig[:], mult), y5_ready, j + 1)

            def fox_s5(j, before=None):
                for r in range(4):
                    s = j * 4 + r
                    er, ei = (et[:, r % 2, c].unsqueeze(1).to_broadcast([P, 2, SEQ]) for c in range(2))
                    pq = psum[:, 2 + 3 * (r % 2):4 + 3 * (r % 2)]
                    dve.wait_ge(e_made, s + 1)
                    dve.wait_ge(pq_mm, s + 1)
                    step(dve.tensor_tensor(s5_a[:], pq, er, mult))
                    step(dve.tensor_tensor(s5_b[:], pq, ei, mult))
                    step(dve.tensor_tensor(s5_a[:, 0], s5_a[:, 0], s5_b[:, 1], add))
                    step(dve.tensor_tensor(s5_a[:, 1], s5_a[:, 1], s5_b[:, 0], sub))
                    mag = sc5[:, 14, bass.ds(s, 1)].to_broadcast([P, SEQ])
                    for c in range(2):
                        step(dve.tensor_tensor_scan(s5_b[:, c], mag, s5_a[:, c], 0.0, mult, add))
                    if r == 0:
                        if before is not None:
                            s5_sum(before)
                        factor(j)
                    elif before is not None:
                        if r == 1:
                            gelu_argument(before)
                        elif r == 2:
                            gelu(before)
                    step(dve.tensor_tensor(s5_a[:], s5_b[:], er, mult))
                    made(dve, dve.tensor_tensor(s5_b[:], s5_b[:], ei, mult), e_used, s + 3)
                    dve.wait_ge(h_free, s + 1)
                    step(dve.tensor_tensor(tmp[4][:], s5_a[:, 0], s5_b[:, 1], sub))
                    made(dve, dve.tensor_tensor(tmp[5][:], s5_a[:, 1], s5_b[:, 0], add), h_ready, s + 1)
            fox_s5(0)
            step.loop(5, 38, lambda i: fox_s5(i + 1, i))
            s5_sum(5)
            gelu_argument(5)
            gelu(5)

            for j in range(6):
                dve.wait_ge(y5h, j + 1)
                made(dve, dve.tensor_tensor(y5_lo[:, j], u5[:, j], y5_hi[:, j].bitcast(f32), sub), y5l, j + 1)
            for j in range(6):
                dve.wait_ge(acc_read, 2 + 36 + j + 1)
                t = tmp[j % 2][:]
                step(dve.tensor_tensor(t, u5[:, j], tmp[2 + j % 2][:], mult))
                made(dve, dve.tensor_tensor(t, t, gs[:, j], mult), s5_in, j + 1)
                dve.wait_ge(s5_hi, j + 1)
                made(dve, dve.tensor_tensor(s_lo[:, j], t, s_hi[:, j].bitcast(f32), sub), s5_done, j + 1)

            def fox_max(h, e):
                dve.wait_ge(fs_mm, h + 1)
                two = fbank(e, 1)[:, 2 * P:].rearrange("p (t s) -> p t s", t=2)
                for x, m in ((fbank(e, 0)[:, 3 * P:], negm[:]), (two, negm[:].unsqueeze(1).to_broadcast([P, 2, P])),
                             (fbank(e, 2)[:, P:2 * P], negm[:])):
                    step(dve.tensor_tensor(x, x, m, add))
                for t in range(4):
                    o, w = FOX_AT[t], (t + 1) * P
                    step(dve.tensor_reduce(fcol(e, t, 0), fbank(e, o // SEQ)[:, o % SEQ:o % SEQ + w], AX.X, vmax))
                made(dve, dve.tensor_scalar(fcol(e, 0, 1, 4), fcol(e, 0, 0, 4), -1.0, None, mult), fmx_ready, h + 1)

            def fox_turned(h, e):
                dve.wait_ge(fp_tr, h * 3 + 2)
                made(dve, dve.tensor_copy(f_pt[:, SEQ:2 * SEQ], fbank(e, 1)[:]), fpt_dve, h + 1)

            def fox_quotients(h, e):
                dve.wait_ge(fe_ready, h * 4 + 4)
                step(dve.reciprocal(fcol(e, 0, 3, 4), fcol(e, 0, 2, 4)))
                for t in range(4):
                    o, w = FOX_AT[t], (t + 1) * P
                    ins = dve.tensor_scalar(f_p[e][:, o:o + w], f_p[e][:, o:o + w], fcol(e, t, 3), None, mult)
                    made(dve, ins, fn_ready, h * 4 + (t + 1))

            def fox_out(j, b):
                dve.wait_ge(fo_mm, j * 2 + 6)
                made(dve, dve.tensor_tensor(tile(fg, j), acc[b][:], tile(fg, j), mult), fo_ready, j + 3)

            def fox(i, first=False):
                for n in range(4):
                    h = i * 4 + n
                    fox_max(h, n % 2)
                    if not (first and n == 0):
                        fox_turned(h - 1, (n + 1) % 2)
                    fox_quotients(h, n % 2)
                    if n == 2 or (n == 0 and not first):
                        fox_out(i * 2 + (n // 2 - 1), 1 - n // 2)
            dve.sem_inc(fo_ready, 2)
            fox(0, True)
            step.loop(2, 32, lambda i: fox(i + 1))
            fox_turned(11, 1)
            fox_out(5, 1)
            for j in range(6):
                dve.wait_ge(fh, j + 1)
                made(dve, dve.tensor_tensor(f_lo[:, j], fg[:, j], f_hi[:, j].bitcast(f32), sub), fl_done, j + 1)

            dve.wait_ge(mem2_loaded, 16)
            norm_split(4, 3 * KT, lambda k: mem2[:, k], "g_mem_norm_2", KT, m2_hi, m2_lo, MEM)
            largest(0, sc2_mm, mx2_ready, P ** -0.5)
            for h in range(4):
                quotients(h, probs2, e2_ready, n2_ready)
                if h < 3:
                    largest(h + 1, sc2_mm, mx2_ready, P ** -0.5)
                for m in range(2):
                    dve.wait_ge(p2_tr, 2 * h + m + 1)
                    made(dve, dve.tensor_copy(probs2_t[:, m], bank[5 + m][:]), p2t_ready, 2 * h + m + 1)
                dve.wait_ge(o2_mm, h + 1)
                made(dve, dve.tensor_tensor(tmp[h % 2][:], bank[7][:], gm[:, h], mult), yn_in, h + 1)
                dve.wait_ge(yn_hi_ready, h + 1)
                made(dve, dve.tensor_tensor(yn_lo[:, h], tmp[h % 2][:], yn_hi[:, h].bitcast(f32), sub), yn_done, h + 1)

            def merge2(i):
                for r in range(2):
                    for n in range(3):
                        v, a = i * 6 + (3 * r + n + 1), acc[(M_OF[B_M2] + 3 * r + n) % 2][:]
                        g = tmp[2 + (r + n) % 2][:]
                        dve.wait_ge(gate2_ready, v)
                        dve.wait_ge(block_done, i * 12 + (B_M2 + 6 * r + 2 * n + 2))
                        if n == 0:
                            made(dve, dve.tensor_tensor(tmp[4][:], a, g, mult), merge2_done, v)
                            free_acc(0)
                        else:
                            step(dve.tensor_tensor(tmp[5][:], a, g, mult))
                            free_acc(0)
                            made(dve, dve.tensor_tensor(tmp[4][:], tmp[4][:], tmp[5][:], add), merge2_done, v)
                    v = i * 2 + (r + 1)
                    dve.wait_ge(mg2_hi, v)
                    made(dve, dve.tensor_tensor(tile(g2_lo, i * 2 + r), tmp[4][:], tile(g2_hi, i * 2 + r).bitcast(f32), sub),
                         mg2_done, v)
            step.loop(4, 4, merge2)
            dve.wait_ge(x3_loaded, 16)
            for j in range(8):
                dve.wait_ge(block_done, B_OUT2 + j + 1)
                made(dve, dve.tensor_tensor(x3[:, j], acc[(M_OF[B_OUT2] + j) % 2][:], x3[:, j], add), x3_ready, j + 1)
                free_acc(0)
            dve.wait_ge(root_ready, 6)
            step(dve.reciprocal(tmp[3][:], tmp[2][:]))
            for k in range(KT):
                made(dve, dve.scalar_tensor_tensor(x3[:, k], x3[:, k], col("g_final_2", k), tmp[3][:], mult, mult),
                     fin_ready, k + 1)

        @block.tensor
        def _(pe):
            step = Steps(pe, s_pe)

            def tile(x, j):
                return x[:, bass.ds(j, 1)].rearrange("p o t -> p (o t)")

            def weights(b, off, out, hi, lo, ks, slots=None, start=True, stop=True):
                pe.wait_ge(lo_ready, off + (b + 1))
                slots = slots or range(len(ks))
                for n, (s, k) in enumerate(zip(slots, ks)):
                    whi, wlo = w_hi[:, b % SLOTS, s], w_lo[:, b % SLOTS, s]
                    pe.matmul(out, whi, hi(k), start=start and n == 0, stop=False)
                    pe.matmul(out, whi, lo(k), start=False, stop=False)
                    last = pe.matmul(out, wlo, hi(k), start=False, stop=stop and n == len(ks) - 1)
                return last

            H = (lambda k: h_hi[:, k], lambda k: h_lo[:, k])

            def sum_square(k, value, ntiles=KT, n=SEQ):
                pe.wait_ge(sq_ready, value)
                pe.matmul(p_norm[:, 0:n], ones[:], tmp[k % 2][:, 0:n], start=k == 0, stop=k == ntiles - 1
                          ).then_inc(sq_summed, 1)

            def sum_squares(sq0, ntiles, n):
                for k in range(ntiles):
                    sum_square(k, sq0 + k + 1, ntiles, n)

            def free(m, off=0):
                pe.wait_ge(acc_free, off + (m + 1))

            pe.wait_ge(consts_ready, 1)
            sum_squares(0, KT, SEQ)
            pe.wait_ge(split_lo, KT)
            free(0)
            weights(B_DT, 0, acc[0][:], *H, range(KT)).then_inc(block_done, 1)

            def simple(base, count):
                m = M_OF[base]

                def body(i):
                    for r in range(4):
                        free(m + r, i * 4)
                        weights(base + r, i * 4, acc[(m + r) % 2][:], *H, range(KT)).then_inc(block_done, 1)
                with pe.Fori(0, count) as i:
                    body(i)
            simple(B_XBC, XBC_T // 4)

            pe.wait_ge(acs_ready, 4)
            for c in range(NCH):
                pe.transpose(p_x[:, 32 * c:32 * c + 32], dt_c[:, c * CH:(c + 1) * CH], ident[0:32, 0:32])
            for c in range(NCH):
                pe.transpose(p_x[:, 128 + 32 * c:160 + 32 * c], acs[:, c * CH:(c + 1) * CH], ident[0:32, 0:32])
            for c in range(NCH):
                ins = pe.matmul(p_x[:, 256 + 32 * c:288 + 32 * c], ones[0:32, :], small[0:32, 128 + 32 * c:160 + 32 * c],
                                start=True, stop=True)
            ins.then_inc(tok_t, 1)
            pe.wait_ge(tok_exp, 1)
            pe.wait_ge(silu_done, XBC_T)
            pe.wait_ge(acc_free, M_OF[B_Z] + 2)

            def summed_decays(pair, i):
                pe.wait_ge(sel_ready, pair * 2 + 2)
                if not isinstance(pair, int) or pair:
                    pe.wait_ge(seg_ready, pair * 2)
                    pe.wait_ge(ebc_ready, pair * 2)
                for e in range(2):
                    pe.matmul(p_bc[e][:], sel[:, i, e], acs[:], start=True, stop=True).then_inc(bc_mm, 1)

            def x_turned(pair):
                pe.wait_ge(x_cur_ready, pair + 1)
                if not isinstance(pair, int) or pair:
                    pe.wait_ge(xd_ready, pair)
                for c in range(NCH):
                    ins = pe.transpose(p_x[:, c * CH:(c + 1) * CH], x_cur[:, c * CH:(c + 1) * CH], ident[:])
                ins.then_inc(x_tr, 1)

            def group_sum(g):
                pe.wait_ge(gss_ready, g + 1)
                pe.matmul(p_st[:], ones[:], gss[:], start=True, stop=True).then_inc(gsum_mm, 1)

            def group(g, first=False, last=False):
                for r in range(4):
                    pair, i = g * 4 + r, r % 2
                    weights(B_Z + r, g * 4, acc[r % 2][:], *H, range(KT)).then_inc(block_done, 1)
                    if r == 0:
                        pe.wait_ge(bcur_ready, g + 1)
                        pe.wait_ge(xd_ready, pair + 1)
                        for c in range(NCH):
                            ins = pe.transpose(p_x[:, c * CH:(c + 1) * CH], b_cur[:, c * CH:(c + 1) * CH], ident[:])
                        ins.then_inc(b_t, 1)
                        pe.wait_ge(y_ready, pair + 1)
                        for c in range(NCH):
                            ins = pe.matmul(p_off[:, c * CH:(c + 1) * CH], b_cur[:, c * CH:(c + 1) * CH],
                                            xs[:, bass.ds(g + 20, 1), c * CH:(c + 1) * CH].rearrange("p o t -> p (o t)"),
                                            start=True, stop=True)
                        ins.then_inc(cb_mm, 1)
                        summed_decays(pair + 1, 1 - i)
                        pe.wait_ge(btok_ready, g + 1)
                        x_turned(pair + 1)
                    elif not (last and r == 3):
                        x_turned(pair + 1)
                        summed_decays(pair + 1, 1 - i)
                    pe.wait_ge(xde_ready, pair + 1)
                    if r == 1 and not first:
                        pe.wait_ge(groot_ready, g)
                    for c in range(NCH - 1):
                        ins = pe.matmul(p_st[:, c * CH:(c + 1) * CH], b_tok[:, c], xde[:, c], start=True, stop=True)
                    ins.then_inc(st_mm, 1)
                    for e in range(2):
                        pe.wait_ge(g_ready, pair * 2 + (e + 1))
                        for c in range(NCH):
                            pe.matmul(p_y[64 * e:64 * e + 64, c * CH:(c + 1) * CH], xdt[i][:, c, 64 * e:64 * e + 64],
                                      seg[i][e][:, c * CH:(c + 1) * CH], start=True, stop=True)
                    pe.wait_ge(prev_ready, pair + 1)
                    for c in range(1, NCH):
                        ins = pe.matmul(p_off[:, c * CH:(c + 1) * CH], prev[:, c - 1],
                                        xs[:, bass.ds(g + 20, 1), c * CH:(c + 1) * CH].rearrange("p o t -> p (o t)"),
                                        start=True, stop=True)
                    ins.then_inc(y_mm, 1)
                    if r == 0 and not first:
                        group_sum(g - 1)
            pe.sem_inc(bc_mm, 2)
            x_turned(0)
            summed_decays(0, 0)
            group(0, first=True)
            with pe.Fori(1, 3) as g:
                group(g)
            group(3, last=True)
            group_sum(3)

            def merge(base, gate0, hi, lo, k1, k2):
                per, tiles, m = (3, 4, M_OF[base]) if k2 else (2, 2, M_OF[base])

                def body(i):
                    off = i * (tiles * per)
                    for r in range(tiles):
                        b = base + per * r
                        weights(b, off, p_gate[:], *H, range(KT)).then_inc(block_done, 1)
                        free(m + r, i * tiles)
                        if base == B_MSSD:
                            pe.wait_ge(gn_lo, 16)
                        weights(b + 1, off, acc[(m + r) % 2][:], hi, lo, range(k1), stop=not k2).then_inc(block_done, 1)
                        if k2:
                            weights(b + 2, off, acc[(m + r) % 2][:], hi, lo, range(KT, KT + k2), start=False
                                    ).then_inc(block_done, 1)
                        pe.wait_ge(gate_ready, i * tiles + (gate0 + r + 1))
                with pe.Fori(0, KT // tiles) as i:
                    body(i)
            merge(B_MSSD, 0, lambda k: y_hi[:, k], lambda k: y_lo[:, k], KT, KT)

            simple(B_LX, LRU_T // 4)

            def lru_gates(i):
                for half in range(2):
                    g = i * 2 + half
                    pe.wait_ge(xls_ready, g * 3 + 3)
                    for t in range(3):
                        b = B_LG + 6 * half + t
                        if t == 2:
                            pe.wait_ge(sig_ready, g * 3 + 1)
                        pa, px = bank[2 + (t % 2) * 2], bank[3 + (t % 2) * 2]
                        X = (lambda k: xl_hi[:, k], lambda k: xl_lo[:, k])
                        ks = LRU_KS[t]
                        weights(b, i * 12, pa[:], *X, ks, slots=ks)
                        weights(b, i * 12, px[:], *X, ks, slots=[3 + k for k in ks]).then_inc(block_done, 1)
                    for t in range(3):
                        if t == 2:
                            pe.wait_ge(lsilu_ready, g * 3 + 1)
                        elif t == 0 and not half:
                            pe.wait_ge(acc_free, M_OF[B_LX] + LRU_T + 2)
                        weights(B_LG + 6 * half + 3 + t, i * 12, acc[(half + t) % 2][:], *H, range(KT)).then_inc(block_done, 1)
            with pe.Fori(0, 2) as i:
                lru_gates(i)

            sum_squares(KT, KT, MEM)
            pe.wait_ge(split_lo, 2 * KT)
            pe.wait_ge(ly_done, LRU_T)
            MM = (lambda k: m_hi[:, k], lambda k: m_lo[:, k])

            def keys(i):
                for r in range(4):
                    free(M_OF[B_KV] + r, i * 4)
                    weights(B_KV + r, i * 4, acc[(M_OF[B_KV] + r) % 2][:, 0:MEM], *MM, range(KT)).then_inc(block_done, 1)
            with pe.Fori(0, 2) as i:
                keys(i)

            def values(i):
                for r in range(4):
                    j = i * 4 + r
                    free(M_OF[B_KV] + KT + r, i * 4)
                    weights(B_KV + KT + r, i * 4, acc[(M_OF[B_KV] + r) % 2][:, 0:MEM], *MM, range(KT)
                            ).then_inc(block_done, 1)
                    pe.wait_ge(kv_ready, j + (KT + 1))
                    for m in range(2):
                        ins = pe.transpose(bank[3 + r % 2][:, m * P:(m + 1) * P], tmp[r % 2][:, m * P:(m + 1) * P], ident[:])
                    ins.then_inc(v_tr, 1)
            with pe.Fori(0, 2) as i:
                values(i)

            merge(B_MLRU, KT, lambda k: l_hi[:, k], lambda k: l_lo[:, k], KT, 4)
            simple(B_Q, 2)

            pe.wait_ge(q_ready, KT)

            def scores(h):
                for t in range(4):
                    for k in range(2):
                        ins = pe.matmul(score(h, t), q[:, 2 * h + k, t * P:(t + 1) * P], mk[:, 2 * h + k], start=k == 0, stop=k == 1)
                ins.then_inc(sc_mm, 1)
            scores(0)
            for h in range(4):
                if h < 3:
                    scores(h + 1)
                pe.wait_ge(pn_ready, h + 1)
                for m in range(2):
                    for t in range(4):
                        ins = pe.transpose(bank[5 + m][:, t * P:(t + 1) * P], probs[h % 2][:, t, m * P:(m + 1) * P], ident[:])
                    ins.then_inc(p_tr, 1)
                pe.wait_ge(pt_ready, 2 * h + 2)
                for d in range(2):
                    for m in range(2):
                        c0 = (2 * h + d) * P
                        ins = pe.matmul(bank[7 - 5 * d][:], mv[:, m, c0:c0 + P], probs_t[:, m], start=m == 0, stop=m == 1)
                    ins.then_inc(o_mm, 1)
            pe.wait_ge(yo_done, KT)

            merge(B_MMEM, 2 * KT, lambda k: ym_hi[:, k], lambda k: ym_lo[:, k], KT, 0)
            pe.wait_ge(mg_done, KT)

            def outs(i):
                for r in range(4):
                    m = M_OF[B_OUT] + r
                    free(m, i * 4)
                    weights(B_OUT + r, i * 4, acc[m % 2][:], lambda k: g_hi[:, k], lambda k: g_lo[:, k], range(KT)
                            ).then_inc(block_done, 1)
            with pe.Fori(0, 2) as i:
                outs(i)
            sum_squares(2 * KT, KT, SEQ)
            sum_squares(3 * KT, KT, SEQ)
            pe.wait_ge(split_lo, 3 * KT)
            free(M_OF[B_FL])
            weights(B_FL, 0, acc[M_OF[B_FL] % 2][:], *H, range(KT)).then_inc(block_done, 1)
            pe.wait_ge(acc_free, M_OF[B_FL] + 3)

            def read(n):
                pe.wait_ge(acc_read, n + 1)

            def u_gs(i):
                for r in range(4):
                    read(i * 4 + r)
                    weights(B_UG + r, i * 4, acc[r % 2][:], *H, range(KT)).then_inc(block_done, 1)
            with pe.Fori(0, 3) as i:
                u_gs(i)
            pe.wait_ge(acc_read, 2 + 12)

            def inputs(j, r):
                rows = slice(32 * r, 32 * r + 32)
                for c in range(2):
                    ins = pe.matmul(bank[2 + 3 * (r % 2) + c][:], s5m[rows, c * P:(c + 1) * P],
                                    u_cur[rows, :], start=True, stop=True)
                ins.then_inc(pq_mm, 1)

            def fox_s5(j):
                for r in range(4):
                    read(j * 4 + (12 + r))
                    weights(B_FOX + r, j * 4, acc[r % 2][:], *H, range(KT)).then_inc(block_done, 1)
                    if r < 3:
                        inputs(j, r + 1)
                    else:
                        pe.wait_ge(s5_loaded, j * 16 + 32)
                        pe.wait_ge(u_cur_ready, j + 2)
                        inputs(j + 1, 0)
                        pe.wait_ge(acc_read, j * 4 + 17)
                        for k in range(NCH):
                            ins = pe.transpose(bank[7][:, k * P:(k + 1) * P], v_tmp[:, k * P:(k + 1) * P], ident[:])
                        ins.then_inc(v5_tr, 1)
                    if r == 0:
                        pe.wait_ge(cf_ready, j + 1)
                        pe.wait_ge(y5_sum, j + 1)
                    pe.wait_ge(h_ready, j * 4 + (r + 1))
                    for c in range(2):
                        ins = pe.matmul(bank[4][32 * r:32 * r + 32, :], cf[:, r, c], tmp[4 + c][:], start=c == 0, stop=c == 1)
                    ins.then_inc(h_free, 1)
                pe.wait_ge(v_evac, j + 1)
            pe.sem_inc(h_free, 1)
            pe.wait_ge(s5_loaded, 16)
            pe.wait_ge(u_cur_ready, 1)
            inputs(0, 0)
            with pe.Fori(0, 6) as j:
                fox_s5(j)
            pe.sem_inc(fo_mm, 4)
            pe.wait_ge(y5l, 6)
            for j in range(6):
                read(36 + j)
                weights(B_GLU + j, 0, acc[j % 2][:], lambda k: y5_hi[:, k], lambda k: y5_lo[:, k], range(6)
                        ).then_inc(block_done, 1)

            def fox_scores(h, j, b, e):
                pe.wait_ge(fcur_ready, j * 5 + 5)
                pe.wait_ge(frow_ready, j * 2 + 2)
                for t in range(4):
                    o, w = FOX_AT[t], (t + 1) * P
                    ins = pe.matmul(fbank(e, o // SEQ)[:, o % SEQ:o % SEQ + w], fq_cur[b][e][:, t * P:w],
                                    fk_cur[b][e][:, 0:w], start=True, stop=True)
                ins.then_inc(fs_mm, 1)

            def fox_values(h, j, b, e):
                pe.wait_ge(fn_ready, h * 4 + 4)
                for ks in ((0,), (1, 3), (2,)):
                    for k in ks:
                        for t in range(k, 4):
                            o = FOX_T_AT[k] + (t - k) * P
                            x = FOX_AT[t] + k * P
                            ins = pe.transpose(fbank(e, o // SEQ)[:, o % SEQ:o % SEQ + P], f_p[e][:, x:x + P], ident[:])
                    ins.then_inc(fp_tr, 1)
                if e == 0:
                    pe.wait_ge(fo_ready, j + 1)
                pe.wait_ge(fpt_ready, h + 1)
                pe.wait_ge(fpt_dve, h + 1)
                for k in range(4):
                    o = FOX_T_AT[k]
                    ins = pe.matmul(acc[b][64 * e:64 * e + 64, k * P:], fv_cur[b][:, k, 64 * e:64 * e + 64],
                                    f_pt[:, o:o + SEQ - k * P], start=k == 0, stop=k == 3)
                ins.then_inc(fo_mm, 1)

            def fox(i, last=False):
                for n in range(4):
                    h, j, b, e = i * 4 + n, i * 2 + n // 2, n // 2, n % 2
                    fox_values(h, j, b, e)
                    if not (last and b):
                        fox_scores(h + 2, j + 1, 1 - b, e)
            for e in range(2):
                fox_scores(e, 0, 0, e)
            with pe.Fori(0, 2) as i:
                fox(i)
            fox(2, True)

            sum_squares(4 * KT, KT, MEM)
            pe.wait_ge(split_lo, 4 * KT)
            for j in range(8):
                read(42 + j)
                weights(B_KV2 + j, 0, acc[j % 2][:, 0:MEM], lambda k: m2_hi[:, k], lambda k: m2_lo[:, k], range(KT)
                        ).then_inc(block_done, 1)
                if j >= 4:
                    pe.wait_ge(acc_read, 2 + 42 + j + 1)
                    for m in range(2):
                        ins = pe.transpose(bank[3 + j % 2][:, m * P:(m + 1) * P], tmp[j % 2][:, m * P:(m + 1) * P], ident[:])
                    ins.then_inc(v2_tr, 1)

            def q_gm(i):
                for r in range(4):
                    read(i * 4 + (50 + r))
                    weights(B_QG + r, i * 4, acc[r % 2][:], *H, range(KT)).then_inc(block_done, 1)
            with pe.Fori(0, 2) as i:
                q_gm(i)
            pe.wait_ge(acc_read, 2 + 58)
            pe.wait_ge(mv2_ready, 4)

            def scores2(h):
                for t in range(4):
                    ins = pe.matmul(score(h, t), q2[:, h, t * P:(t + 1) * P], mk2[:, h], start=True, stop=True)
                ins.then_inc(sc2_mm, 1)
            scores2(0)
            for h in range(4):
                if h < 3:
                    scores2(h + 1)
                pe.wait_ge(n2_ready, h + 1)
                for m in range(2):
                    for t in range(4):
                        ins = pe.transpose(bank[5 + m][:, t * P:(t + 1) * P], probs2[h % 2][:, t, m * P:(m + 1) * P], ident[:])
                    ins.then_inc(p2_tr, 1)
                pe.wait_ge(p2t_ready, 2 * h + 2)
                for m in range(2):
                    ins = pe.matmul(bank[7][:], mv2[:, m, h * P:(h + 1) * P], probs2_t[:, m], start=m == 0, stop=m == 1)
                ins.then_inc(o2_mm, 1)
            pe.wait_ge(yn_done, 4)

            branches = ((lambda k: f_hi[:, k], lambda k: f_lo[:, k], 6), (lambda k: s_hi[:, k], lambda k: s_lo[:, k], 6),
                        (lambda k: yn_hi[:, k], lambda k: yn_lo[:, k], 4))

            def merge2(i):
                for r in range(2):
                    for n, (hi, lo, ks) in enumerate(branches):
                        b, m = B_M2 + 6 * r + 2 * n, M_OF[B_M2] + 3 * r + n
                        weights(b, i * 12, p_gate[:], *H, range(KT)).then_inc(block_done, 1)
                        free(m, i * 6)
                        weights(b + 1, i * 12, acc[m % 2][:], hi, lo, range(ks)).then_inc(block_done, 1)
                        pe.wait_ge(gate2_ready, i * 6 + (3 * r + n + 1))
            with pe.Fori(0, 4) as i:
                merge2(i)
            pe.wait_ge(mg2_done, KT)
            for j in range(8):
                m = M_OF[B_OUT2] + j
                free(m)
                weights(B_OUT2 + j, 0, acc[m % 2][:], lambda k: g2_hi[:, k], lambda k: g2_lo[:, k], range(KT)
                        ).then_inc(block_done, 1)
                if j >= 1:
                    sum_square(j - 1, 5 * KT + j)
            sum_square(KT - 1, 6 * KT)

def _stream2(I, np):
    w_in = I["w_in_2"][0]
    o_q, o_k, o_v, o_f, o_gf, o_u, o_gs, o_qm, o_gm, o_gl = 0, 768, 1536, 2304, 2316, 3084, 3852, 4620, 5132, 5644
    cols = lambda w, c, n=P: _block(w, slice(0, DM), slice(c, c + n), np)
    halves = np.zeros((DM, P), w_in.dtype)
    halves[:, 0:12] = halves[:, 64:76] = w_in[:, o_f:o_f + 12]
    out = [cols(halves, 0)]
    for j in range(6):
        out += [cols(w_in, o_u + j * P), cols(w_in, o_gs + j * P)]
    for j in range(6):
        out += [cols(w_in, o + j * P) for o in (o_q, o_k, o_v, o_gf)]
    out += [cols(I["w_glu_2"][0], j * P) for j in range(6)]
    out += [cols(I["w_mem_kv_2"][0], j * P) for j in range(8)]
    for j in range(4):
        out += [cols(w_in, o_qm + j * P), cols(w_in, o_gm + j * P)]
    for j in range(KT):
        for n, w in enumerate(("w_proj_fox_2", "w_proj_s5_2", "w_proj_mem_2")):
            out += [cols(w_in, o_gl + n * DM + j * P), cols(I[w][0], j * P)]
    return out + [cols(I["w_out_2"][0], j * P) for j in range(KT)]


def _params2(I, np):
    b_forget = np.zeros(P, np.float32)
    b_forget[0:12] = b_forget[64:76] = I["b_forget_2"][0]
    return [_columns(I["g_norm_2"][0], np), _columns(I["g_mem_norm_2"][0], np), _columns(I["g_final_2"], np),
            _columns(I["b_merge_2"][0], np), _columns(I["lam_re_2"][0].reshape(-1), np),
            _columns(I["lam_im_2"][0].reshape(-1), np), _columns(np.repeat(I["log_step_2"][0], 64), np),
            _columns(I["s5_d_2"][0], np), _columns(I["b_glu_2"][0], np), _columns(b_forget, np)]


def _arrays2(I, np):
    s5m = np.zeros((7, P, 512), np.float32)
    for j in range(6):
        c = s5m[j, :, 256:].reshape(P, 4, 2, 32)
        for g in range(8):
            s, e = g // 2, g % 2
            for n, (b_, c_) in enumerate((("s5_b_re_2", "s5_c_re_2"), ("s5_b_im_2", "s5_c_im_2"))):
                s5m[j, 16 * g:16 * g + 16, n * P + 64 * e:n * P + 64 * e + 64] = I[b_][0, 8 * j + g].T
                c[64 * e:64 * e + 64, s, n, 16 * e:16 * e + 16] = I[c_][0, 8 * j + g].T
    return {"mem2_t": _channels_first(I["mem_2"][0], np), "s5m": s5m}


def _columns(v, np):
    v = np.asarray(v)
    if v.shape[-1] % P:
        padded = np.zeros(v.shape[:-1] + (P,), v.dtype)
        padded[..., :v.shape[-1]] = v
        v = padded
    return np.moveaxis(v.reshape(v.shape[:-1] + (-1, P)), -1, 0)


def _taps(w, np):
    return np.swapaxes(_columns(w, np), 1, 2).reshape(P, -1)


def _block(w, rows, cols, np):
    part = w[rows, cols]
    padded = np.zeros((KT * P, P), w.dtype)
    padded[:part.shape[0], :part.shape[1]] = part
    return padded.reshape(KT, P, P).transpose(1, 0, 2)


def _channels_first(x, np):
    return np.ascontiguousarray(x.T.reshape(-1, P, x.shape[0]).transpose(1, 0, 2))


def _lru_blocks(w_a, w_x, group, t, np):
    block = np.zeros((P, KT, P), w_a.dtype)
    for n, w in enumerate((w_a, w_x)):
        wide = np.zeros((3 * P, 3 * P), w.dtype)
        for b in range(4):
            wide[96 * b:96 * b + 96, 96 * b:96 * b + 96] = w[4 * group + b]
        block[:, 3 * n:3 * n + 3] = wide[:, t * P:(t + 1) * P].reshape(3, P, P).transpose(1, 0, 2)
    return block


def _stream1(I, np):
    w_in = I["w_in"][0]
    c_z, c_xbc, c_dt, c_lg, c_lx, c_q, c_g = 0, 2048, 5120, 5152, 6688, 8224, 9248
    wide = lambda w, c, n: [_block(w, slice(0, DM), slice(c + j * P, min(c + (j + 1) * P, c + n)), np)
                            for j in range((n + P - 1) // P)]
    out = wide(w_in, c_dt, 32) + wide(w_in, c_xbc, 3072) + wide(w_in, c_z, 2048)
    gates = [wide(w_in, c_g + DM * n, DM) for n in range(3)]

    def branch(n, w):
        parts = [[_block(w, slice(k, min(k + DM, w.shape[0])), slice(j * P, (j + 1) * P), np)
                  for k in range(0, w.shape[0], DM)] for j in range(KT)]
        return [b for j in range(KT) for b in [gates[n][j]] + parts[j]]
    out += branch(0, I["w_br_ssd"][0])
    out += wide(w_in, c_lx, 1536)
    lg = wide(w_in, c_lg, 1536)
    for g in range(4):
        out += [_lru_blocks(I["lru_w_a"][0], I["lru_w_x"][0], g, t, np) for t in range(3)] + lg[3 * g:3 * g + 3]
    out += wide(I["w_kv"][0], 0, 2048)
    out += branch(1, I["w_br_lru"][0])
    out += wide(w_in, c_q, DM)
    out += branch(2, I["w_br_mem"][0])
    out += wide(I["w_out"][0], 0, DM)
    return out


def _params(I, np):
    rep = np.repeat(I["ssd_d"][0], 64)
    t = [_columns(I["norm_g"][0], np), _taps(I["ssd_conv_w"][0], np), _columns(I["ssd_conv_b"][0], np), _columns(rep, np),
         _columns(I["ssd_norm_g"][0].reshape(-1), np), _taps(I["lru_conv_w"][0], np), _columns(I["lru_conv_b"][0], np),
         _columns(I["lru_b_a"][0].reshape(-1), np), _columns(I["lru_b_x"][0].reshape(-1), np),
         _columns(I["lru_lambda"][0], np), _columns(I["mem_norm_g"][0], np), _columns(I["final_g"], np),
         _columns(I["ssd_dt_bias"][0], np), _columns(I["ssd_a_log"][0], np)]
    t += _params2(I, np)
    return np.ascontiguousarray(np.concatenate(t, axis=1))


def kernel(**inputs):
    import numpy as np
    import concourse.bacc as bacc
    from concourse.bass_utils import run_bass_kernel_spmd

    I = {k: np.asarray(v) for k, v in inputs.items()}
    arrays = {
        "x_t": _channels_first(I["x"][0], np),
        "mem_t": _channels_first(I["mem"][0], np),
        "pcol": _params(I, np),
        "wstream": np.ascontiguousarray(np.stack(_stream1(I, np) + _stream2(I, np)).reshape(-1, P, KT * P)),
    }
    arrays.update(_arrays2(I, np))
    nc = bacc.Bacc("TRN2", target_bir_lowering=False, num_devices=1)
    A = {k: nc.dram_tensor(f"in_{k}", a.shape, mybir.dt.float32, kind="ExternalInput").ap() for k, a in arrays.items()}
    out = nc.dram_tensor("out", (P, KT, SEQ), mybir.dt.float32, kind="ExternalOutput").ap()
    build(nc, A, out)
    r = run_bass_kernel_spmd(nc, [{f"in_{k}": a for k, a in arrays.items()}], core_ids=[0])
    y = r.results[0]["out"]
    return np.ascontiguousarray(y.transpose(1, 0, 2).reshape(1, DM, SEQ).transpose(0, 2, 1))
```

```python
import concourse.bass as bass
from concourse import mybir
from contextlib import ExitStack

P = 128
SEQ, MEM, DM = 512, 256, 1024
KT = DM // P
CH, NCH = 128, SEQ // 128
EPS = 1e-6
SLOTS, RAW = 4, 2
SQRT_2_OVER_PI = 0.7978845608028654

XBC_T, Z_T, LRU_T, MEMKV_T = 24, 16, 12, 16
B_DT = 0
B_XBC = B_DT + 1
B_Z = B_XBC + XBC_T
B_MSSD = B_Z + Z_T
B_LX = B_MSSD + 3 * KT
B_LG = B_LX + LRU_T
B_KV = B_LG + 2 * LRU_T
B_MLRU = B_KV + MEMKV_T
B_Q = B_MLRU + 3 * KT
B_MMEM = B_Q + KT
B_OUT = B_MMEM + 2 * KT
B_END1 = B_OUT + KT

PCOLS = [("norm_g", 8), ("conv_w", 4 * 24), ("conv_b", 24), ("ssd_d", 16), ("ssd_g", 16),
         ("lconv_w", 4 * 12), ("lconv_b", 12), ("lru_b_a", 12), ("lru_b_x", 12), ("lru_lam", 12),
         ("mem_g", 8), ("final_g", 8), ("dt_bias", 1), ("a_log", 1),
         ("g_norm_2", 8), ("g_mem_norm_2", 8), ("g_final_2", 8), ("b_merge", 24), ("lam_re", 24), ("lam_im", 24),
         ("log_step", 24), ("s5_d", 6), ("b_glu", 6), ("b_forget", 1)]
PC, _n = {}, 0
for _name, _w in PCOLS:
    PC[_name] = _n
    _n += _w
NPC = _n

B_FL = B_END1
B_UG = B_FL + 1
B_FOX = B_UG + 12
B_GLU = B_FOX + 24
B_KV2 = B_GLU + 6
B_QG = B_KV2 + 8
B_M2 = B_QG + 8
B_OUT2 = B_M2 + 6 * KT
B_END = B_OUT2 + KT
LRU_KS = ((0, 1), (0, 1, 2), (1, 2))
M_OF = {B_DT: 0, B_XBC: 1, B_Z: 25, B_MSSD: 25, B_LX: 33, B_KV: 45, B_MLRU: 61, B_Q: 69, B_MMEM: 77, B_OUT: 85,
        B_FL: 93, B_M2: 94, B_OUT2: 118}
FOX_AT = (7 * P, 8 * P, 4 * P, 0)
FOX_T_AT = (0, 4 * P, 8 * P, 7 * P)
BASE, ARENA = 16512, 212800
MAGIC = 12582912.0


def build(nc, A, out):
    f32, f32r = mybir.dt.float32, mybir.dt.float32r
    ALU, ACT, AX = mybir.AluOpType, mybir.ActivationFunctionType, mybir.AxisListType
    mult, add, sub, vmin, vmax = ALU.mult, ALU.add, ALU.subtract, ALU.min, ALU.max

    ctx = ExitStack()
    with ctx:
        ctx.enter_context(nc.sbuf_tensor("arena", [P, ARENA // 4], f32))

        def at(name, shape, kb, dt=f32):
            size = 4
            for s in shape[1:]:
                size *= s
            assert kb * 1024 + size <= ARENA, (name, kb, size)
            return nc.alloc_sbuf_tensor_at(name, shape, dt, offset=BASE + int(kb * 1024))

        def sem(name):
            return ctx.enter_context(nc.semaphore(name))

        h_hi, h_lo = at("h_hi", [P, KT, SEQ], 0, f32r), at("h_lo", [P, KT, SEQ], 16, f32r)
        raw = at("raw", [P, RAW, KT * P], 32)
        w_hi, w_lo = at("w_hi", [P, SLOTS, KT, P], 40, f32r), at("w_lo", [P, SLOTS, KT, P], 56, f32r)
        pcol = at("pcol", [P, NPC], 72)
        ones = at("ones", [P, P], 74.5)
        ident = at("ident", [P, P], 75)
        tril = at("tril", [P, P], 75.5)
        negm = at("negm", [P, P], 76)
        small = at("small", [P, 512], 76.5)
        tmp = [at(f"tmp{i}", [P, SEQ], 79 + 2 * i) for i in range(6)]
        REG = 93
        xs = at("xs", [P, XBC_T, SEQ], REG)
        y_hi = at("y_hi", [P, 16, SEQ], REG, f32r)
        y_lo = at("y_lo", [P, 16, SEQ], REG + 48, f32r)
        W0 = REG + 80
        x_t = at("x_t", [P, KT, SEQ], REG + 48)
        acs = at("acs", [32, SEQ], W0)
        dt_c = at("dt_c", [32, SEQ], W0 + 2)
        b_cur = at("b_cur", [P, SEQ], W0 + 2)
        tok = at("tok", [P, 4, NCH, 32], W0 + 4)
        b_tok = at("b_tok", [P, NCH, P], W0 + 6)
        cb = at("cb", [P, NCH, P], W0 + 8)
        xdt = [at(f"xdt{i}", [P, NCH, P], W0 + 10 + 2 * i) for i in range(2)]
        xde = at("xde", [P, NCH, P], W0 + 14)
        prev = at("prev", [P, NCH - 1, P], W0 + 16)
        tmp_dt = at("tmp_dt", [32, 3, SEQ], W0 + 19.5)
        sel = at("sel", [32, 2, 2, P], W0 + 17.5)
        ebc = [at(f"ebc{i}", [P, SEQ], W0 + 19.5 + 2 * i) for i in range(2)]
        gss, gsq = at("gss", [P, SEQ], W0 + 23.5), at("gsq", [P, SEQ], W0 + 25.5)
        gn = [at(f"gn{i}", [P, SEQ], W0 + 27.5 + 2 * i) for i in range(2)]
        rinv = at("rinv", [P, SEQ], W0 + 31.5)
        x_cur, z_silu, y_tmp = at("x_cur", [P, SEQ], 79), at("z_silu", [P, SEQ], 89), at("y_tmp", [P, SEQ], 91)
        seg = [[at(f"seg{i}{e}", [P, SEQ], 81 + 4 * i + 2 * e) for e in range(2)] for i in range(2)]
        merged = at("merged", [P, KT, SEQ], REG + 80)
        xl = at("xl", [P, LRU_T, SEQ], REG)
        l_hi = at("l_hi", [P, LRU_T, SEQ], REG, f32r)
        l_lo = at("l_lo", [P, LRU_T, SEQ], REG + 24, f32r)
        xl_hi, xl_lo = at("xl_hi", [P, 3, SEQ], REG + 48, f32r), at("xl_lo", [P, 3, SEQ], REG + 54, f32r)
        l_r, l_i, l_a = (at(n, [P, 3, SEQ], REG + o) for n, o in (("l_r", 60), ("l_i", 66), ("l_a", 72)))
        l_sq = at("l_sq", [P, 3, SEQ], 79)
        l_gate, l_y = tmp[0:3], tmp[3:6]
        mem_t = at("mem_t", [P, KT, MEM], REG + 106.8125)
        mem_rms = small[:, 256:512]
        mk = at("mk", [P, KT, MEM], REG + 56)
        mv = at("mv", [P, 2, DM], REG + 64)
        m_hi, m_lo = at("m_hi", [P, KT, MEM], REG + 72, f32r), at("m_lo", [P, KT, MEM], REG + 48, f32r)
        q = at("q", [P, KT, SEQ], REG)
        ym_hi, ym_lo = at("ym_hi", [P, KT, SEQ], REG + 16, f32r), at("ym_lo", [P, KT, SEQ], REG + 32, f32r)
        probs = [at(f"probs{i}", [P, 4, MEM], REG + 72 + 4 * i) for i in range(2)]
        probs_t = at("probs_t", [P, 2, SEQ], REG + 48)
        g_hi, g_lo = at("g_hi", [P, KT, SEQ], REG + 48, f32r), at("g_lo", [P, KT, SEQ], REG + 64, f32r)
        x1 = at("x1", [P, KT, SEQ], REG + 80)

        x2_keep = nc.dram_tensor("x2_keep", (P, KT, SEQ), f32, kind="Internal").ap()
        ug = at("ug", [P, 12, SEQ], REG)
        u5, gs = ug[:, 0:6], ug[:, 6:12]
        s_lo, s_hi = at("s_lo", [P, 6, SEQ], REG, f32r), at("s_hi", [P, 6, SEQ], REG + 12, f32r)
        fq, fk = at("fq", [P, 6, SEQ], REG + 24), at("fk", [P, 6, SEQ], REG + 36)
        fv = at("fv", [P, NCH, 6 * P], REG + 48)
        fg = at("fg", [P, 6, SEQ], REG + 60)
        turn_v = at("turn_v", [P, 24, 32, 2], REG + 96)
        turn_u = at("turn_u", [P, 24, 16, 2], REG + 102)
        et = at("et", [P, 2, 2, SEQ], REG + 72)
        s5m = at("s5m", [P, 512], REG + 80)
        cf = at("cf", [P, 4, 2, 32], REG + 82)
        cf_tmp = at("cf_tmp", [P, P], REG + 93)
        v_tmp = at("v_tmp", [P, SEQ], REG + 83)
        sc5 = at("sc5", [P, 19, 24], REG + 105)
        sum_f = at("sum_f", [P, SEQ], REG + 111)
        pool_t = at("pool_t", [P, SEQ], REG + 85)
        u_cur = at("u_cur", [P, SEQ], REG + 87)
        gelu_arg, gelu_sig = at("gelu_arg", [P, SEQ], REG + 89), at("gelu_sig", [P, SEQ], REG + 91)
        s5_a, s5_b = at("s5_a", [P, 2, SEQ], 79), at("s5_b", [P, 2, SEQ], 83)
        y5_hi, y5_lo = at("y5_hi", [P, 6, SEQ], REG + 72, f32r), at("y5_lo", [P, 6, SEQ], REG + 84, f32r)
        PAIR_AT = (REG + 97, REG + 72)
        fq_cur = [[at(f"fq_cur{b}{e}", [P, SEQ], PAIR_AT[b] + 2 * e) for e in range(2)] for b in range(2)]
        fk_cur = [[at(f"fk_cur{b}{e}", [P, SEQ], PAIR_AT[b] + 4 + 2 * e) for e in range(2)] for b in range(2)]
        fv_cur = [at(f"fv_cur{b}", [P, NCH, P], PAIR_AT[b] + 8) for b in range(2)]
        f_p = [at(f"f_p{e}", [P, 1280], REG + 82 + 5 * e) for e in range(2)]
        f_pt = at("f_pt", [P, 1280], REG + 92)
        f_hi, f_lo = at("f_hi", [P, 6, SEQ], REG + 24, f32r), at("f_lo", [P, 6, SEQ], REG + 36, f32r)
        mem2 = at("mem2", [P, KT, MEM], REG + 97)
        mem2_half = at("mem2_half", [P, KT // 2, MEM], REG + 107)
        mem2_rms = small[:, 0:256]
        mk2, mv2 = at("mk2", [P, 4, MEM], REG + 48), at("mv2", [P, 2, SEQ], REG + 52)
        m2_hi, m2_lo = at("m2_hi", [P, KT, MEM], REG + 72, f32r), at("m2_lo", [P, KT, MEM], REG + 80, f32r)
        yn_hi, yn_lo = at("yn_hi", [P, 4, SEQ], REG + 56, f32r), at("yn_lo", [P, 4, SEQ], REG + 64, f32r)
        gm = at("gm", [P, 4, SEQ], REG + 72)
        q2 = at("q2", [P, 4, SEQ], REG + 80)
        probs2 = [at(f"probs2_{i}", [P, 4, MEM], REG + 88 + 4 * i) for i in range(2)]
        probs2_t = at("probs2_t", [P, 2, SEQ], REG + 96)
        g2_hi, g2_lo = at("g2_hi", [P, KT, SEQ], REG + 72, f32r), at("g2_lo", [P, KT, SEQ], REG + 88, f32r)
        x3 = at("x3", [P, KT, SEQ], REG)

        psum = ctx.enter_context(nc.psum_tensor("psum", [P, 8, SEQ], f32))
        bank = [psum[:, i] for i in range(8)]
        acc = bank[0:2]
        p_gate, p_x, p_bc, p_y, p_off, p_st = bank[2], bank[2], bank[3:5], bank[5], bank[6], bank[7]
        p_norm = bank[7]
        lg_bank = (bank[0], bank[1], bank[6])

        address_step, s_act, s_dve, s_pool = (sem(f"{n}_step") for n in ("address", "act", "dve", "pool"))
        x_loaded = [sem(f"x_loaded{i}") for i in range(4)]
        raw_ready = [sem(f"raw_ready{i}") for i in range(RAW)]
        xre_loaded = [sem(f"xre_loaded{i}") for i in range(2)]
        par_loaded, mem_loaded, out_stored = (sem(n) for n in ("par_loaded", "mem_loaded", "out_stored"))
        consts_ready, hi_ready, lo_ready, block_done, acc_free = (
            sem(n) for n in ("consts_ready", "hi_ready", "lo_ready", "block_done", "acc_free"))
        sq_ready, sq_summed, root_ready, split_in, split_hi, split_lo = (
            sem(n) for n in ("sq_ready", "sq_summed", "root_ready", "split_in", "split_hi", "split_lo"))
        u_ready, eu_ready, conv_ready, silu_done = (sem(n) for n in ("u_ready", "eu_ready", "conv_ready", "silu_done"))
        a_exp, acs_ready, tok_t, tok_sub, tok_exp = (
            sem(n) for n in ("a_exp", "acs_ready", "tok_t", "tok_sub", "tok_exp"))
        bcur_ready, b_t, btok_ready, cb_mm, cb_ready, x_cur_ready, x_tr, sel_ready, bc_mm = (
            sem(n) for n in ("bcur_ready", "b_t", "btok_ready", "cb_mm", "cb_ready", "x_cur_ready", "x_tr",
                             "sel_ready", "bc_mm"))
        xd_ready, xde_ready, seg_ready, exp_ready, g_ready, ebc_ready, st_mm, prev_ready, y_mm, z_ready, y_ready = (
            sem(n) for n in ("xd_ready", "xde_ready", "seg_ready", "exp_ready", "g_ready", "ebc_ready", "st_mm",
                             "prev_ready", "y_mm", "z_ready", "y_ready"))
        gss_ready, gsum_mm, groot_ready, gn_in, gn_hi, gn_lo = (
            sem(n) for n in ("gss_ready", "gsum_mm", "groot_ready", "gn_in", "gn_hi", "gn_lo"))
        gate_ready, merge_done = sem("gate_ready"), sem("merge_done")
        lx_done, lam_ready, xlh_ready, xls_ready, sig_ready, dec_ready, m2_ready, m_ready = (
            sem(n) for n in ("lx_done", "lam_ready", "xlh_ready", "xls_ready", "sig_ready", "dec_ready",
                             "m2_ready", "m_ready"))
        lsilu_ready, lg_free, ly_in, ly_hi, ly_done = (sem(n) for n in ("lsilu_ready", "lg_free", "ly_in", "ly_hi", "ly_done"))
        kv_ready, v_tr = sem("kv_ready"), sem("v_tr")
        q_ready, sc_mm, mx_ready, pe_ready, pn_ready, p_tr, pt_ready, o_mm, yo_in, yo_hi, yo_done = (
            sem(n) for n in ("q_ready", "sc_mm", "mx_ready", "pe_ready", "pn_ready", "p_tr", "pt_ready", "o_mm",
                             "yo_in", "yo_hi", "yo_done"))
        mg_hi, mg_done, x1_ready = sem("mg_hi"), sem("mg_done"), sem("x1_ready")
        x2_ready, var_ready, x2_kept, nu_ready, enu_ready, f_ready = (
            sem(n) for n in ("x2_ready", "var_ready", "x2_kept", "nu_ready", "enu_ready", "f_ready"))
        acc_read, step_ready, t_exp, tables_ready = (
            sem(n) for n in ("acc_read", "step_ready", "t_exp", "tables_ready"))
        s5_loaded, u_cur_ready, fval_ready, pool_address_step = (
            sem(n) for n in ("s5_loaded", "u_cur_ready", "fval_ready", "pool_address_step"))
        e_made, e_used, pq_mm, h_ready, h_free, cf_ready, y5_sq, y5_arg, y5_sig, y5_sum, y5_ready, v_evac, v5_tr = (
            sem(n) for n in ("e_made", "e_used", "pq_mm", "h_ready", "h_free", "cf_ready", "y5_sq", "y5_arg", "y5_sig",
                             "y5_sum", "y5_ready", "v_evac", "v5_tr"))
        y5h, y5l, s5_in, s5_hi, s5_done = (
            sem(n) for n in ("y5h", "y5l", "s5_in", "s5_hi", "s5_done"))
        fz_ready, fcur_ready, fs_mm, fmx_ready, fe_ready, fn_ready, fp_tr, fpt_ready, fo_mm, fo_ready = (
            sem(n) for n in ("fz_ready", "fcur_ready", "fs_mm", "fmx_ready", "fe_ready", "fn_ready",
                             "fp_tr", "fpt_ready", "fo_mm", "fo_ready"))
        fh, frow_ready, fl_done, mem2_loaded, v2_tr, mv2_ready = (
            sem(n) for n in ("fh", "frow_ready", "fl_done", "mem2_loaded", "v2_tr", "mv2_ready"))
        sc2_mm, mx2_ready, e2_ready, n2_ready, p2_tr, p2t_ready, o2_mm, yn_in, yn_hi_ready, yn_done = (
            sem(n) for n in ("sc2_mm", "mx2_ready", "e2_ready", "n2_ready", "p2_tr", "p2t_ready", "o2_mm", "yn_in",
                             "yn_hi_ready", "yn_done"))
        gate2_ready, merge2_done, mg2_hi, mg2_done, x3_loaded, x3_ready, fin_ready = (
            sem(n) for n in ("gate2_ready", "merge2_done", "mg2_hi", "mg2_done", "x3_loaded", "x3_ready", "fin_ready"))

        class Steps:

            def __init__(self, eng, own):
                self.eng, self.own, self.n, self.turn = eng, own, 0, 0

            def __call__(self, ins):
                ins.then_inc(self.own, 1)
                self.n += 1
                self.eng.wait_ge(self.own, self.turn + self.n)

            def loop(self, count, steps, body):
                first = self.n
                with self.eng.Fori(0, count) as i:
                    self.turn = i * steps
                    body(i)
                assert self.n - first == steps, f"{self.own}: {self.n - first} steps in a turn, not {steps}"
                self.turn, self.n = 0, first + count * steps

        def made(eng, ins, what, value):
            ins.then_inc(what, 1)
            eng.wait_ge(what, value)

        def col(name, j=0, rows=P):
            return pcol[0:rows, bass.ds(j + PC[name], 1)]

        def cols(name, n):
            return pcol[:, PC[name]:PC[name] + n]

        def score(h, t):
            return bank[3 * (1 - h % 2) + t // 2][:, (t % 2) * MEM:(t % 2 + 1) * MEM]

        def maxima(h, t, n=1, what=0):
            return scol(96 + 16 * (h % 2) + 4 * what + t, n)

        def fbank(e, n):
            return bank[2 + 3 * e + n]

        def fcol(e, t, what, n=1):
            return scol(300 + 16 * e + 4 * what + t, n)

        def scol(j, n=1, rows=P):
            return small[0:rows, j:j + n]

        block = ctx.enter_context(nc.Block())

        @block.sync
        def _(sp):
            for n in range(2):
                sp.dma_start(x_t[:, 2 * n:2 * n + 2], A["x_t"][:, 2 * n:2 * n + 2]).then_inc(x_loaded[n], 16)
            sp.dma_start(pcol[:], A["pcol"]).then_inc(par_loaded, 16)
            for b in range(RAW):
                sp.dma_start(raw[:, b], A["wstream"][b]).then_inc(raw_ready[b], 16)

            with sp.Fori(0, (B_END - RAW) // RAW) as i:
                for r in range(RAW):
                    sp.wait_ge(lo_ready, i * RAW + (r + 1))
                    sp.dma_start(raw[:, r], A["wstream"][bass.ds(i * RAW + (RAW + r), 1)].rearrange("o p c -> (o p) c")
                                 ).then_inc(raw_ready[r], 16)
            for b in range(B_END - (B_END - RAW) % RAW, B_END):
                sp.wait_ge(lo_ready, b - RAW + 1)
                sp.dma_start(raw[:, b % RAW], A["wstream"][b]).then_inc(raw_ready[b % RAW], 16)
            sp.wait_ge(out_stored, 16 * KT)

        @block.gpsimd
        def _(pool):
            step = Steps(pool, s_pool)
            step(pool.memset(ones[:], 1.0))
            step(pool.memset(negm[:], 0.0))
            step(pool.affine_select(out=ident[:], in_=ones[:], compare_op=ALU.is_equal, fill=0.0, base=0,
                                    pattern=[[-1, P]], channel_multiplier=1))
            step(pool.affine_select(out=tril[:], in_=ones[:], compare_op=ALU.is_ge, fill=0.0, base=0,
                                    pattern=[[1, P]], channel_multiplier=-1))
            made(pool, pool.affine_select(out=negm[:], in_=negm[:], compare_op=ALU.is_ge, fill=-1e30, base=0,
                                          pattern=[[-1, P]], channel_multiplier=1), consts_ready, 1)

            def lower_parts(first, off, count):
                for b in range(first, first + count):
                    pool.wait_ge(hi_ready, off + (b + 1))
                    made(pool, pool.tensor_tensor(w_lo[:, b % SLOTS].rearrange("p k c -> p (k c)"), raw[:, b % RAW],
                                                  w_hi[:, b % SLOTS].rearrange("p k c -> p (k c)").bitcast(f32), sub),
                         lo_ready, off + (b + 1))
            
            def blocks(first, end):
                up = min(-(-first // SLOTS) * SLOTS, end)
                for b in range(first, up):
                    lower_parts(b, 0, 1)
                if end // SLOTS > up // SLOTS:
                    with pool.Fori(up // SLOTS, end // SLOTS) as i:
                        lower_parts(0, i * SLOTS, SLOTS)
                    up = end // SLOTS * SLOTS
                for b in range(up, end):
                    lower_parts(b, 0, 1)
            blocks(0, B_Z + SLOTS)

            def select(pair, i):
                if not isinstance(pair, int) or pair:
                    pool.wait_ge(bc_mm, pair * 2)
                for e in range(2):
                    pool.sem_inc(pool_address_step, 1)
                    made(pool, pool.tensor_copy(sel[:, i, e], ident[0:32, bass.ds(pair * 2 + e, 1)].to_broadcast([32, P])),
                         sel_ready, pair * 2 + (e + 1))

            def to_end(pair, i):
                pool.wait_ge(xd_ready, pair + 1)
                if not isinstance(pair, int) or pair:
                    pool.wait_ge(st_mm, pair)
                w4 = lambda a: a.rearrange("p c (e d) -> p c e d", e=2)
                decay = tok[:, 2, :, bass.ds(pair * 2, 2)].unsqueeze(3).to_broadcast([P, NCH, 2, 64])
                pool.sem_inc(pool_address_step, 1)
                made(pool, pool.tensor_tensor(w4(xde[:]), w4(xdt[i][:]), decay, mult), xde_ready, pair + 1)

            def tile_p(x, j):
                return x[:, bass.ds(j, 1)].rearrange("p o t -> p (o t)")

            def squared(g, r):
                y = tile_p(xs, g * 4 + r)
                pool.wait_ge(y_ready, g * 4 + (r + 2))
                pool.sem_inc(pool_address_step, 1)
                if r == 0:
                    step(pool.tensor_tensor(gss[:], y, y, mult))
                    return
                step(pool.tensor_tensor(gsq[:], y, y, mult))
                ins = pool.tensor_tensor(gss[:], gss[:], gsq[:], add)
                step(ins) if r < 3 else made(pool, ins, gss_ready, g + 1)

            def group_lower(g, tiles):
                for t in tiles:
                    v = g * 4 + (t + 1)
                    pool.wait_ge(gn_hi, v)
                    pool.sem_inc(pool_address_step, 1)
                    made(pool, pool.tensor_tensor(tile_p(y_lo, g * 4 + t), gn[t % 2][:], tile_p(y_hi, g * 4 + t).bitcast(f32),
                                                  sub), gn_lo, v)

            def group(g, first=False, last=False):
                for r in range(4):
                    pair = g * 4 + r
                    lower_parts(B_Z + r + SLOTS, g * 4, 1)
                    if not (last and r == 3):
                        to_end(pair + 1, (r + 1) % 2)
                    if not (last and r >= 2):
                        select(pair + 2, r % 2)
                    if not first and r in (1, 2):
                        group_lower(g - 1, (0, 1) if r == 1 else (2, 3))
                    if r == 0 and not first:
                        pool.wait_ge(gsum_mm, g)
                    squared(g, r)
            pool.wait_ge(tok_exp, 1)
            select(0, 0)
            select(1, 1)
            to_end(0, 0)
            group(0, first=True)
            step.loop(2, 6, lambda i: group(i + 1))
            group(3, last=True)
            group_lower(3, range(4))
            blocks(B_Z + Z_T + SLOTS, B_FOX)
            pool.wait_ge(tables_ready, 1)
            pool.wait_ge(x2_kept, 16)

            def powers(j):
                for r in range(4):
                    lower_parts(B_FOX + r, j * 4, 1)
                    s, e = j * 4 + r, et[:, r % 2]
                    pool.wait_ge(e_used, s + 1)

                    def u(c):
                        return turn_u[:, bass.ds(s, 1), :, c].rearrange("p o a -> p (o a)").unsqueeze(2).to_broadcast([P, 16, 32])

                    def v(c):
                        return turn_v[:, bass.ds(s, 1), :, c].to_broadcast([P, 16, 32])
                    w = [x.rearrange("p (a b) -> p a b", a=16) for x in (e[:, 0], e[:, 1], pool_t[:])]

                    def product(out, a, b):
                        pool.sem_inc(pool_address_step, 1)
                        step(pool.tensor_tensor(out, a, b, mult))
                    product(w[0], u(0), v(0))
                    product(w[2], u(1), v(1))
                    step(pool.tensor_tensor(e[:, 0], e[:, 0], pool_t[:], sub))
                    product(w[1], u(0), v(1))
                    product(w[2], u(1), v(0))
                    made(pool, pool.tensor_tensor(e[:, 1], e[:, 1], pool_t[:], add), e_made, s + 1)
            step.loop(6, 20, powers)
            def forget(b):
                for e in range(2):
                    other = slice(64 - 64 * e, 128 - 64 * e)
                    made(pool, pool.tensor_copy(fk_cur[b][e][other], sum_f[other]), fz_ready, 2 * b + e + 1)

            def rows(i, b):
                j = i * 2 + b
                if not isinstance(i, int):
                    pool.wait_ge(fs_mm, j * 2 - 2)
                for e in range(2):
                    other = slice(64 - 64 * e, 128 - 64 * e)
                    pool.sem_inc(pool_address_step, 1)
                    made(pool, pool.tensor_copy(fq_cur[b][e][other],
                                                ident[other, bass.ds(j * 2 + (64 * (1 - e) + e), 1)].to_broadcast([64, SEQ])),
                         frow_ready, j * 2 + (e + 1))
            blocks(B_FOX + 24, B_GLU + SLOTS)
            pool.wait_ge(y5_ready, 6)
            pool.wait_ge(f_ready, 1)
            forget(0)
            rows(0, 0)
            blocks(B_GLU + SLOTS, B_KV2 + SLOTS)
            pool.wait_ge(block_done, B_GLU + 6)
            forget(1)
            rows(0, 1)

            def pairs(i):
                for b in range(2):
                    rows(i + 1, b)
            with pool.Fori(0, 2) as i:
                pairs(i)
            blocks(B_KV2 + SLOTS, B_END)

        @block.scalar
        def _(act):
            step = Steps(act, s_act)

            def activate(out, *args, **more):
                act.sem_inc(address_step, 1)
                return act.activation(out, *args, **more)

            def upper(b, off):
                act.wait_ge(raw_ready[b % RAW], off * 8 + 16 * (b // RAW + 1))
                made(act, act.activation(w_hi[:, b % SLOTS].rearrange("p k c -> p (k c)"), raw[:, b % RAW], ACT.Copy),
                     hi_ready, off + (b + 1))

            def turn(b, off, more=True):
                act.wait_ge(block_done, off + (b + 1))
                if more:
                    upper(b + SLOTS, off)

            def squares(k, x, value, scratch=tmp):
                if k >= 2:
                    act.wait_ge(sq_summed, value - 2)
                made(act, act.activation(scratch[k % 2][:, 0:x.shape[1]], x, ACT.Square), sq_ready, value)

            def split(n0, ntiles, hi):
                for k in range(ntiles):
                    act.wait_ge(split_in, n0 + k + 1)
                    made(act, act.activation(hi[:, k], tmp[k % 2][:, 0:hi.shape[2]], ACT.Copy), split_hi, n0 + k + 1)

            for n in range(2, 4):
                act.dma_start(x_t[:, 2 * n:2 * n + 2], A["x_t"][:, 2 * n:2 * n + 2]).then_inc(x_loaded[n], 16)
            for k in range(KT):
                act.wait_ge(x_loaded[k // 2], 16)
                squares(k, x_t[:, k], k + 1)
                if k == 3:
                    for b in range(RAW):
                        upper(b, 0)
            act.wait_ge(sq_summed, KT)
            made(act, act.activation(tmp[2][:], p_norm[:], ACT.Sqrt, scale=1.0 / DM, bias=EPS), root_ready, 1)
            for b in range(RAW, SLOTS):
                upper(b, 0)
            split(0, KT, h_hi)

            turn(B_DT, 0)
            act.wait_ge(u_ready, 1)
            step(act.activation(tmp[1][0:32], tmp[0][0:32], ACT.Abs))
            made(act, act.activation(tmp[1][0:32], tmp[1][0:32], ACT.Exp, scale=-1.0), eu_ready, 1)
            made(act, act.activation(scol(0, 1, 32), col("a_log", 0, 32), ACT.Exp), a_exp, 1)

            def xbc(i):
                for r in range(4):
                    turn(B_XBC + r, i * 4)
                    act.wait_ge(conv_ready, i * 4 + (r + 1))
                    made(act, activate(xs[:, bass.ds(i * 4 + r, 1)].rearrange("p o t -> p (o t)"), tmp[2 + r % 2][:],
                                       ACT.Silu), silu_done, i * 4 + (r + 1))
            step.loop(XBC_T // 4, 0, xbc)

            act.wait_ge(tok_sub, 1)
            step(act.activation(tok[:, 2], tok[:, 2], ACT.Exp))
            made(act, act.activation(tok[:, 3].rearrange("p c h -> p (c h)"), p_x[:, 256:384], ACT.Exp), tok_exp, 1)

            def x_copy(pair):
                act.wait_ge(x_tr, pair) if not isinstance(pair, int) or pair else None
                made(act, activate(x_cur[:], xs[:, bass.ds(pair, 1)].rearrange("p o t -> p (o t)"), ACT.Copy),
                     x_cur_ready, pair + 1)

            def decays(pair, i):
                for e in range(2):
                    v = pair * 2 + (e + 1)
                    act.wait_ge(seg_ready, v)
                    made(act, act.activation(ebc[i][64 * e:64 * e + 64], p_bc[e][64 * e:64 * e + 64, :], ACT.Exp), ebc_ready, v)
                    made(act, act.activation(seg[i][e][:], seg[i][e][:], ACT.Exp), exp_ready, v)

            def group_root(g):
                act.wait_ge(gsum_mm, g + 1)
                made(act, act.activation(rinv[:], p_st[:], ACT.Sqrt, scale=1.0 / 512, bias=EPS), groot_ready, g + 1)

            def group_upper(g, tiles):
                for t in tiles:
                    v = g * 4 + (t + 1)
                    act.wait_ge(gn_in, v)
                    made(act, activate(y_hi[:, bass.ds(g * 4 + t, 1)].rearrange("p o t -> p (o t)"), gn[t % 2][:], ACT.Copy),
                         gn_hi, v)

            def group(g, first=False, last=False):
                made(act, activate(b_cur[:], xs[:, bass.ds(g + 16, 1)].rearrange("p o t -> p (o t)"), ACT.Copy), bcur_ready, g + 1)
                for r in range(4):
                    pair = g * 4 + r
                    if r == 1 and not first:
                        group_root(g - 1)
                    if not (last and r == 3):
                        x_copy(pair + 1)
                    turn(B_Z + r, g * 4)
                    act.wait_ge(y_ready, pair + 1)
                    made(act, act.activation(z_silu[:], acc[r % 2][:], ACT.Silu), z_ready, pair + 1)
                    if r == 0:
                        act.wait_ge(b_t, g + 1)
                        made(act, act.activation(b_tok[:].rearrange("p c n -> p (c n)"), p_x[:], ACT.Copy), btok_ready, g + 1)
                    if not (last and r == 3):
                        decays(pair + 1, (r + 1) % 2)
                    if not first and r in (1, 2):
                        group_upper(g - 1, (0, 1) if r == 1 else (2, 3))
            x_copy(0)
            decays(0, 0)
            group(0, first=True)
            step.loop(2, 0, lambda i: group(i + 1))
            group(3, last=True)
            group_root(3)
            group_upper(3, range(4))

            def merge(base, per, gate0):
                tiles = 4 if per == 3 else 2

                def body(i, beside=None):
                    for r in range(tiles):
                        if beside:
                            beside(i * tiles + r)
                        for x in range(per):
                            turn(base + per * r + x, i * (tiles * per))
                            if x == 0:
                                v = i * tiles + (gate0 + r + 1)
                                made(act, act.activation(tmp[2 + r % 2][:], p_gate[:], ACT.Sigmoid), gate_ready, v)
                        act.wait_ge(merge_done, v)
                return body, KT // tiles

            def s5_constants(j):
                if j == 0:
                    step(act.activation(scol(40, 12), cols("lru_lam", LRU_T), ACT.Abs))
                    made(act, act.activation(scol(52, 12), scol(40, 12), ACT.Exp, scale=-1.0), lam_ready, 1)
                if j != 1:
                    return
                act.wait_ge(step_ready, 1)
                step(act.activation(sc5[:, 3], sc5[:, 1], ACT.Sin))
                step(act.activation(sc5[:, 4], sc5[:, 1], ACT.Sin, scale=0.5))
                step(act.activation(sc5[:, 5], sc5[:, 2], ACT.Tanh, scale=0.5))
                step(act.activation(sc5[:, 7], sc5[:, 6], ACT.Exp))
                made(act, act.activation(sc5[:, 8], ones[:, 0:24], ACT.Exp), t_exp, 1)
            body, count = merge(B_MSSD, 3, 0)
            body(0, s5_constants)
            body(1)

            def split_xl(g):
                for t in range(3):
                    act.wait_ge(lx_done, g * 3 + (t + 1))
                    made(act, activate(xl_hi[:, t], xl[:, bass.ds(g * 3 + t, 1)].rearrange("p o t -> p (o t)"), ACT.Copy),
                         xlh_ready, g * 3 + (t + 1))

            act.wait_ge(gn_lo, 16)
            act.dma_start(mem_t[:], A["mem_t"]).then_inc(mem_loaded, 16)
            act.wait_ge(mem_loaded, 16)
            for j in range(LRU_T):
                turn(B_LX + j, 0)
                if j < KT:
                    squares(j, mem_t[:, j], KT + j + 1)
                elif j == KT:
                    split_xl(0)
            act.wait_ge(sq_summed, 2 * KT)
            made(act, act.activation(mem_rms, p_norm[:, 0:MEM], ACT.Sqrt, scale=1.0 / DM, bias=EPS), root_ready, 2)
            act.wait_ge(lam_ready, 2)

            def lru_gates(g):
                for t in range(3):
                    turn(B_LG + 6 * g + t, 0)
                    step(activate(l_r[:, t], bank[2 + (t % 2) * 2][:], ACT.Sigmoid, bias=col("lru_b_a", g * 3 + t)))
                    made(act, activate(l_i[:, t], bank[3 + (t % 2) * 2][:], ACT.Sigmoid,
                                             bias=col("lru_b_x", g * 3 + t)), sig_ready, g * 3 + (t + 1))
                if g < 3:
                    split_xl(g + 1)
                for t in range(3):
                    step(activate(l_a[:, t], l_r[:, t], ACT.Exp, scale=small[:, bass.ds(g * 3 + (t + 64), 1)]))
                    step(activate(l_r[:, t], l_r[:, t], ACT.Tanh, scale=small[:, bass.ds(g * 3 + (t + 76), 1)]))
                made(act, act.activation(l_sq[:], l_a[:], ACT.Square), dec_ready, g + 1)
                act.wait_ge(m2_ready, g + 1)
                made(act, act.activation(l_r[:].rearrange("p t n -> p (t n)"), l_r[:].rearrange("p t n -> p (t n)"),
                                         ACT.Sqrt), m_ready, g + 1)
                for t in range(3):
                    turn(B_LG + 6 * g + 3 + t, 0)
                    v = g * 3 + (t + 1)
                    made(act, act.activation(l_gate[t][:], lg_bank[t][:], ACT.Sigmoid), lsilu_ready, v)
                for t in range(3):
                    v = g * 3 + (t + 1)
                    act.wait_ge(ly_in, v)
                    made(act, activate(l_hi[:, bass.ds(g * 3 + t, 1)].rearrange("p o t -> p (o t)"),
                                             l_y[t][:], ACT.Copy), ly_hi, v)
            for g in range(4):
                lru_gates(g)

            split(KT, KT, m_hi)

            def kv(i):
                for r in range(4):
                    turn(B_KV + r, i * 4)
            step.loop(MEMKV_T // 4, 0, kv)
            body, count = merge(B_MLRU, 3, KT)
            step.loop(count, 0, body)

            def queries(i):
                for r in range(4):
                    turn(B_Q + r, i * 4)
            step.loop(2, 0, queries)

            def exponentials(h):
                act.wait_ge(mx_ready, h + 1)
                if h >= 2:
                    act.wait_ge(p_tr, 2 * h - 2)
                for t in range(4):
                    ins = act.activation(probs[h % 2][:, t], score(h, t), ACT.Exp, scale=1.0 / 16, bias=maxima(h, t, what=1),
                                         accum_out=maxima(h, t, what=2))
                    made(act, ins, pe_ready, 4 * h + t + 1)
            exponentials(0)
            for h in range(4):
                if h < 3:
                    exponentials(h + 1)
                for d in range(2):
                    v = 2 * h + d + 1
                    act.wait_ge(yo_in, v)
                    made(act, act.activation(ym_hi[:, 2 * h + d], tmp[d][:], ACT.Copy), yo_hi, v)

            def merge_mem(i):
                for r in range(2):
                    turn(B_MMEM + 2 * r, i * 4)
                    v = i * 2 + (r + 1)
                    made(act, act.activation(tmp[2 + r % 2][:], p_gate[:], ACT.Sigmoid), gate_ready, v + 2 * KT)
                    turn(B_MMEM + 2 * r + 1, i * 4)
                    act.wait_ge(merge_done, v + 2 * KT)
                    made(act, activate(g_hi[:, bass.ds(i * 2 + r, 1)].rearrange("p o t -> p (o t)"),
                                             merged[:, bass.ds(i * 2 + r, 1)].rearrange("p o t -> p (o t)"), ACT.Copy),
                         mg_hi, v)
            step.loop(4, 0, merge_mem)
            act.wait_ge(mg_done, KT)
            for n in range(2):
                act.dma_start(x1[:, 4 * n:4 * n + 4], A["x_t"][:, 4 * n:4 * n + 4]).then_inc(xre_loaded[n], 16)

            for j in range(KT):
                turn(B_OUT + j, 0)
                act.wait_ge(x1_ready, j + 1)
                if j >= 2:
                    act.wait_ge(sq_summed, 2 * KT + 2 * (j - 1))
                made(act, act.activation(tmp[j % 2][:], x1[:, j], ACT.Square), sq_ready, 2 * KT + 2 * j + 1)
                made(act, act.activation(tmp[4 + j % 2][:], x1[:, j], ACT.Square, scale=col("final_g", j)), sq_ready,
                     2 * KT + 2 * j + 2)
            
            act.wait_ge(var_ready, 1)
            made(act, act.activation(tmp[5][:], tmp[4][:], ACT.Sqrt), root_ready, 3)
            made(act, act.activation(tmp[2][:], p_norm[:], ACT.Sqrt, scale=1.0 / DM, bias=EPS), root_ready, 4)
            split(2 * KT, KT, h_hi)

            act.sem_inc(acc_read, 2)
            turn(B_FL, 0)
            act.wait_ge(nu_ready, 1)
            step(act.activation(tmp[1][:], tmp[0][:], ACT.Abs))
            made(act, act.activation(tmp[1][:], tmp[1][:], ACT.Exp, scale=-1.0), enu_ready, 1)
            act.wait_ge(x2_ready, KT)
            act.dma_start(x2_keep, x1[:]).then_inc(x2_kept, 16)

            def tile(x, j):
                return x[:, bass.ds(j, 1)].rearrange("p o t -> p (o t)")

            def read(out, *args, n, **more):
                made(act, activate(out, *args, **more), acc_read, n + 3)

            def u_gs(i):
                for r in range(4):
                    turn(B_UG + r, i * 4)
                    j, n = i * 2 + r // 2, i * 4 + r
                    read(tile(ug, j + 6 * (r % 2)), acc[r % 2][:], ACT.Silu if r % 2 else ACT.Copy, n=n)
            u_gs(0)
            act.wait_ge(x2_kept, 16)
            act.dma_start(s5m[:], A["s5m"][0]).then_inc(s5_loaded, 16)

            made(act, act.activation(u_cur[:], u5[:, 0], ACT.Copy), u_cur_ready, 1)
            step.loop(2, 0, lambda i: u_gs(i + 1))

            def gelu_square(j):
                act.wait_ge(y5_sum, j + 2)
                made(act, activate(gelu_arg[:], tile(ug, j), ACT.Square), y5_sq, j + 1)

            def gelu_sigmoid(j):
                act.wait_ge(y5_arg, j + 1)
                made(act, act.activation(gelu_sig[:], gelu_arg[:], ACT.Sigmoid, scale=2 * SQRT_2_OVER_PI), y5_sig, j + 1)

            def fox_s5(j, before=None):
                for r in range(4):
                    turn(B_FOX + r, j * 4)
                    n = j * 4 + (12 + r)
                    if r == 0:
                        read(tile(fq, j), acc[0][:], ACT.Copy, n=n, scale=0.125)
                        if before is not None:
                            gelu_square(before)
                    elif r == 1:
                        read(tile(fk, j), acc[1][:], ACT.Copy, n=n)
                        if before is not None:
                            gelu_sigmoid(before)
                    elif r == 2:
                        read(v_tmp[:], acc[0][:], ACT.Copy, n=n)
                        act.wait_ge(pq_mm, j * 4 + 4)
                        act.wait_ge(cf_ready, j + 1)
                        act.dma_start(s5m[:], A["s5m"][bass.ds(j + 1, 1)].rearrange("o p c -> (o p) c")).then_inc(s5_loaded, 16)
                        made(act, activate(u_cur[:], tile(ug, j + 1), ACT.Copy), u_cur_ready, j + 2)
                    else:
                        read(tile(fg, j), acc[1][:], ACT.Silu, n=n)
                act.wait_ge(v5_tr, j + 1)
                made(act, activate(fv[:, :, bass.ds(j * P, P)], bank[7][:].rearrange("p (k d) -> p k d", k=NCH), ACT.Copy),
                     v_evac, j + 1)
            fox_s5(0)
            step.loop(5, 0, lambda i: fox_s5(i + 1, i))
            gelu_square(5)
            gelu_sigmoid(5)

            act.wait_ge(s5_loaded, 16 * 7)
            for j in range(6):
                act.wait_ge(y5_ready, 6)
                made(act, act.activation(y5_hi[:, j], u5[:, j], ACT.Copy), y5h, j + 1)
            act.wait_ge(y5_ready, 6) 
            act.dma_start(mem2_half[:], A["mem2_t"][:, 0:KT // 2]).then_inc(mem2_loaded, 16)
            for j in range(6):
                turn(B_GLU + j, 0)
                made(act, act.activation(tmp[2 + j % 2][:], acc[j % 2][:], ACT.Sigmoid, bias=col("b_glu", j)), acc_read,
                     2 + 36 + j + 1)
                act.wait_ge(s5_in, j + 1)
                made(act, act.activation(s_hi[:, j], tmp[j % 2][:], ACT.Copy), s5_hi, j + 1)
                if j in (1, 2, 4, 5):
                    if j in (1, 4):
                        act.wait_ge(mem2_loaded, 16 if j == 1 else 32)
                    for k in ((0, 1), (2, 3), (4, 5), (6, 7))[(1, 2, 4, 5).index(j)]:
                        squares(k, mem2_half[:, k % 4], 4 * KT + k + 1, tmp[4:6])
                    if j == 2:
                        act.dma_start(mem2_half[:], A["mem2_t"][:, KT // 2:]).then_inc(mem2_loaded, 16)
            act.wait_ge(sq_summed, 5 * KT)
            made(act, act.activation(mem2_rms, p_norm[:, 0:MEM], ACT.Sqrt, scale=1.0 / DM, bias=EPS), root_ready, 5)

            def fox_turned(h, e):
                act.wait_ge(fp_tr, h * 3 + 1)
                step(act.activation(f_pt[:, 0:SEQ], fbank(e, 0)[:], ACT.Copy))
                act.wait_ge(fp_tr, h * 3 + 2)
                step(act.activation(f_pt[:, SEQ:2 * SEQ], fbank(e, 1)[:], ACT.Copy))
                act.wait_ge(fp_tr, h * 3 + 3)
                made(act, act.activation(f_pt[:, 2 * SEQ:], fbank(e, 2)[:, 0:2 * P], ACT.Copy), fpt_ready, h + 1)

            def fox_exp(h, e):
                act.wait_ge(fmx_ready, h + 1)
                for t in range(4):
                    o, w = FOX_AT[t], (t + 1) * P
                    ins = act.activation(f_p[e][:, o:o + w], fbank(e, o // SEQ)[:, o % SEQ:o % SEQ + w], ACT.Exp,
                                         bias=fcol(e, t, 1), accum_out=fcol(e, t, 2))
                    made(act, ins, fe_ready, h * 4 + (t + 1))

            def fox_queries(j):
                b = j % 2
                if j >= 2:
                    act.wait_ge(fs_mm, j * 2 - 2)
                copies = [(x[hs], y[hs, j]) for e in range(2) for hs in (slice(64 * e, 64 * e + 64),)
                          for x, y in ((fq_cur[b][e], fq), (fk_cur[b][e], fk))]
                for n, (out_, x) in enumerate(copies):
                    made(act, act.activation(out_, x, ACT.Copy), fcur_ready, j * 4 + (n + 1))

            fox_queries(0)
            act.wait_ge(block_done, B_GLU + 6)
            fox_queries(1)
            for h in range(12):
                if h:
                    fox_turned(h - 1, (h - 1) % 2)
                fox_exp(h, h % 2)
                j = h // 2
                if h % 2 == 0:
                    if j >= 2:
                        act.wait_ge(fo_mm, j * 2 + 2)
                    made(act, act.activation(fv_cur[j % 2][:], fv[:, :, j * P:(j + 1) * P], ACT.Copy), fval_ready, j + 1)
                elif j < 4:
                    fox_queries(j + 2)
            fox_turned(11, 1)
            act.wait_ge(fo_mm, 4 + 10)
            act.dma_start(mem2[:], A["mem2_t"]).then_inc(mem2_loaded, 16)

            act.wait_ge(fo_ready, 2 + 6)
            split(3 * KT, KT, m2_hi)
            for j in range(8):
                turn(B_KV2 + j, 0)
                if j < 4:
                    made(act, act.activation(mk2[:, j], acc[j % 2][:, 0:MEM], ACT.Copy), acc_read, 2 + 42 + j + 1)
                else:
                    made(act, act.activation(tmp[j % 2][:, 0:MEM], acc[j % 2][:, 0:MEM], ACT.Copy), acc_read, 2 + 42 + j + 1)
                    act.wait_ge(v2_tr, j - 3)
                    made(act, act.activation(mv2[:, :, (j - 4) * P:(j - 3) * P],
                                             bank[3 + j % 2][:, 0:MEM].rearrange("p (m d) -> p m d", m=2), ACT.Copy),
                         mv2_ready, j - 3)
                if j < 6:
                    made(act, act.activation(f_hi[:, j], fg[:, j], ACT.Copy), fh, j + 1)

            def q_gm(i):
                for r in range(4):
                    turn(B_QG + r, i * 4)
                    j, n = i * 2 + r // 2, i * 4 + (50 + r)
                    read(tile(gm if r % 2 else q2, j), acc[r % 2][:], ACT.Silu if r % 2 else ACT.Copy, n=n)
            step.loop(2, 0, q_gm)

            def exponentials2(h):
                act.wait_ge(mx2_ready, h + 1)
                if h >= 2:
                    act.wait_ge(p2_tr, 2 * h - 2)
                for t in range(4):
                    ins = act.activation(probs2[h % 2][:, t], score(h, t), ACT.Exp, scale=P ** -0.5,
                                         bias=maxima(h, t, what=1), accum_out=maxima(h, t, what=2))
                    made(act, ins, e2_ready, 4 * h + t + 1)
            exponentials2(0)
            for h in range(4):
                if h < 3:
                    exponentials2(h + 1)
                act.wait_ge(yn_in, h + 1)
                made(act, act.activation(yn_hi[:, h], tmp[h % 2][:], ACT.Copy), yn_hi_ready, h + 1)

            def merge2(i):
                for r in range(2):
                    for n in range(3):
                        v = i * 6 + (3 * r + n + 1)
                        turn(B_M2 + 6 * r + 2 * n, i * 12)
                        made(act, activate(tmp[2 + (r + n) % 2][:], p_gate[:], ACT.Sigmoid,
                                           bias=col("b_merge", i * 2 + (r + n * KT))), gate2_ready, v)
                        turn(B_M2 + 6 * r + 2 * n + 1, i * 12)
                        act.wait_ge(merge2_done, v)
                    v = i * 2 + (r + 1)
                    made(act, activate(tile(g2_hi, i * 2 + r), tmp[4][:], ACT.Copy), mg2_hi, v)
            step.loop(4, 0, merge2)
            act.dma_start(x3[:], x2_keep).then_inc(x3_loaded, 16)
            for j in range(8):
                turn(B_OUT2 + j, 0, more=B_OUT2 + j + SLOTS < B_END)
                act.wait_ge(x3_ready, j + 1)
                squares(j, x3[:, j], 5 * KT + j + 1)
            act.wait_ge(sq_summed, 6 * KT)
            made(act, act.activation(tmp[2][:], p_norm[:], ACT.Sqrt, scale=1.0 / DM, bias=EPS), root_ready, 6)
            for k in range(KT):
                act.wait_ge(fin_ready, k + 1)
                act.dma_start(out[:, k], x3[:, k]).then_inc(out_stored, 16)

        @block.vector
        def _(dve):
            step = Steps(dve, s_dve)

            def flat(ap):
                return ap.rearrange("p o t -> p (o t)")

            def tile(x, j):
                return flat(x[:, bass.ds(j, 1)])

            def free_acc(value):
                dve.sem_inc(acc_free, 1)

            def norm_split(t, n0, x, g, ntiles, hi, lo, n, inverse=None):
                if inverse is None:
                    inverse = tmp[3][:, 0:n]
                    dve.wait_ge(root_ready, t + 1)
                    step(dve.reciprocal(inverse, tmp[2][:, 0:n]))

                def lower(k):
                    dve.wait_ge(split_hi, n0 + k + 1)
                    made(dve, dve.tensor_tensor(lo[:, k], tmp[k % 2][:, 0:n], hi[:, k].bitcast(f32), sub),
                         split_lo, n0 + k + 1)
                for k in range(ntiles):
                    made(dve, dve.scalar_tensor_tensor(tmp[k % 2][:, 0:n], x(k), g(k), inverse, mult, mult),
                         split_in, n0 + k + 1)
                    if k:
                        lower(k - 1)
                lower(ntiles - 1)

            def log1p_start(e, w):
                z, z2, s = w
                step(dve.tensor_scalar(z, e, 2.0, None, add))
                step(dve.reciprocal(z, z))
                step(dve.tensor_tensor(z, z, e, mult))
                step(dve.tensor_tensor(z2, z, z, mult))
                step(dve.tensor_scalar(s, z2, 1.0 / 17, None, mult))
                for m in (15, 13, 11):
                    step(dve.scalar_tensor_tensor(s, s, 1.0 / m, z2, add, mult))

            def log1p_end(u, out, w):
                z, z2, s = w
                for m in (9, 7, 5, 3):
                    step(dve.scalar_tensor_tensor(s, s, 1.0 / m, z2, add, mult))
                step(dve.scalar_tensor_tensor(s, s, 1.0, z, add, mult))
                step(dve.tensor_scalar(z2, u, 0.0, None, vmax))
                step(dve.scalar_tensor_tensor(out, s, 2.0, z2, mult, add))

            def log1p_exp(u, e, out, w):
                log1p_start(e, w)
                log1p_end(u, out, w)

            dve.sem_inc(acc_free, 2)
            dve.wait_ge(par_loaded, 16)
            for n in range(4):
                dve.wait_ge(x_loaded[n], 16)
            norm_split(0, 0, lambda k: x_t[:, k], lambda k: col("norm_g", k), KT, h_hi, h_lo, SEQ)

            def dt_part(n):
                z, z2, s = (tmp_dt[:, i] for i in range(3))
                u, e, out_ = tmp[0][0:32], tmp[1][0:32], dt_c[:]
                if n == 0:
                    dve.wait_ge(block_done, B_DT + 1)
                    made(dve, dve.tensor_scalar(u, acc[0][0:32, :], col("dt_bias", 0, 32), None, add), u_ready, 1)
                    free_acc(1)
                elif n == 1:
                    dve.wait_ge(eu_ready, 1)
                    log1p_start(e, (z, z2, s))
                elif n == 2:
                    log1p_end(u, out_, (z, z2, s))
                elif n == 3:
                    dve.wait_ge(a_exp, 1)
                    step(dve.tensor_scalar(u, out_, scol(0, 1, 32), -1.0, mult, mult))
                    dve.wait_ge(consts_ready, 1)
                    for c in range(NCH):
                        cs = slice(c * CH, (c + 1) * CH)
                        step(dve.tensor_tensor_scan(acs[:, cs], ones[0:32, :], tmp[0][0:32, cs], 0.0, mult, add))
                elif n == 4:
                    for c in range(NCH):
                        ins = dve.tensor_scalar(small[0:32, 128 + 32 * c:160 + 32 * c], ident[0:32, 0:32],
                                                acs[:, (c + 1) * CH - 1:(c + 1) * CH], None, mult)
                        made(dve, ins, acs_ready, c + 1)

            def conv(j, src, y, w, b):
                step(dve.tensor_scalar(y[:], src[:], col(w, j * 4 + 3), col(b, j), mult, add))
                for d in (1, 2, 3):
                    ins = dve.scalar_tensor_tensor(y[:, d:SEQ], src[:, 0:SEQ - d], col(w, j * 4 + (3 - d)), y[:, d:SEQ],
                                                   mult, add)
                    if d < 3:
                        step(ins)
                return ins

            def xbc(i, dt=False):
                for r in range(4):
                    j = i * 4 + r
                    if dt:
                        dt_part(j)
                    dve.wait_ge(block_done, j + (B_XBC + 1))
                    dve.wait_ge(hi_ready, i * 4 + (B_XBC + SLOTS + r))
                    made(dve, conv(j, acc[(B_XBC + r) % 2], tmp[2 + r % 2], "conv_w", "conv_b"), conv_ready, j + 1)
                    free_acc(0)
            xbc(0, dt=True)
            dt_part(4)
            step.loop(XBC_T // 4 - 1, 12, lambda i: xbc(i + 1))

            dve.wait_ge(tok_t, 1)
            step(dve.tensor_copy(tok[:, 0:2].rearrange("p a c h -> p (a c h)"), p_x[:, 0:256]))
            made(dve, dve.tensor_tensor(tok[:, 2].rearrange("p c h -> p (c h)"), p_x[:, 256:384],
                                        tok[:, 1].rearrange("p c h -> p (c h)"), sub), tok_sub, 1)
            dve.wait_ge(tok_exp, 1)

            def heads(t, pair):
                return tok[:, t, :, bass.ds(pair * 2, 2)].unsqueeze(3).to_broadcast([P, NCH, 2, 64])

            def inputs(pair, i):
                dve.wait_ge(x_tr, pair + 1)
                v4 = p_x[:].rearrange("p (c e d) -> p c e d", c=NCH, e=2)
                made(dve, dve.tensor_tensor(xdt[i][:].rearrange("p c (e d) -> p c e d", e=2), v4, heads(0, pair), mult),
                     xd_ready, pair + 1)

            def exponents(pair, i, e):
                dve.wait_ge(bc_mm, pair * 2 + (e + 3))
                for c in range(NCH):
                    cs = slice(c * CH, (c + 1) * CH)
                    ins = dve.tensor_scalar(seg[i][e][:, cs], p_bc[e][:, cs], tok[:, 1, c, bass.ds(pair * 2 + e, 1)],
                                            0.0, sub, vmin)
                    if c < NCH - 1:
                        step(ins)
                made(dve, ins, seg_ready, pair * 2 + (e + 1))

            def weighted(pair, i):
                for e in range(2):
                    dve.wait_ge(exp_ready, pair * 2 + (e + 1))
                    made(dve, dve.tensor_tensor(seg[i][e][:], seg[i][e][:], cb[:].rearrange("p c l -> p (c l)"), mult),
                         g_ready, pair * 2 + (e + 1))

            def carried(pair):
                dve.wait_ge(st_mm, pair + 1)
                step(dve.tensor_copy(prev[:, 0], p_st[:, 0:CH]))
                for c in (1, 2):
                    for e in range(2):
                        hs = slice(64 * e, 64 * e + 64)
                        ins = dve.scalar_tensor_tensor(prev[:, c, hs], prev[:, c - 1, hs],
                                                       tok[:, 3, c, bass.ds(pair * 2 + e, 1)],
                                                       p_st[:, c * CH + 64 * e:c * CH + 64 * e + 64], mult, add)
                        if c == 2 and e == 1:
                            made(dve, ins, prev_ready, pair + 1)
                        else:
                            step(ins)

            def outputs(pair, i):
                dve.wait_ge(y_mm, pair + 1)
                dve.wait_ge(ebc_ready, pair * 2 + 2)
                step(dve.scalar_tensor_tensor(y_tmp[:], tile(xs, pair), col("ssd_d", pair), p_y[:], mult, add))
                step(dve.tensor_tensor(ebc[i][:, CH:], p_off[:, CH:], ebc[i][:, CH:], mult))
                step(dve.tensor_tensor(y_tmp[:, CH:], y_tmp[:, CH:], ebc[i][:, CH:], add))
                dve.wait_ge(z_ready, pair + 1)
                made(dve, dve.tensor_tensor(tile(xs, pair), y_tmp[:], z_silu[:], mult), y_ready, pair + 2)

            def group_norm(g, tiles):
                if 0 in tiles:
                    dve.wait_ge(groot_ready, g + 1)
                    step(dve.reciprocal(rinv[:], rinv[:]))
                for t in tiles:
                    if t >= 2:
                        dve.wait_ge(gn_lo, g * 4 + (t - 1))
                    made(dve, dve.scalar_tensor_tensor(gn[t % 2][:], tile(xs, g * 4 + t), col("ssd_g", g * 4 + t), rinv[:],
                                                       mult, mult), gn_in, g * 4 + (t + 1))

            def group(g, first=False, last=False):
                for r in range(4):
                    pair, i = g * 4 + r, r % 2
                    if r == 0:
                        dve.wait_ge(cb_mm, g + 1)
                        made(dve, dve.tensor_tensor(cb[:], p_off[:].rearrange("p (c l) -> p c l", c=NCH),
                                                    tril[:].unsqueeze(1).to_broadcast([P, NCH, CH]), mult), cb_ready, g + 1)
                    weighted(pair, i)
                    if not first and r in (1, 2):
                        group_norm(g - 1, (0, 1) if r == 1 else (2, 3))
                    if not (last and r == 3):
                        inputs(pair + 1, 1 - i)
                        exponents(pair + 1, 1 - i, 0)
                    carried(pair)
                    if not (last and r == 3):
                        exponents(pair + 1, 1 - i, 1)
                    outputs(pair, i)
            dve.sem_inc(y_ready, 1)
            inputs(0, 0)
            for e in range(2):
                exponents(0, 0, e)
            group(0, first=True)
            step.loop(2, 53, lambda i: group(i + 1))
            group(3, last=True)
            group_norm(3, range(4))
            dve.wait_ge(gn_lo, 16)

            def merge(base, per, gate0, first):
                tiles = 4 if per == 3 else 2

                def body(i, beside=None):
                    for r in range(tiles):
                        j = i * tiles + r
                        v = i * tiles + (gate0 + r + 1)
                        if beside:
                            beside(j)
                        dve.wait_ge(gate_ready, v)
                        dve.wait_ge(block_done, i * (tiles * per) + (base + per * (r + 1)))
                        if first:
                            made(dve, dve.tensor_tensor(tile(merged, j), acc[(M_OF[base] + r) % 2][:], tmp[2 + r % 2][:], mult),
                                 merge_done, v)
                            free_acc(0)
                        else:
                            step(dve.tensor_tensor(tmp[4][:], acc[(M_OF[base] + r) % 2][:], tmp[2 + r % 2][:], mult))
                            free_acc(0)
                            made(dve, dve.tensor_tensor(tile(merged, j), tile(merged, j), tmp[4][:], add), merge_done, v)
                return body, KT // tiles
            def exponential(x, out, w):
                n, p, two_n = w
                step(dve.tensor_scalar(p, x, -88.0, 88.0, vmax, vmin))
                step(dve.tensor_scalar(n, p, 1.4426950408889634, MAGIC, mult, add))
                step(dve.tensor_scalar(n, n, -MAGIC, None, add))
                step(dve.scalar_tensor_tensor(p, n, -0.693359375, p, mult, add))
                step(dve.scalar_tensor_tensor(p, n, 2.12194440e-4, p, mult, add))
                step(dve.tensor_scalar(n, n, 127.0, 8388608.0, add, mult))
                step(dve.tensor_copy(two_n.bitcast(mybir.dt.int32), n))
                step(dve.tensor_scalar(out, p, 1.0 / 5040, None, mult))
                for c in (1.0 / 720, 1.0 / 120, 1.0 / 24, 1.0 / 6, 0.5, 1.0):
                    step(dve.scalar_tensor_tensor(out, out, c, p, add, mult))
                step(dve.tensor_scalar(out, out, 1.0, None, add))
                step(dve.tensor_tensor(out, out, two_n, mult))

            def cmul(or_, oi, ar, ai, br, bi, w):
                step(dve.tensor_tensor(w, ai, bi, mult))
                step(dve.tensor_tensor(or_, ar, br, mult))
                step(dve.tensor_tensor(or_, or_, w, sub))
                step(dve.tensor_tensor(w, ai, br, mult))
                step(dve.tensor_tensor(oi, ar, bi, mult))
                step(dve.tensor_tensor(oi, oi, w, add))

            s5 = lambda c: sc5[:, c]
            lam_re, lam_im, log_step = (pcol[:, PC[n]:PC[n] + 24] for n in ("lam_re", "lam_im", "log_step"))
            pr, pi, t = s5(12), s5(3), (s5(10), s5(11))

            def doubled(table, m):
                wide = lambda x: x.unsqueeze(2).to_broadcast([P, 24, m])
                w = tmp[0][:, 0:24 * m].rearrange("p (s b) -> p s b", s=24)
                cmul(table[:, :, m:2 * m, 0], table[:, :, m:2 * m, 1], table[:, :, 0:m, 0], table[:, :, 0:m, 1],
                     wide(pr), wide(pi), w)
                cmul(t[0], t[1], pr, pi, pr, pi, s5(17))
                step(dve.tensor_copy(pr, t[0]))
                step(dve.tensor_copy(pi, t[1]))

            def s5_part(j):
                if j == 0:
                    exponential(log_step, s5(0), (s5(10), s5(11), s5(12)))
                    step(dve.tensor_tensor(s5(1), lam_im, s5(0), mult))
                    step(dve.tensor_scalar(s5(10), s5(1), 0.15915494309189535, MAGIC, mult, add))
                    step(dve.tensor_scalar(s5(10), s5(10), -MAGIC, None, add))
                    for c in (6.28125, 1.9340515136718750e-3, 1.2556659146e-6):
                        step(dve.scalar_tensor_tensor(s5(1), s5(10), -c, s5(1), mult, add))
                    step(dve.tensor_scalar(s5(1), s5(1), 3.1415925, -3.1415925, vmin, vmax))
                    step(dve.tensor_tensor(s5(13), lam_re, s5(0), mult))
                    step(dve.tensor_scalar(s5(2), s5(13), 1.0, None, vmin))
                    made(dve, dve.tensor_scalar(s5(6), s5(13), 1.0, 88.0, vmax, vmin), step_ready, 1)
                elif j == 1:
                    dve.wait_ge(lam_ready, 1)
                    step(dve.tensor_scalar(scol(40, 12), cols("lru_lam", LRU_T), -1.0, None, mult))
                    log1p_exp(scol(40, 12), scol(52, 12), scol(88, 12), (scol(256, 12), scol(268, 12), scol(280, 12)))
                    step(dve.tensor_scalar(scol(64, 12), scol(88, 12), -8.0, None, mult))
                    made(dve, dve.tensor_scalar(scol(76, 12), scol(88, 12), 8.0, None, mult), lam_ready, 2)
                elif j == 2:
                    dve.wait_ge(t_exp, 1)
                    step(dve.tensor_scalar(s5(10), s5(5), -1.0, 1.0, mult, add))
                    step(dve.reciprocal(s5(10), s5(10)))
                    step(dve.scalar_tensor_tensor(s5(10), s5(5), 2.0, s5(10), mult, mult))
                    step(dve.tensor_tensor(s5(11), s5(7), s5(8), sub))
                    step(dve.tensor_tensor(s5(10), s5(10), s5(11), add))
                    step(dve.tensor_scalar(s5(14), s5(10), 1.0, None, add))
                    step(dve.tensor_tensor(s5(11), s5(4), s5(4), mult))
                    step(dve.tensor_scalar(s5(11), s5(11), -2.0, None, mult))
                    step(dve.tensor_scalar(s5(12), s5(11), 1.0, None, add))
                    step(dve.tensor_tensor(s5(13), s5(10), s5(12), mult))
                    step(dve.tensor_tensor(s5(13), s5(13), s5(11), add))
                    step(dve.tensor_tensor(s5(15), s5(14), s5(3), mult))
                    step(dve.tensor_tensor(s5(16), lam_re, lam_re, mult))
                    step(dve.tensor_tensor(s5(17), lam_im, lam_im, mult))
                    step(dve.tensor_tensor(s5(16), s5(16), s5(17), add))
                    step(dve.reciprocal(s5(16), s5(16)))
                    for out_, a, b, op in ((18, (13, lam_re), (15, lam_im), add), (9, (15, lam_re), (13, lam_im), sub)):
                        step(dve.tensor_tensor(s5(17), s5(a[0]), a[1], mult))
                        step(dve.tensor_tensor(s5(10), s5(b[0]), b[1], mult))
                        step(dve.tensor_tensor(s5(17), s5(17), s5(10), op))
                        step(dve.tensor_tensor(s5(out_), s5(17), s5(16), mult))
                    for table in (turn_v, turn_u):
                        step(dve.memset(table[:, :, 0, 0], 1.0))
                        step(dve.memset(table[:, :, 0, 1], 0.0))
                elif j >= 3:
                    for n in (2 * j - 6, 2 * j - 5):
                        if n < 5:
                            doubled(turn_v, 1 << n)
                        elif n < 9:
                            doubled(turn_u, 1 << (n - 5))
                    if j == 7:
                        dve.sem_inc(tables_ready, 1)
            body, count = merge(B_MSSD, 3, 0, True)
            for i in range(count):
                body(i, s5_part)

            def lru_x(i):
                for r in range(4):
                    j = i * 4 + r
                    dve.wait_ge(block_done, j + (B_LX + 1))
                    y = tmp[2 + r % 2]
                    step(conv(j, acc[(M_OF[B_LX] + r) % 2], y, "lconv_w", "lconv_b"))
                    free_acc(0)
                    made(dve, dve.tensor_copy(tile(xl, j), y[:]), lx_done, j + 1)
            def lower_xl(g):
                for t in range(3):
                    v = g * 3 + (t + 1)
                    dve.wait_ge(xlh_ready, v)
                    made(dve, dve.tensor_tensor(xl_lo[:, t], tile(xl, g * 3 + t), xl_hi[:, t].bitcast(f32), sub), xls_ready, v)

            step.loop(2, 16, lru_x)
            lower_xl(0)
            lru_x(2)
            dve.wait_ge(root_ready, 2)
            step(dve.reciprocal(mem_rms, mem_rms))

            def lower_ly(g):
                for t in range(3):
                    v = g * 3 + (t + 1)
                    dve.wait_ge(ly_hi, v)
                    made(dve, dve.tensor_tensor(tile(l_lo, g * 3 + t), l_y[t][:], tile(l_hi, g * 3 + t).bitcast(f32), sub),
                         ly_done, v)

            def lru_gates(g):
                for t in range(3):
                    v = g * 3 + (t + 1)
                    dve.wait_ge(sig_ready, v)
                    step(dve.tensor_tensor(l_i[:, t], l_i[:, t], tile(xl, g * 3 + t), mult))
                if g < 3:
                    lower_xl(g + 1)
                dve.wait_ge(dec_ready, g + 1)
                made(dve, dve.scalar_tensor_tensor(l_r[:], l_sq[:], 1.0, l_r[:], add, mult), m2_ready, g + 1)
                dve.wait_ge(m_ready, g + 1)
                for t in range(3):
                    step(dve.tensor_tensor(l_i[:, t], l_i[:, t], l_r[:, t], mult))
                    step(dve.tensor_tensor_scan(l_r[:, t], l_a[:, t], l_i[:, t], 0.0, mult, add))
                for t in range(3):
                    v = g * 3 + (t + 1)
                    y, gate = l_y[t], l_gate[t]
                    dve.wait_ge(lsilu_ready, v)
                    step(dve.tensor_tensor(gate[:], lg_bank[t][:], gate[:], mult))
                    dve.sem_inc(lg_free, 1)
                    made(dve, dve.tensor_tensor(y[:], l_r[:, t], gate[:], mult), ly_in, v)
                if g < 3:
                    lower_ly(g)

            for g in range(4):
                lru_gates(g)

            norm_split(1, KT, lambda k: mem_t[:, k], lambda k: col("mem_g", k), KT, m_hi, m_lo, MEM, mem_rms)
            lower_ly(3)

            def kv(i):
                for r in range(4):
                    j = i * 4 + r
                    dve.wait_ge(block_done, j + (B_KV + 1))
                    made(dve, dve.tensor_copy(tile(mk, j), acc[(M_OF[B_KV] + r) % 2][:, 0:MEM]), kv_ready, j + 1)
                    free_acc(0)
            step.loop(2, 0, kv)

            def values(i):
                for r in range(4):
                    j = i * 4 + r
                    dve.wait_ge(block_done, j + (B_KV + KT + 1))
                    made(dve, dve.tensor_copy(tmp[r % 2][:, 0:MEM], acc[(M_OF[B_KV] + r) % 2][:, 0:MEM]), kv_ready, j + (KT + 1))
                    free_acc(0)
                    dve.wait_ge(v_tr, j + 1)
                    step(dve.tensor_copy(mv[:, :, bass.ds(j * P, P)],
                                         bank[3 + r % 2][:, 0:MEM].rearrange("p (m d) -> p m d", m=2)))
            step.loop(2, 4, values)
            body, count = merge(B_MLRU, 3, KT, False)
            step.loop(count, 4, body)

            def queries(i):
                for r in range(4):
                    j = i * 4 + r
                    dve.wait_ge(block_done, j + (B_Q + 1))
                    made(dve, dve.tensor_copy(tile(q, j), acc[(M_OF[B_Q] + r) % 2][:]), q_ready, j + 1)
                    free_acc(0)
            step.loop(2, 0, queries)

            def largest(h, done, ready, scale):
                dve.wait_ge(done, h + 1)
                for t in (0, 2):
                    two = bank[3 * (1 - h % 2) + t // 2][:].rearrange("p (t m) -> p t m", t=2)
                    step(dve.tensor_reduce(maxima(h, t, 2), two, AX.X, vmax))
                made(dve, dve.tensor_scalar(maxima(h, 0, 4, 1), maxima(h, 0, 4), -scale, None, mult), ready, h + 1)

            def quotients(h, p, done, ready):
                dve.wait_ge(done, 4 * h + 4)
                step(dve.reciprocal(maxima(h, 0, 4, 3), maxima(h, 0, 4, 2)))
                inverse = maxima(h, 0, 4, 3).unsqueeze(2).to_broadcast([P, 4, MEM])
                made(dve, dve.tensor_tensor(p[h % 2][:], p[h % 2][:], inverse, mult), ready, h + 1)
            largest(0, sc_mm, mx_ready, 1.0 / 16)
            for h in range(4):
                quotients(h, probs, pe_ready, pn_ready)
                if h < 3:
                    largest(h + 1, sc_mm, mx_ready, 1.0 / 16)
                for m in range(2):
                    dve.wait_ge(p_tr, 2 * h + m + 1)
                    made(dve, dve.tensor_copy(probs_t[:, m], bank[5 + m][:]), pt_ready, 2 * h + m + 1)
                for d in range(2):
                    v = 2 * h + d + 1
                    dve.wait_ge(o_mm, v)
                    made(dve, dve.tensor_copy(tmp[d][:], bank[7 - 5 * d][:]), yo_in, v)
                    dve.wait_ge(yo_hi, v)
                    made(dve, dve.tensor_tensor(ym_lo[:, 2 * h + d], tmp[d][:], ym_hi[:, 2 * h + d].bitcast(f32), sub),
                         yo_done, v)

            def merge_mem(i):
                for r in range(2):
                    j, v = i * 2 + r, i * 2 + (r + 1)
                    dve.wait_ge(gate_ready, v + 2 * KT)
                    dve.wait_ge(block_done, i * 4 + (B_MMEM + 2 * r + 2))
                    step(dve.tensor_tensor(tmp[4][:], acc[(M_OF[B_MMEM] + r) % 2][:], tmp[2 + r % 2][:], mult))
                    free_acc(0)
                    made(dve, dve.tensor_tensor(tile(merged, j), tile(merged, j), tmp[4][:], add), merge_done, v + 2 * KT)
                    dve.wait_ge(mg_hi, v)
                    made(dve, dve.tensor_tensor(tile(g_lo, j), tile(merged, j), tile(g_hi, j).bitcast(f32), sub), mg_done, v)
            step.loop(4, 2, merge_mem)


            def outs(i):
                dve.wait_ge(xre_loaded[i], 16)
                for r in range(4):
                    j = i * 4 + r
                    dve.wait_ge(block_done, j + (B_OUT + 1))
                    made(dve, dve.tensor_tensor(tile(x1, j), acc[(M_OF[B_OUT] + r) % 2][:], tile(x1, j), add), x1_ready, j + 1)
                    free_acc(0)
            outs(0)
            outs(1)
            step(dve.tensor_tensor(scol(40, KT), cols("final_g", KT), cols("g_norm_2", KT), mult))
            dve.wait_ge(sq_summed, 4 * KT)
            step(dve.tensor_scalar(tmp[4][:], p_norm[:], EPS / DM, EPS * EPS, mult, add))
            made(dve, dve.scalar_tensor_tensor(tmp[4][:], bank[6][:], 1.0 / DM, tmp[4][:], mult, add), var_ready, 1)
            dve.wait_ge(root_ready, 3)
            step(dve.reciprocal(tmp[3][:], tmp[5][:]))
            norm_split(3, 2 * KT, lambda k: x1[:, k], lambda k: scol(40 + k), KT, h_hi, h_lo, SEQ, tmp[3][:])
            dve.wait_ge(block_done, B_FL + 1)
            step(dve.tensor_scalar(tmp[0][:], acc[M_OF[B_FL] % 2][:], col("b_forget"), -1.0, add, mult))
            free_acc(0)
            dve.sem_inc(nu_ready, 1)
            dve.wait_ge(root_ready, 4)
            step(dve.reciprocal(tmp[3][:], tmp[2][:]))
            for k in range(KT):
                made(dve, dve.scalar_tensor_tensor(x1[:, k], x1[:, k], col("final_g", k), tmp[3][:], mult, mult),
                     x2_ready, k + 1)
            dve.wait_ge(enu_ready, 1)
            log1p_exp(tmp[0][:], tmp[1][:], tmp[5][:], (tmp[2][:], tmp[3][:], tmp[4][:]))
            step(dve.memset(tmp[0][:], 1.0))
            made(dve, dve.tensor_tensor_scan(sum_f[:], tmp[0][:], tmp[5][:], 0.0, mult, add), f_ready, 1)

            dve.sem_inc(e_used, 2)

            dve.sem_inc(y5_sum, 1)

            def factor(j):
                dve.wait_ge(s5_loaded, j * 16 + 16)
                cm = s5m[:, 256:512].rearrange("p (s c h) -> p s c h", s=4, c=2)
                f = [sc5[:, c, bass.ds(j * 4, 4)].unsqueeze(2).to_broadcast([P, 4, 32]) for c in (18, 9)]
                w = cf_tmp[:].rearrange("p (s h) -> p s h", s=4)
                step(dve.tensor_tensor(w, cm[:, :, 1], f[1], mult))
                step(dve.tensor_tensor(cf[:, :, 0], cm[:, :, 0], f[0], mult))
                step(dve.tensor_tensor(cf[:, :, 0], cf[:, :, 0], w, sub))
                step(dve.tensor_tensor(w, cm[:, :, 1], f[0], mult))
                step(dve.tensor_tensor(cf[:, :, 1], cm[:, :, 0], f[1], mult))
                made(dve, dve.scalar_tensor_tensor(cf[:, :, 1], cf[:, :, 1], -1.0, w, mult, sub), cf_ready, j + 1)

            def s5_sum(j):
                dve.wait_ge(h_free, j * 4 + 5)
                made(dve, dve.scalar_tensor_tensor(tile(ug, j), tile(ug, j), col("s5_d", j), bank[4][:], mult, add),
                     y5_sum, j + 2)

            def gelu_argument(j):
                dve.wait_ge(y5_sq, j + 1)
                step(dve.tensor_scalar(gelu_arg[:], gelu_arg[:], 0.044715, 1.0, mult, add))
                made(dve, dve.tensor_tensor(gelu_arg[:], gelu_arg[:], tile(ug, j), mult), y5_arg, j + 1)

            def gelu(j):
                dve.wait_ge(y5_sig, j + 1)
                made(dve, dve.tensor_tensor(tile(ug, j), tile(ug, j), gelu_sig[:], mult), y5_ready, j + 1)

            def fox_s5(j, before=None):
                for r in range(4):
                    s = j * 4 + r
                    er, ei = (et[:, r % 2, c].unsqueeze(1).to_broadcast([P, 2, SEQ]) for c in range(2))
                    pq = psum[:, 2 + 3 * (r % 2):4 + 3 * (r % 2)]
                    dve.wait_ge(e_made, s + 1)
                    dve.wait_ge(pq_mm, s + 1)
                    step(dve.tensor_tensor(s5_a[:], pq, er, mult))
                    step(dve.tensor_tensor(s5_b[:], pq, ei, mult))
                    step(dve.tensor_tensor(s5_a[:, 0], s5_a[:, 0], s5_b[:, 1], add))
                    step(dve.tensor_tensor(s5_a[:, 1], s5_a[:, 1], s5_b[:, 0], sub))
                    mag = sc5[:, 14, bass.ds(s, 1)].to_broadcast([P, SEQ])
                    for c in range(2):
                        step(dve.tensor_tensor_scan(s5_b[:, c], mag, s5_a[:, c], 0.0, mult, add))
                    if r == 0:
                        if before is not None:
                            s5_sum(before)
                        factor(j)
                    elif before is not None:
                        if r == 1:
                            gelu_argument(before)
                        elif r == 2:
                            gelu(before)
                    step(dve.tensor_tensor(s5_a[:], s5_b[:], er, mult))
                    made(dve, dve.tensor_tensor(s5_b[:], s5_b[:], ei, mult), e_used, s + 3)
                    dve.wait_ge(h_free, s + 1)
                    step(dve.tensor_tensor(tmp[4][:], s5_a[:, 0], s5_b[:, 1], sub))
                    made(dve, dve.tensor_tensor(tmp[5][:], s5_a[:, 1], s5_b[:, 0], add), h_ready, s + 1)
            fox_s5(0)
            step.loop(5, 38, lambda i: fox_s5(i + 1, i))
            s5_sum(5)
            gelu_argument(5)
            gelu(5)

            for j in range(6):
                dve.wait_ge(y5h, j + 1)
                made(dve, dve.tensor_tensor(y5_lo[:, j], u5[:, j], y5_hi[:, j].bitcast(f32), sub), y5l, j + 1)
            for j in range(6):
                dve.wait_ge(acc_read, 2 + 36 + j + 1)
                t = tmp[j % 2][:]
                step(dve.tensor_tensor(t, u5[:, j], tmp[2 + j % 2][:], mult))
                made(dve, dve.tensor_tensor(t, t, gs[:, j], mult), s5_in, j + 1)
                dve.wait_ge(s5_hi, j + 1)
                made(dve, dve.tensor_tensor(s_lo[:, j], t, s_hi[:, j].bitcast(f32), sub), s5_done, j + 1)

            def fox_max(h, e):
                dve.wait_ge(fs_mm, h + 1)
                two = fbank(e, 1)[:, 2 * P:].rearrange("p (t s) -> p t s", t=2)
                for x, m in ((fbank(e, 0)[:, 3 * P:], negm[:]), (two, negm[:].unsqueeze(1).to_broadcast([P, 2, P])),
                             (fbank(e, 2)[:, P:2 * P], negm[:])):
                    step(dve.tensor_tensor(x, x, m, add))
                for t in range(4):
                    o, w = FOX_AT[t], (t + 1) * P
                    step(dve.tensor_reduce(fcol(e, t, 0), fbank(e, o // SEQ)[:, o % SEQ:o % SEQ + w], AX.X, vmax))
                made(dve, dve.tensor_scalar(fcol(e, 0, 1, 4), fcol(e, 0, 0, 4), -1.0, None, mult), fmx_ready, h + 1)

            def fox_quotients(h, e):
                dve.wait_ge(fe_ready, h * 4 + 4)
                step(dve.reciprocal(fcol(e, 0, 3, 4), fcol(e, 0, 2, 4)))
                for t in range(4):
                    o, w = FOX_AT[t], (t + 1) * P
                    ins = dve.tensor_scalar(f_p[e][:, o:o + w], f_p[e][:, o:o + w], fcol(e, t, 3), None, mult)
                    made(dve, ins, fn_ready, h * 4 + (t + 1))

            def fox_out(j, b):
                dve.wait_ge(fo_mm, j * 2 + 6)
                made(dve, dve.tensor_tensor(tile(fg, j), acc[b][:], tile(fg, j), mult), fo_ready, j + 3)

            def fox(i, first=False):
                for n in range(4):
                    h = i * 4 + n
                    fox_max(h, n % 2)
                    fox_quotients(h, n % 2)
                    if n == 2 or (n == 0 and not first):
                        fox_out(i * 2 + (n // 2 - 1), 1 - n // 2)
            dve.wait_ge(root_ready, 5)
            step(dve.reciprocal(mem2_rms, mem2_rms))
            dve.sem_inc(fo_ready, 2)
            fox(0, True)
            step.loop(2, 32, lambda i: fox(i + 1))
            fox_out(5, 1)
            dve.wait_ge(mem2_loaded, 48)
            norm_split(4, 3 * KT, lambda k: mem2[:, k], lambda k: col("g_mem_norm_2", k), KT, m2_hi, m2_lo, MEM, mem2_rms)
            for j in range(6):
                dve.wait_ge(fh, j + 1)
                made(dve, dve.tensor_tensor(f_lo[:, j], fg[:, j], f_hi[:, j].bitcast(f32), sub), fl_done, j + 1)
            largest(0, sc2_mm, mx2_ready, P ** -0.5)
            for h in range(4):
                quotients(h, probs2, e2_ready, n2_ready)
                if h < 3:
                    largest(h + 1, sc2_mm, mx2_ready, P ** -0.5)
                for m in range(2):
                    dve.wait_ge(p2_tr, 2 * h + m + 1)
                    made(dve, dve.tensor_copy(probs2_t[:, m], bank[5 + m][:]), p2t_ready, 2 * h + m + 1)
                dve.wait_ge(o2_mm, h + 1)
                made(dve, dve.tensor_tensor(tmp[h % 2][:], bank[7][:], gm[:, h], mult), yn_in, h + 1)
                dve.wait_ge(yn_hi_ready, h + 1)
                made(dve, dve.tensor_tensor(yn_lo[:, h], tmp[h % 2][:], yn_hi[:, h].bitcast(f32), sub), yn_done, h + 1)

            def merge2(i):
                for r in range(2):
                    for n in range(3):
                        v, a = i * 6 + (3 * r + n + 1), acc[(M_OF[B_M2] + 3 * r + n) % 2][:]
                        g = tmp[2 + (r + n) % 2][:]
                        dve.wait_ge(gate2_ready, v)
                        dve.wait_ge(block_done, i * 12 + (B_M2 + 6 * r + 2 * n + 2))
                        if n == 0:
                            made(dve, dve.tensor_tensor(tmp[4][:], a, g, mult), merge2_done, v)
                            free_acc(0)
                        else:
                            step(dve.tensor_tensor(tmp[5][:], a, g, mult))
                            free_acc(0)
                            made(dve, dve.tensor_tensor(tmp[4][:], tmp[4][:], tmp[5][:], add), merge2_done, v)
                    v = i * 2 + (r + 1)
                    dve.wait_ge(mg2_hi, v)
                    made(dve, dve.tensor_tensor(tile(g2_lo, i * 2 + r), tmp[4][:], tile(g2_hi, i * 2 + r).bitcast(f32), sub),
                         mg2_done, v)
            step.loop(4, 4, merge2)
            dve.wait_ge(x3_loaded, 16)
            for j in range(8):
                dve.wait_ge(block_done, B_OUT2 + j + 1)
                made(dve, dve.tensor_tensor(x3[:, j], acc[(M_OF[B_OUT2] + j) % 2][:], x3[:, j], add), x3_ready, j + 1)
                free_acc(0)
            dve.wait_ge(root_ready, 6)
            step(dve.reciprocal(tmp[3][:], tmp[2][:]))
            for k in range(KT):
                made(dve, dve.scalar_tensor_tensor(x3[:, k], x3[:, k], col("g_final_2", k), tmp[3][:], mult, mult),
                     fin_ready, k + 1)

        @block.tensor
        def _(pe):
            def tile(x, j):
                return x[:, bass.ds(j, 1)].rearrange("p o t -> p (o t)")

            def weights(b, off, out, hi, lo, ks, slots=None, start=True, stop=True, ready=None):
                pe.wait_ge(lo_ready, off + (b + 1))
                slots = slots or range(len(ks))
                for n, (s, k) in enumerate(zip(slots, ks)):
                    whi, wlo = w_hi[:, b % SLOTS, s], w_lo[:, b % SLOTS, s]
                    if ready:
                        pe.wait_ge(ready[0], ready[1] + k + 1)
                    pe.matmul(out, whi, hi(k), start=start and n == 0, stop=False)
                    pe.matmul(out, whi, lo(k), start=False, stop=False)
                    last = pe.matmul(out, wlo, hi(k), start=False, stop=stop and n == len(ks) - 1)
                return last

            H = (lambda k: h_hi[:, k], lambda k: h_lo[:, k])

            def sum_square(k, value, ntiles=KT, n=SEQ, scratch=tmp):
                pe.wait_ge(sq_ready, value)
                pe.matmul(p_norm[:, 0:n], ones[:], scratch[k % 2][:, 0:n], start=k == 0, stop=k == ntiles - 1
                          ).then_inc(sq_summed, 1)

            def sum_squares(sq0, ntiles, n):
                for k in range(ntiles):
                    sum_square(k, sq0 + k + 1, ntiles, n)

            def free(m, off=0):
                pe.wait_ge(acc_free, off + (m + 1))

            pe.wait_ge(consts_ready, 1)
            sum_squares(0, KT, SEQ)
            free(0)
            weights(B_DT, 0, acc[0][:], *H, range(KT), ready=(split_lo, 0)).then_inc(block_done, 1)

            def simple(base, count):
                m = M_OF[base]

                def body(i):
                    for r in range(4):
                        free(m + r, i * 4)
                        weights(base + r, i * 4, acc[(m + r) % 2][:], *H, range(KT)).then_inc(block_done, 1)
                with pe.Fori(0, count) as i:
                    body(i)
            simple(B_XBC, XBC_T // 4)

            pe.wait_ge(acs_ready, 4)
            for c in range(NCH):
                pe.transpose(p_x[:, 32 * c:32 * c + 32], dt_c[:, c * CH:(c + 1) * CH], ident[0:32, 0:32])
            for c in range(NCH):
                pe.transpose(p_x[:, 128 + 32 * c:160 + 32 * c], acs[:, c * CH:(c + 1) * CH], ident[0:32, 0:32])
            for c in range(NCH):
                ins = pe.matmul(p_x[:, 256 + 32 * c:288 + 32 * c], ones[0:32, :], small[0:32, 128 + 32 * c:160 + 32 * c],
                                start=True, stop=True)
            ins.then_inc(tok_t, 1)
            pe.wait_ge(tok_exp, 1)
            pe.wait_ge(silu_done, XBC_T)
            pe.wait_ge(acc_free, M_OF[B_Z] + 2)

            def summed_decays(pair, i):
                pe.wait_ge(sel_ready, pair * 2 + 2)
                if not isinstance(pair, int) or pair:
                    pe.wait_ge(seg_ready, pair * 2)
                    pe.wait_ge(ebc_ready, pair * 2)
                for e in range(2):
                    pe.matmul(p_bc[e][:], sel[:, i, e], acs[:], start=True, stop=True).then_inc(bc_mm, 1)

            def x_turned(pair):
                pe.wait_ge(x_cur_ready, pair + 1)
                if not isinstance(pair, int) or pair:
                    pe.wait_ge(xd_ready, pair)
                for c in range(NCH):
                    ins = pe.transpose(p_x[:, c * CH:(c + 1) * CH], x_cur[:, c * CH:(c + 1) * CH], ident[:])
                ins.then_inc(x_tr, 1)

            def group_sum(g):
                pe.wait_ge(gss_ready, g + 1)
                pe.matmul(p_st[:], ones[:], gss[:], start=True, stop=True).then_inc(gsum_mm, 1)

            def group(g, first=False, last=False):
                for r in range(4):
                    pair, i = g * 4 + r, r % 2
                    weights(B_Z + r, g * 4, acc[r % 2][:], *H, range(KT)).then_inc(block_done, 1)
                    if r == 0:
                        pe.wait_ge(bcur_ready, g + 1)
                        pe.wait_ge(xd_ready, pair + 1)
                        for c in range(NCH):
                            ins = pe.transpose(p_x[:, c * CH:(c + 1) * CH], b_cur[:, c * CH:(c + 1) * CH], ident[:])
                        ins.then_inc(b_t, 1)
                        pe.wait_ge(y_ready, pair + 1)
                        for c in range(NCH):
                            ins = pe.matmul(p_off[:, c * CH:(c + 1) * CH], b_cur[:, c * CH:(c + 1) * CH],
                                            xs[:, bass.ds(g + 20, 1), c * CH:(c + 1) * CH].rearrange("p o t -> p (o t)"),
                                            start=True, stop=True)
                        ins.then_inc(cb_mm, 1)
                        summed_decays(pair + 1, 1 - i)
                        pe.wait_ge(btok_ready, g + 1)
                        x_turned(pair + 1)
                    elif not (last and r == 3):
                        x_turned(pair + 1)
                        summed_decays(pair + 1, 1 - i)
                    pe.wait_ge(xde_ready, pair + 1)
                    if r == 1 and not first:
                        pe.wait_ge(groot_ready, g)
                    for c in range(NCH - 1):
                        ins = pe.matmul(p_st[:, c * CH:(c + 1) * CH], b_tok[:, c], xde[:, c], start=True, stop=True)
                    ins.then_inc(st_mm, 1)
                    for e in range(2):
                        pe.wait_ge(g_ready, pair * 2 + (e + 1))
                        for c in range(NCH):
                            pe.matmul(p_y[64 * e:64 * e + 64, c * CH:(c + 1) * CH], xdt[i][:, c, 64 * e:64 * e + 64],
                                      seg[i][e][:, c * CH:(c + 1) * CH], start=True, stop=True)
                    pe.wait_ge(prev_ready, pair + 1)
                    for c in range(1, NCH):
                        ins = pe.matmul(p_off[:, c * CH:(c + 1) * CH], prev[:, c - 1],
                                        xs[:, bass.ds(g + 20, 1), c * CH:(c + 1) * CH].rearrange("p o t -> p (o t)"),
                                        start=True, stop=True)
                    ins.then_inc(y_mm, 1)
                    if r == 0 and not first:
                        group_sum(g - 1)
            pe.sem_inc(bc_mm, 2)
            x_turned(0)
            summed_decays(0, 0)
            group(0, first=True)
            with pe.Fori(1, 3) as g:
                group(g)
            group(3, last=True)
            group_sum(3)

            def merge(base, gate0, hi, lo, k1, k2):
                per, tiles, m = (3, 4, M_OF[base]) if k2 else (2, 2, M_OF[base])

                def body(i):
                    off = i * (tiles * per)
                    for r in range(tiles):
                        b = base + per * r
                        weights(b, off, p_gate[:], *H, range(KT)).then_inc(block_done, 1)
                        free(m + r, i * tiles)
                        if base == B_MSSD:
                            pe.wait_ge(gn_lo, 16)
                        weights(b + 1, off, acc[(m + r) % 2][:], hi, lo, range(k1), stop=not k2).then_inc(block_done, 1)
                        if k2:
                            weights(b + 2, off, acc[(m + r) % 2][:], hi, lo, range(KT, KT + k2), start=False
                                    ).then_inc(block_done, 1)
                        pe.wait_ge(gate_ready, i * tiles + (gate0 + r + 1))
                with pe.Fori(0, KT // tiles) as i:
                    body(i)
            merge(B_MSSD, 0, lambda k: y_hi[:, k], lambda k: y_lo[:, k], KT, KT)

            for j in range(LRU_T):
                free(M_OF[B_LX] + j)
                weights(B_LX + j, 0, acc[(M_OF[B_LX] + j) % 2][:], *H, range(KT)).then_inc(block_done, 1)
                if 1 <= j <= KT:
                    sum_square(j - 1, KT + j, n=MEM)

            pe.wait_ge(acc_free, M_OF[B_LX] + LRU_T + 2)
            pe.sem_inc(lg_free, 3)
            for g in range(4):
                pe.wait_ge(xls_ready, g * 3 + 3)
                for t in range(3):
                    if t == 2:
                        pe.wait_ge(sig_ready, g * 3 + 1)
                    pa, px = bank[2 + (t % 2) * 2], bank[3 + (t % 2) * 2]
                    X = (lambda k: xl_hi[:, k], lambda k: xl_lo[:, k])
                    ks = LRU_KS[t]
                    weights(B_LG + 6 * g + t, 0, pa[:], *X, ks, slots=ks)
                    weights(B_LG + 6 * g + t, 0, px[:], *X, ks, slots=[3 + k for k in ks]).then_inc(block_done, 1)
                for t in range(3):
                    pe.wait_ge(lg_free, g * 3 + (t + 1))
                    weights(B_LG + 6 * g + 3 + t, 0, lg_bank[t][:], *H, range(KT)).then_inc(block_done, 1)
                pe.wait_ge(sig_ready, g * 3 + 3)
            pe.wait_ge(lg_free, LRU_T + 3)
            MM = (lambda k: m_hi[:, k], lambda k: m_lo[:, k])

            def keys(i):
                for r in range(4):
                    free(M_OF[B_KV] + r, i * 4)
                    first = (split_lo, KT) if isinstance(i, int) and r == 0 else None
                    weights(B_KV + r, i * 4, acc[(M_OF[B_KV] + r) % 2][:, 0:MEM], *MM, range(KT), ready=first
                            ).then_inc(block_done, 1)
            keys(0)
            with pe.Fori(1, 2) as i:
                keys(i)

            def values(i):
                for r in range(4):
                    j = i * 4 + r
                    free(M_OF[B_KV] + KT + r, i * 4)
                    weights(B_KV + KT + r, i * 4, acc[(M_OF[B_KV] + r) % 2][:, 0:MEM], *MM, range(KT)
                            ).then_inc(block_done, 1)
                    pe.wait_ge(kv_ready, j + (KT + 1))
                    for m in range(2):
                        ins = pe.transpose(bank[3 + r % 2][:, m * P:(m + 1) * P], tmp[r % 2][:, m * P:(m + 1) * P], ident[:])
                    ins.then_inc(v_tr, 1)
            with pe.Fori(0, 2) as i:
                values(i)

            pe.wait_ge(ly_done, LRU_T)
            merge(B_MLRU, KT, lambda k: l_hi[:, k], lambda k: l_lo[:, k], KT, 4)
            simple(B_Q, 2)

            pe.wait_ge(q_ready, KT)

            def scores(h):
                for t in range(4):
                    for k in range(2):
                        ins = pe.matmul(score(h, t), q[:, 2 * h + k, t * P:(t + 1) * P], mk[:, 2 * h + k], start=k == 0, stop=k == 1)
                ins.then_inc(sc_mm, 1)
            scores(0)
            for h in range(4):
                if h < 3:
                    scores(h + 1)
                pe.wait_ge(pn_ready, h + 1)
                for m in range(2):
                    for t in range(4):
                        ins = pe.transpose(bank[5 + m][:, t * P:(t + 1) * P], probs[h % 2][:, t, m * P:(m + 1) * P], ident[:])
                    ins.then_inc(p_tr, 1)
                pe.wait_ge(pt_ready, 2 * h + 2)
                for d in range(2):
                    for m in range(2):
                        c0 = (2 * h + d) * P
                        ins = pe.matmul(bank[7 - 5 * d][:], mv[:, m, c0:c0 + P], probs_t[:, m], start=m == 0, stop=m == 1)
                    ins.then_inc(o_mm, 1)
            pe.wait_ge(yo_done, KT)

            merge(B_MMEM, 2 * KT, lambda k: ym_hi[:, k], lambda k: ym_lo[:, k], KT, 0)
            pe.wait_ge(mg_done, KT)

            def two_sums(k):
                for n, (out_, x) in enumerate(((p_norm, tmp[k % 2]), (bank[6], tmp[4 + k % 2]))):
                    pe.wait_ge(sq_ready, 2 * KT + 2 * k + n + 1)
                    pe.matmul(out_[:], ones[:], x[:], start=k == 0, stop=k == KT - 1).then_inc(sq_summed, 1)
            for j in range(KT):
                m = M_OF[B_OUT] + j
                free(m)
                weights(B_OUT + j, 0, acc[m % 2][:], lambda k: g_hi[:, k], lambda k: g_lo[:, k], range(KT)
                        ).then_inc(block_done, 1)
                if j:
                    two_sums(j - 1)
            two_sums(KT - 1)
            free(M_OF[B_FL])
            weights(B_FL, 0, acc[M_OF[B_FL] % 2][:], *H, range(KT), ready=(split_lo, 2 * KT)).then_inc(block_done, 1)

            def read(n):
                pe.wait_ge(acc_read, n + 1)

            def u_gs(i):
                for r in range(4):
                    read(i * 4 + r)
                    if r == 1:
                        pe.wait_ge(acc_free, M_OF[B_FL] + 3)
                    weights(B_UG + r, i * 4, acc[r % 2][:], *H, range(KT)).then_inc(block_done, 1)
            def inputs(j, r):
                rows = slice(32 * r, 32 * r + 32)
                for c in range(2):
                    ins = pe.matmul(bank[2 + 3 * (r % 2) + c][:], s5m[rows, c * P:(c + 1) * P],
                                    u_cur[rows, :], start=True, stop=True)
                ins.then_inc(pq_mm, 1)

            def fox_s5(j):
                for r in range(4):
                    read(j * 4 + (12 + r))
                    weights(B_FOX + r, j * 4, acc[r % 2][:], *H, range(KT)).then_inc(block_done, 1)
                    if r < 3:
                        inputs(j, r + 1)
                    else:
                        pe.wait_ge(s5_loaded, j * 16 + 32)
                        pe.wait_ge(u_cur_ready, j + 2)
                        inputs(j + 1, 0)
                        pe.wait_ge(acc_read, j * 4 + 17)
                        for k in range(NCH):
                            ins = pe.transpose(bank[7][:, k * P:(k + 1) * P], v_tmp[:, k * P:(k + 1) * P], ident[:])
                        ins.then_inc(v5_tr, 1)
                    if r == 0:
                        pe.wait_ge(cf_ready, j + 1)
                        pe.wait_ge(y5_sum, j + 1)
                    pe.wait_ge(h_ready, j * 4 + (r + 1))
                    for c in range(2):
                        ins = pe.matmul(bank[4][32 * r:32 * r + 32, :], cf[:, r, c], tmp[4 + c][:], start=c == 0, stop=c == 1)
                    ins.then_inc(h_free, 1)
                pe.wait_ge(v_evac, j + 1)
            pe.sem_inc(h_free, 1)
            u_gs(0)
            with pe.Fori(1, 2) as i:
                u_gs(i)
            pe.wait_ge(s5_loaded, 16)
            pe.wait_ge(u_cur_ready, 1)
            inputs(0, 0)
            u_gs(2)
            with pe.Fori(0, 6) as j:
                fox_s5(j)
            pe.sem_inc(fo_mm, 4)
            for j in range(6):
                read(36 + j)
                weights(B_GLU + j, 0, acc[j % 2][:], lambda k: y5_hi[:, k], lambda k: y5_lo[:, k], range(6),
                        ready=None if j else (y5l, 0)
                        ).then_inc(block_done, 1)
                if j in (2, 3):
                    for k in (0, 1) if j == 2 else (2, 3):
                        sum_square(k, 4 * KT + k + 1, n=MEM, scratch=tmp[4:6])
            for k in range(4, KT):
                sum_square(k, 4 * KT + k + 1, n=MEM, scratch=tmp[4:6])

            def fox_scores(h, j, b, e):
                pe.wait_ge(fcur_ready, j * 4 + 4)
                pe.wait_ge(frow_ready, j * 2 + 2)
                for t in range(4):
                    o, w = FOX_AT[t], (t + 1) * P
                    ins = pe.matmul(fbank(e, o // SEQ)[:, o % SEQ:o % SEQ + w], fq_cur[b][e][:, t * P:w],
                                    fk_cur[b][e][:, 0:w], start=True, stop=True)
                ins.then_inc(fs_mm, 1)

            def fox_turn(h, e):
                pe.wait_ge(fn_ready, h * 4 + 4)
                for ks in ((0,), (1, 3), (2,)):
                    for k in ks:
                        for t in range(k, 4):
                            o = FOX_T_AT[k] + (t - k) * P
                            x = FOX_AT[t] + k * P
                            ins = pe.transpose(fbank(e, o // SEQ)[:, o % SEQ:o % SEQ + P], f_p[e][:, x:x + P], ident[:])
                    ins.then_inc(fp_tr, 1)
                pe.wait_ge(fpt_ready, h + 1)

            def fox_values(j, b, e):
                pe.wait_ge(fval_ready, j + 1)
                if e == 0:
                    pe.wait_ge(fo_ready, j + 1)
                for k in range(4):
                    o = FOX_T_AT[k]
                    ins = pe.matmul(acc[b][64 * e:64 * e + 64, k * P:], fv_cur[b][:, k, 64 * e:64 * e + 64],
                                    f_pt[:, o:o + SEQ - k * P], start=k == 0, stop=k == 3)
                ins.then_inc(fo_mm, 1)

            def fox(i, last=False):
                for n in range(4):
                    h, j, b, e = i * 4 + n, i * 2 + n // 2, n // 2, n % 2
                    fox_turn(h, e)
                    if not (last and b):
                        fox_scores(h + 2, j + 1, 1 - b, e)
                    fox_values(j, b, e)
            for e in range(2):
                fox_scores(e, 0, 0, e)
            with pe.Fori(0, 2) as i:
                fox(i)
            fox(2, True)

            for j in range(8):
                read(42 + j)
                weights(B_KV2 + j, 0, acc[j % 2][:, 0:MEM], lambda k: m2_hi[:, k], lambda k: m2_lo[:, k], range(KT),
                        ready=None if j else (split_lo, 3 * KT)
                        ).then_inc(block_done, 1)
                if j >= 4:
                    pe.wait_ge(acc_read, 2 + 42 + j + 1)
                    for m in range(2):
                        ins = pe.transpose(bank[3 + j % 2][:, m * P:(m + 1) * P], tmp[j % 2][:, m * P:(m + 1) * P], ident[:])
                    ins.then_inc(v2_tr, 1)

            def q_gm(i):
                for r in range(4):
                    read(i * 4 + (50 + r))
                    weights(B_QG + r, i * 4, acc[r % 2][:], *H, range(KT)).then_inc(block_done, 1)
            with pe.Fori(0, 2) as i:
                q_gm(i)
            pe.wait_ge(acc_read, 2 + 58)
            pe.wait_ge(mv2_ready, 4)

            def scores2(h):
                for t in range(4):
                    ins = pe.matmul(score(h, t), q2[:, h, t * P:(t + 1) * P], mk2[:, h], start=True, stop=True)
                ins.then_inc(sc2_mm, 1)
            scores2(0)
            for h in range(4):
                if h < 3:
                    scores2(h + 1)
                pe.wait_ge(n2_ready, h + 1)
                for m in range(2):
                    for t in range(4):
                        ins = pe.transpose(bank[5 + m][:, t * P:(t + 1) * P], probs2[h % 2][:, t, m * P:(m + 1) * P], ident[:])
                    ins.then_inc(p2_tr, 1)
                pe.wait_ge(p2t_ready, 2 * h + 2)
                for m in range(2):
                    ins = pe.matmul(bank[7][:], mv2[:, m, h * P:(h + 1) * P], probs2_t[:, m], start=m == 0, stop=m == 1)
                ins.then_inc(o2_mm, 1)
            pe.wait_ge(yn_done, 4)
            pe.wait_ge(fl_done, 6)

            branches = ((lambda k: f_hi[:, k], lambda k: f_lo[:, k], 6), (lambda k: s_hi[:, k], lambda k: s_lo[:, k], 6),
                        (lambda k: yn_hi[:, k], lambda k: yn_lo[:, k], 4))

            def merge2(i):
                for r in range(2):
                    for n, (hi, lo, ks) in enumerate(branches):
                        b, m = B_M2 + 6 * r + 2 * n, M_OF[B_M2] + 3 * r + n
                        weights(b, i * 12, p_gate[:], *H, range(KT)).then_inc(block_done, 1)
                        free(m, i * 6)
                        weights(b + 1, i * 12, acc[m % 2][:], hi, lo, range(ks)).then_inc(block_done, 1)
                        pe.wait_ge(gate2_ready, i * 6 + (3 * r + n + 1))
            with pe.Fori(0, 4) as i:
                merge2(i)
            pe.wait_ge(mg2_done, KT)
            for j in range(8):
                m = M_OF[B_OUT2] + j
                free(m)
                weights(B_OUT2 + j, 0, acc[m % 2][:], lambda k: g2_hi[:, k], lambda k: g2_lo[:, k], range(KT)
                        ).then_inc(block_done, 1)
                if j >= 1:
                    sum_square(j - 1, 5 * KT + j)
            sum_square(KT - 1, 6 * KT)

def _stream2(I, np):
    w_in = I["w_in_2"][0]
    o_q, o_k, o_v, o_f, o_gf, o_u, o_gs, o_qm, o_gm, o_gl = 0, 768, 1536, 2304, 2316, 3084, 3852, 4620, 5132, 5644
    cols = lambda w, c, n=P: _block(w, slice(0, DM), slice(c, c + n), np)
    halves = np.zeros((DM, P), w_in.dtype)
    halves[:, 0:12] = halves[:, 64:76] = w_in[:, o_f:o_f + 12]
    out = [cols(halves, 0)]
    for j in range(6):
        out += [cols(w_in, o_u + j * P), cols(w_in, o_gs + j * P)]
    for j in range(6):
        out += [cols(w_in, o + j * P) for o in (o_q, o_k, o_v, o_gf)]
    out += [cols(I["w_glu_2"][0], j * P) for j in range(6)]
    out += [cols(I["w_mem_kv_2"][0], j * P) for j in range(8)]
    for j in range(4):
        out += [cols(w_in, o_qm + j * P), cols(w_in, o_gm + j * P)]
    for j in range(KT):
        for n, w in enumerate(("w_proj_fox_2", "w_proj_s5_2", "w_proj_mem_2")):
            out += [cols(w_in, o_gl + n * DM + j * P), cols(I[w][0], j * P)]
    return out + [cols(I["w_out_2"][0], j * P) for j in range(KT)]


def _params2(I, np):
    b_forget = np.zeros(P, np.float32)
    b_forget[0:12] = b_forget[64:76] = I["b_forget_2"][0]
    return [_columns(I["g_norm_2"][0], np), _columns(I["g_mem_norm_2"][0], np), _columns(I["g_final_2"], np),
            _columns(I["b_merge_2"][0], np), _columns(I["lam_re_2"][0].reshape(-1), np),
            _columns(I["lam_im_2"][0].reshape(-1), np), _columns(np.repeat(I["log_step_2"][0], 64), np),
            _columns(I["s5_d_2"][0], np), _columns(I["b_glu_2"][0], np), _columns(b_forget, np)]


def _arrays2(I, np):
    s5m = np.zeros((7, P, 512), np.float32)
    for j in range(6):
        c = s5m[j, :, 256:].reshape(P, 4, 2, 32)
        for g in range(8):
            s, e = g // 2, g % 2
            for n, (b_, c_) in enumerate((("s5_b_re_2", "s5_c_re_2"), ("s5_b_im_2", "s5_c_im_2"))):
                s5m[j, 16 * g:16 * g + 16, n * P + 64 * e:n * P + 64 * e + 64] = I[b_][0, 8 * j + g].T
                c[64 * e:64 * e + 64, s, n, 16 * e:16 * e + 16] = I[c_][0, 8 * j + g].T
    return {"mem2_t": _channels_first(I["mem_2"][0], np), "s5m": s5m}


def _columns(v, np):
    v = np.asarray(v)
    if v.shape[-1] % P:
        padded = np.zeros(v.shape[:-1] + (P,), v.dtype)
        padded[..., :v.shape[-1]] = v
        v = padded
    return np.moveaxis(v.reshape(v.shape[:-1] + (-1, P)), -1, 0)


def _taps(w, np):
    return np.swapaxes(_columns(w, np), 1, 2).reshape(P, -1)


def _block(w, rows, cols, np):
    part = w[rows, cols]
    padded = np.zeros((KT * P, P), w.dtype)
    padded[:part.shape[0], :part.shape[1]] = part
    return padded.reshape(KT, P, P).transpose(1, 0, 2)


def _channels_first(x, np):
    return np.ascontiguousarray(x.T.reshape(-1, P, x.shape[0]).transpose(1, 0, 2))


def _lru_blocks(w_a, w_x, group, t, np):
    block = np.zeros((P, KT, P), w_a.dtype)
    for n, w in enumerate((w_a, w_x)):
        wide = np.zeros((3 * P, 3 * P), w.dtype)
        for b in range(4):
            wide[96 * b:96 * b + 96, 96 * b:96 * b + 96] = w[4 * group + b]
        block[:, 3 * n:3 * n + 3] = wide[:, t * P:(t + 1) * P].reshape(3, P, P).transpose(1, 0, 2)
    return block


def _stream1(I, np):
    w_in = I["w_in"][0]
    c_z, c_xbc, c_dt, c_lg, c_lx, c_q, c_g = 0, 2048, 5120, 5152, 6688, 8224, 9248
    wide = lambda w, c, n: [_block(w, slice(0, DM), slice(c + j * P, min(c + (j + 1) * P, c + n)), np)
                            for j in range((n + P - 1) // P)]
    out = wide(w_in, c_dt, 32) + wide(w_in, c_xbc, 3072) + wide(w_in, c_z, 2048)
    gates = [wide(w_in, c_g + DM * n, DM) for n in range(3)]

    def branch(n, w):
        parts = [[_block(w, slice(k, min(k + DM, w.shape[0])), slice(j * P, (j + 1) * P), np)
                  for k in range(0, w.shape[0], DM)] for j in range(KT)]
        return [b for j in range(KT) for b in [gates[n][j]] + parts[j]]
    out += branch(0, I["w_br_ssd"][0])
    out += wide(w_in, c_lx, 1536)
    lg = wide(w_in, c_lg, 1536)
    for g in range(4):
        out += [_lru_blocks(I["lru_w_a"][0], I["lru_w_x"][0], g, t, np) for t in range(3)] + lg[3 * g:3 * g + 3]
    out += wide(I["w_kv"][0], 0, 2048)
    out += branch(1, I["w_br_lru"][0])
    out += wide(w_in, c_q, DM)
    out += branch(2, I["w_br_mem"][0])
    out += wide(I["w_out"][0], 0, DM)
    return out


def _params(I, np):
    rep = np.repeat(I["ssd_d"][0], 64)
    t = [_columns(I["norm_g"][0], np), _taps(I["ssd_conv_w"][0], np), _columns(I["ssd_conv_b"][0], np), _columns(rep, np),
         _columns(I["ssd_norm_g"][0].reshape(-1), np), _taps(I["lru_conv_w"][0], np), _columns(I["lru_conv_b"][0], np),
         _columns(I["lru_b_a"][0].reshape(-1), np), _columns(I["lru_b_x"][0].reshape(-1), np),
         _columns(I["lru_lambda"][0], np), _columns(I["mem_norm_g"][0], np), _columns(I["final_g"], np),
         _columns(I["ssd_dt_bias"][0], np), _columns(I["ssd_a_log"][0], np)]
    t += _params2(I, np)
    return np.ascontiguousarray(np.concatenate(t, axis=1))


def kernel(**inputs):
    import numpy as np
    import concourse.bacc as bacc
    from concourse.bass_utils import run_bass_kernel_spmd

    I = {k: np.asarray(v) for k, v in inputs.items()}
    arrays = {
        "x_t": _channels_first(I["x"][0], np),
        "mem_t": _channels_first(I["mem"][0], np),
        "pcol": _params(I, np),
        "wstream": np.ascontiguousarray(np.stack(_stream1(I, np) + _stream2(I, np)).reshape(-1, P, KT * P)),
    }
    arrays.update(_arrays2(I, np))
    nc = bacc.Bacc("TRN2", target_bir_lowering=False, num_devices=1)
    A = {k: nc.dram_tensor(f"in_{k}", a.shape, mybir.dt.float32, kind="ExternalInput").ap() for k, a in arrays.items()}
    out = nc.dram_tensor("out", (P, KT, SEQ), mybir.dt.float32, kind="ExternalOutput").ap()
    build(nc, A, out)
    r = run_bass_kernel_spmd(nc, [{f"in_{k}": a for k, a in arrays.items()}], core_ids=[0])
    y = r.results[0]["out"]
    return np.ascontiguousarray(y.transpose(1, 0, 2).reshape(1, DM, SEQ).transpose(0, 2, 1))
```
